# Optimizing a Trainium2 kernel written in Bass

```python
import jax, jax.numpy as jnp
from jax import lax
import numpy as np

D_MODEL = 1024
BATCH = 1
SEQ = 256
DEPTH = 2

GRID_W = 64
CTX_LEN = 256
N_MIXERS = 3
HEAD_DIM = 64
N_HEADS = D_MODEL // HEAD_DIM
MLA_Q_LORA = 3 * D_MODEL // 8
MLA_KV_LORA = D_MODEL // 4
MLA_QK_NOPE = 64
MLA_QK_ROPE = 32
MLA_V_DIM = 64
SWA_KV_HEADS = N_HEADS // 4
SWA_WINDOW = 128
GA_KV_HEADS = N_HEADS // 2
Q_BLOCK = 128
D_FF = ((8 * D_MODEL // 3 + 127) // 128) * 128
N_EXPERTS = 8
TOP_K = 2
EXPERT_FF = D_FF // 2
ROPE_THETA = 10000.0
NORM_EPS = 1e-6
NEG_INF = -1e30

kernel_name = "hybrid_mla_swa_axialgqa_moe_dit"

def _rmsnorm(x, g):
    xf = x.astype(jnp.float32)
    y = xf * lax.rsqrt(jnp.mean(xf * xf, axis=-1, keepdims=True) + NORM_EPS)
    return (y * g.astype(jnp.float32)).astype(x.dtype)

def _modulate(h, shift, scale):
    return h * (1 + scale) + shift

def _axial_rope_tables(rows_n, rot_dim):
    n_freq = rot_dim // 4
    inv = ROPE_THETA ** (-jnp.arange(n_freq, dtype=jnp.float32) / n_freq)
    rows = jnp.broadcast_to(jnp.arange(rows_n, dtype=jnp.float32)[:, None], (rows_n, GRID_W)).reshape(-1)
    cols = jnp.broadcast_to(jnp.arange(GRID_W, dtype=jnp.float32)[None, :], (rows_n, GRID_W)).reshape(-1)
    ang = jnp.concatenate([rows[:, None] * inv, cols[:, None] * inv], axis=-1)
    return jnp.cos(ang), jnp.sin(ang)

def _rope(x, cos, sin):
    half = x.shape[-1] // 2
    xf = x.astype(jnp.float32)
    x1, x2 = xf[..., :half], xf[..., half:]
    cs = cos[None, :, None, :]
    sn = sin[None, :, None, :]
    return jnp.concatenate([x1 * cs - x2 * sn, x2 * cs + x1 * sn], axis=-1).astype(x.dtype)

def _softmax_attend(q, ks, vs, masks, sink):
    scores = []
    for k, m in zip(ks, masks):
        s = jnp.einsum('bqhgd,bkhd->bhgqk', q, k).astype(jnp.float32)
        if m is not None:
            s = jnp.where(m, s, NEG_INF)
        scores.append(s)
    lens = [s.shape[-1] for s in scores]
    if sink is not None:
        sk = sink.astype(jnp.float32)[None, :, :, None, None]
        scores.append(jnp.broadcast_to(sk, scores[0].shape[:-1] + (1,)))
    p = jax.nn.softmax(jnp.concatenate(scores, axis=-1), axis=-1)
    out = 0
    off = 0
    for v, n in zip(vs, lens):
        out = out + jnp.einsum('bhgqk,bkhd->bqhgd', p[..., off:off + n].astype(v.dtype), v)
        off += n
    return out

def _dense_blocks(q, k_l, v_l, k_c, v_c):
    b, s, hkv, g, dk = q.shape
    nb = s // Q_BLOCK
    qb = jnp.moveaxis(q.reshape(b, nb, Q_BLOCK, hkv, g, dk), 1, 0)
    ob = lax.map(lambda qi: _softmax_attend(qi, (k_l, k_c), (v_l, v_c), (None, None), None), qb)
    return jnp.moveaxis(ob, 0, 1).reshape(b, s, hkv, g, -1)

def _window_blocks(q, k_l, v_l, k_c, v_c, sink):
    b, s, hkv, g, dk = q.shape
    nb = s // Q_BLOCK

    def bands(t):
        tp = jnp.pad(t, ((0, 0), (Q_BLOCK, Q_BLOCK), (0, 0), (0, 0))).reshape(b, nb + 2, Q_BLOCK, hkv, -1)
        band = jnp.concatenate([tp[:, :-2], tp[:, 1:-1], tp[:, 2:]], axis=2)
        return jnp.moveaxis(band, 1, 0)

    qpos = jnp.arange(s).reshape(nb, Q_BLOCK)
    kpos = jnp.arange(nb)[:, None] * Q_BLOCK - Q_BLOCK + jnp.arange(3 * Q_BLOCK)[None, :]
    inside = (kpos >= 0) & (kpos < s)
    valid = (jnp.abs(qpos[:, :, None] - kpos[:, None, :]) <= SWA_WINDOW) & inside[:, None, :]
    qb = jnp.moveaxis(q.reshape(b, nb, Q_BLOCK, hkv, g, dk), 1, 0)
    ob = lax.map(lambda a: _softmax_attend(a[0], (a[1], k_c), (a[2], v_c), (a[3], None), sink),
                 (qb, bands(k_l), bands(v_l), valid))
    return jnp.moveaxis(ob, 0, 1).reshape(b, s, hkv, g, -1)

def _mla(h_l, h_c, w_dq, q_norm_g, w_uq, w_dkv, kv_norm_g, w_ukv, w_o, cos, sin, need_ctx):
    def project(h, rotate):
        b, l, _ = h.shape
        q = (_rmsnorm(h @ w_dq, q_norm_g) @ w_uq).reshape(b, l, N_HEADS, MLA_QK_NOPE + MLA_QK_ROPE)
        q_nope, q_rope = q[..., :MLA_QK_NOPE], q[..., MLA_QK_NOPE:]
        kv_a = h @ w_dkv
        c_kv = _rmsnorm(kv_a[..., :MLA_KV_LORA], kv_norm_g)
        k_rope = kv_a[..., MLA_KV_LORA:][:, :, None, :]
        if rotate:
            q_rope = _rope(q_rope, cos, sin)
            k_rope = _rope(k_rope, cos, sin)
        kv = (c_kv @ w_ukv).reshape(b, l, N_HEADS, MLA_QK_NOPE + MLA_V_DIM)
        k = jnp.concatenate([kv[..., :MLA_QK_NOPE],
                             jnp.broadcast_to(k_rope, (b, l, N_HEADS, MLA_QK_ROPE))], axis=-1)
        v = kv[..., MLA_QK_NOPE:]
        q = jnp.concatenate([q_nope, q_rope], axis=-1) * (MLA_QK_NOPE + MLA_QK_ROPE) ** -0.5
        return q[:, :, :, None, :], k, v

    b, s, _ = h_l.shape
    q_l, k_l, v_l = project(h_l, True)
    q_c, k_c, v_c = project(h_c, False)
    y_l = _dense_blocks(q_l, k_l, v_l, k_c, v_c).reshape(b, s, -1) @ w_o
    y_c = None
    if need_ctx:
        o_c = _softmax_attend(q_c, (k_c,), (v_c,), (None,), None)
        y_c = o_c.reshape(b, h_c.shape[1], -1) @ w_o
    return y_l, y_c

def _gqa_project(h, w_qkv, n_kv, q_norm_g, k_norm_g, cos, sin, rotate):
    b, l, _ = h.shape
    nq = N_HEADS * HEAD_DIM
    nk = n_kv * HEAD_DIM
    qkv = h @ w_qkv
    q = qkv[..., :nq].reshape(b, l, N_HEADS, HEAD_DIM)
    k = qkv[..., nq:nq + nk].reshape(b, l, n_kv, HEAD_DIM)
    v = qkv[..., nq + nk:].reshape(b, l, n_kv, HEAD_DIM)
    if q_norm_g is not None:
        q = _rmsnorm(q, q_norm_g)
        k = _rmsnorm(k, k_norm_g)
    if rotate:
        q = _rope(q, cos, sin)
        k = _rope(k, cos, sin)
    q = (q * HEAD_DIM ** -0.5).reshape(b, l, n_kv, N_HEADS // n_kv, HEAD_DIM)
    return q, k, v

def _swa(h_l, h_c, w_qkv, sinks, w_o, cos, sin, need_ctx):
    b, s, _ = h_l.shape
    sink = sinks.reshape(SWA_KV_HEADS, N_HEADS // SWA_KV_HEADS)
    q_l, k_l, v_l = _gqa_project(h_l, w_qkv, SWA_KV_HEADS, None, None, cos, sin, True)
    q_c, k_c, v_c = _gqa_project(h_c, w_qkv, SWA_KV_HEADS, None, None, cos, sin, False)
    y_l = _window_blocks(q_l, k_l, v_l, k_c, v_c, sink).reshape(b, s, -1) @ w_o
    y_c = None
    if need_ctx:
        o_c = _softmax_attend(q_c, (k_c,), (v_c,), (None,), sink)
        y_c = o_c.reshape(b, h_c.shape[1], -1) @ w_o
    return y_l, y_c

def _axial_gqa(h_l, h_c, w_qkv, q_norm_g, k_norm_g, w_o, cos, sin, need_ctx):
    b, s, _ = h_l.shape
    q_l, k_l, v_l = _gqa_project(h_l, w_qkv, GA_KV_HEADS, q_norm_g, k_norm_g, cos, sin, True)
    q_c, k_c, v_c = _gqa_project(h_c, w_qkv, GA_KV_HEADS, q_norm_g, k_norm_g, cos, sin, False)
    y_l = _dense_blocks(q_l, k_l, v_l, k_c, v_c).reshape(b, s, -1) @ w_o
    y_c = None
    if need_ctx:
        o_c = _softmax_attend(q_c, (k_c,), (v_c,), (None,), None)
        y_c = o_c.reshape(b, h_c.shape[1], -1) @ w_o
    return y_l, y_c

def _swiglu(t, w_gate_up, w_down):
    gu = t @ w_gate_up
    f = w_down.shape[0]
    return (jax.nn.silu(gu[..., :f]) * gu[..., f:]) @ w_down

def _moe(t, router_w, router_b, w_gate_up, w_down):
    logits = (t @ router_w).astype(jnp.float32) + router_b.astype(jnp.float32)
    top_v, top_i = lax.top_k(logits, TOP_K)
    gates = jax.nn.softmax(top_v, axis=-1)
    combine = jnp.sum(jax.nn.one_hot(top_i, N_EXPERTS, dtype=jnp.float32) * gates[..., None], axis=-2)
    y = jnp.zeros_like(t)
    for e in range(N_EXPERTS):
        y = y + combine[:, e:e + 1].astype(t.dtype) * _swiglu(t, w_gate_up[e], w_down[e])
    return y

def setup_inputs(seed: int = 0) -> dict:
    key = jax.random.key(seed)
    ks = iter(jax.random.split(key, 40))
    n_a = len(range(0, DEPTH, N_MIXERS))
    n_b = len(range(1, DEPTH, N_MIXERS))
    n_c = len(range(2, DEPTH, N_MIXERS))
    n_dense = len(range(0, DEPTH, 2))
    n_moe = len(range(1, DEPTH, 2))
    d = D_MODEL
    attn = N_HEADS * HEAD_DIM

    def rn(shape, std=1.0):
        return jax.random.normal(next(ks), shape, jnp.float32) * std

    def w(shape, fan_in, gain=1.0):
        return rn(shape, gain * fan_in ** -0.5)

    def g(shape):
        return 1.0 + rn(shape, 0.05)

    return {
        "x": rn((BATCH, SEQ, d)),
        "c": rn((BATCH, d)),
        "ctx": rn((BATCH, CTX_LEN, d)),
        "c_ctx": rn((d,)),
        "ada_w": w((DEPTH, d, 6 * d), d, 0.5),
        "ada_b": rn((DEPTH, 6 * d), 0.02),
        "norm_g": g((DEPTH, 2, d)),
        "final_norm_g": g((d,)),
        "mla_w_dq": w((n_a, d, MLA_Q_LORA), d),
        "mla_q_norm_g": g((n_a, MLA_Q_LORA)),
        "mla_w_uq": w((n_a, MLA_Q_LORA, N_HEADS * (MLA_QK_NOPE + MLA_QK_ROPE)), MLA_Q_LORA),
        "mla_w_dkv": w((n_a, d, MLA_KV_LORA + MLA_QK_ROPE), d),
        "mla_kv_norm_g": g((n_a, MLA_KV_LORA)),
        "mla_w_ukv": w((n_a, MLA_KV_LORA, N_HEADS * (MLA_QK_NOPE + MLA_V_DIM)), MLA_KV_LORA),
        "mla_w_o": w((n_a, N_HEADS * MLA_V_DIM, d), N_HEADS * MLA_V_DIM),
        "swa_w_qkv": w((n_b, d, (N_HEADS + 2 * SWA_KV_HEADS) * HEAD_DIM), d),
        "swa_sinks": rn((n_b, N_HEADS), 0.5),
        "swa_w_o": w((n_b, attn, d), attn),
        "ga_w_qkv": w((n_c, d, (N_HEADS + 2 * GA_KV_HEADS) * HEAD_DIM), d),
        "ga_q_norm_g": g((n_c, HEAD_DIM)),
        "ga_k_norm_g": g((n_c, HEAD_DIM)),
        "ga_w_o": w((n_c, attn, d), attn),
        "ffn_w_gate_up": w((n_dense, d, 2 * D_FF), d),
        "ffn_w_down": w((n_dense, D_FF, d), D_FF),
        "moe_router_w": w((n_moe, d, N_EXPERTS), d),
        "moe_router_b": rn((n_moe, N_EXPERTS), 0.01),
        "moe_w_gate_up": w((n_moe, N_EXPERTS, d, 2 * EXPERT_FF), d),
        "moe_w_down": w((n_moe, N_EXPERTS, EXPERT_FF, d), EXPERT_FF),
    }

def reference(x, c, ctx, c_ctx, ada_w, ada_b, norm_g, final_norm_g,
              mla_w_dq, mla_q_norm_g, mla_w_uq, mla_w_dkv, mla_kv_norm_g, mla_w_ukv, mla_w_o,
              swa_w_qkv, swa_sinks, swa_w_o,
              ga_w_qkv, ga_q_norm_g, ga_k_norm_g, ga_w_o,
              ffn_w_gate_up, ffn_w_down,
              moe_router_w, moe_router_b, moe_w_gate_up, moe_w_down):
    b, s, d = x.shape
    n_lat = b * s
    rows_n = s // GRID_W
    cos_mla, sin_mla = _axial_rope_tables(rows_n, MLA_QK_ROPE)
    cos_h, sin_h = _axial_rope_tables(rows_n, HEAD_DIM)
    sc = jax.nn.silu(c)
    scc = jax.nn.silu(c_ctx)

    for i in range(DEPTH):
        need_ctx = i < DEPTH - 1
        mod_l = (sc @ ada_w[i] + ada_b[i]).reshape(b, 6, 1, d)
        mod_c = (scc @ ada_w[i] + ada_b[i]).reshape(6, d)

        h_l = _modulate(_rmsnorm(x, norm_g[i, 0]), mod_l[:, 0], mod_l[:, 1])
        h_c = _modulate(_rmsnorm(ctx, norm_g[i, 0]), mod_c[0], mod_c[1])
        kind, j = i % N_MIXERS, i // N_MIXERS
        if kind == 0:
            y_l, y_c = _mla(h_l, h_c, mla_w_dq[j], mla_q_norm_g[j], mla_w_uq[j], mla_w_dkv[j],
                            mla_kv_norm_g[j], mla_w_ukv[j], mla_w_o[j], cos_mla, sin_mla, need_ctx)
        elif kind == 1:
            y_l, y_c = _swa(h_l, h_c, swa_w_qkv[j], swa_sinks[j], swa_w_o[j], cos_h, sin_h, need_ctx)
        else:
            y_l, y_c = _axial_gqa(h_l, h_c, ga_w_qkv[j], ga_q_norm_g[j], ga_k_norm_g[j], ga_w_o[j],
                                  cos_h, sin_h, need_ctx)
        x = x + mod_l[:, 2] * y_l
        if need_ctx:
            ctx = ctx + mod_c[2] * y_c

        h_l = _modulate(_rmsnorm(x, norm_g[i, 1]), mod_l[:, 3], mod_l[:, 4])
        tokens = h_l.reshape(n_lat, d)
        if need_ctx:
            h_c = _modulate(_rmsnorm(ctx, norm_g[i, 1]), mod_c[3], mod_c[4])
            tokens = jnp.concatenate([tokens, h_c.reshape(-1, d)], axis=0)
        f = i // 2
        if i % 2 == 0:
            out = _swiglu(tokens, ffn_w_gate_up[f], ffn_w_down[f])
        else:
            out = _moe(tokens, moe_router_w[f], moe_router_b[f], moe_w_gate_up[f], moe_w_down[f])
        x = x + mod_l[:, 5] * out[:n_lat].reshape(b, s, d)
        if need_ctx:
            ctx = ctx + mod_c[5] * out[n_lat:].reshape(ctx.shape)

    return _rmsnorm(x, final_norm_g)


_drawn_inputs = setup_inputs


def setup_inputs(seed=0):
    import zlib

    import numpy as np

    out = dict(_drawn_inputs(seed))
    spreads = {}
    factors = {'mla_q_norm_g': 8.0, 'mla_kv_norm_g': 7.35, 'swa_sinks': 64.0, 'moe_router_b': 23.072}
    for name, (base, spread) in spreads.items():
        noise = np.random.default_rng([zlib.crc32(name.encode()), seed]).standard_normal(out[name].shape)
        drawn = base * np.exp(spread * noise) if base else spread * noise
        out[name] = __import__('jax').numpy.asarray(drawn.astype(out[name].dtype))
    for name, factor in factors.items():
        out[name] = (out[name] * factor).astype(out[name].dtype)
    return out
```

```python
import numpy as np

import concourse.bass as bass
from concourse import mybir
from contextlib import ExitStack

D = 1024
T = 512
TL = 256
GRID_W = 64
H = 16
HD = 64
QL, KVL, NOPE, ROPE = 384, 256, 64, 32
QKD = NOPE + ROPE
DFF = 2816
NEXP, EFF = 8, 1408
EPS = 1e-6
NEG = -1e30
P = 128
KC = D // P
NMOD = 6 * KC

SLOTS = 3
ONE = 1
SLOT = 2304
ADA_W = 256
ADA_FIRST = 8
ADA_TILES = 6 * D // ADA_W
GROUPS = ((0, 6, (3, 3, 2)), (6, 5, (2, 2, 2, 2)))
WO_COLS_0 = (256, 256, 128, 128, 128, 128)
WO_COLS_1 = (256, 256, 256, 256)


def ffn_items():
    items = []
    for g, (f0, nf, parts) in enumerate(GROUPS):
        items += [("up", g, f, f0 + f, 0) for f in range(nf)]
        m = 0
        for parted in parts:
            items.append(("down", g, parted, f0, m))
            m += parted
    return items


ITEMS = ffn_items()
NITEMS = len(ITEMS)
assert NITEMS % SLOTS == 0


def item_size(item):
    return KC * 256 if item[0] == "up" else GROUPS[item[1]][1] * item[2] * P


DONE_BY_ITEM = [0]
for _kind, _g, _k, _f, _m in ITEMS:
    DONE_BY_ITEM.append(DONE_BY_ITEM[-1] + (1 if _kind == "up" else _k))
PER_EXP = DONE_BY_ITEM[-1]
HALF_EXP = DONE_BY_ITEM[NITEMS // 2]

N_PROJ0 = 3
BASE_WO0 = N_PROJ0
BASE_FFN0 = BASE_WO0 + len(WO_COLS_0)
BASE_KV1 = BASE_FFN0 + 2 * NITEMS
BASE_WO1 = BASE_KV1 + 2
BASE_FFN1 = BASE_WO1 + len(WO_COLS_1)
assert BASE_FFN0 % SLOTS == 0 and BASE_KV1 % SLOTS == 0 and BASE_FFN1 % SLOTS == 0
Q_SLOT = 2

ROWS_A = {"norm_g": (0, 32), "final_g": (32, 8), "q_norm_g": (40, 3), "kv_norm_g": (43, 2),
          "c": (45, 8), "c_ctx": (53, 8), "ada_b0": (61, NMOD)}
NROWS_A = 61 + NMOD


def build(nc, x, c, ctx_x, c_ctx, ada_w, ada_b, norm_g, final_g, w_dq, q_norm_g, w_uq, w_dkv, kv_norm_g,
          w_ukv, w_o0, w_qkv, sinks, w_o1, ffn_gu, ffn_dn, router_w, router_b, moe_gu, moe_dn,
          k_ident, k_rot_mla, k_rot_gqa, k_cs_mla, k_cs_gqa, k_mask, k_iota, out):
    f32, f32r, u32 = mybir.dt.float32, mybir.dt.float32r, mybir.dt.uint32
    ALU, ACT, AX = mybir.AluOpType, mybir.ActivationFunctionType, mybir.AxisListType
    stack = ExitStack()
    with stack:
        words = {f32: 4, f32r: 4, u32: 4}
        cursor = [16640]

        def place(name, shape, dt=f32, at=None):
            size = int(np.prod(shape[1:])) * words[dt]
            off = cursor[0] if at is None else at
            if at is None:
                cursor[0] = (off + size + 31) // 32 * 32
            return nc.alloc_sbuf_tensor_at(name, shape, dt, offset=off)

        def sem(name):
            return stack.enter_context(nc.semaphore(name))

        x_t = place("x_t", [P, KC, T])
        h_hi = place("h_hi", [P, KC, T], f32r)
        h_lo = place("h_lo", [P, KC, T], f32r)
        ident = place("ident", [P, P])
        ident_r = place("ident_r", [P, P], f32r)
        ones = place("ones", [P, P])
        rot_mla = place("rot_mla", [P, QKD])
        rot_gqa = place("rot_gqa", [P, P])
        cs_mla = place("cs_mla", [P, 2, 2, TL])
        cs_gqa = place("cs_gqa", [P, 2, 2, TL])
        mask = place("mask", [P, 2, P])
        mask_r = place("mask_r", [P, 2, P], f32r)
        iota = place("iota", [P, NEXP])
        sink_b = place("sink_b", [P, H])
        rb_b = place("rb_b", [P, NEXP])
        rw = place("rw", [P, KC, NEXP])
        rw_hi = place("rw_hi", [P, KC, NEXP], f32r)
        rw_lo = place("rw_lo", [P, KC, NEXP], f32r)
        rows_a = place("rows_a", [P, P])
        rows_b = place("rows_b", [NMOD, P])
        cols_a = place("cols_a", [P, NROWS_A])
        cols_b = place("cols_b", [P, NMOD])
        silu_c = place("silu_c", [P, KC, 2])
        mod = [place(f"mod{i}", [P, NMOD, 2]) for i in range(2)]
        gain = [place(f"gain{i}", [P, 2, KC, 2]) for i in range(2)]
        rstd = place("rstd", [P, T])
        eps_col = place("eps_col", [P, 1])
        pool_mark = place("pool_mark", [P, 1])
        ring0 = cursor[0]
        raw = place("raw", [P, SLOTS, SLOT])
        w_hi = place("w_hi", [P, SLOTS, SLOT], f32r)
        w_lo = place("w_lo", [P, SLOTS, SLOT], f32r)
        ring1 = cursor[0]
        ada_raw = place("ada_raw", [P, 2, KC, ADA_W])
        work0 = cursor[0]

        cursor[0] = ring0
        uq_raw = place("uq_raw", [P, QL // P, H * QKD])
        ukv_raw = place("ukv_raw", [P, KVL // P, H * 128])
        uq_hi = place("uq_hi", [P, QL // P, 2 * QKD], f32r)
        uq_lo = place("uq_lo", [P, QL // P, 2 * QKD], f32r)
        ukv_hi = place("ukv_hi", [P, KVL // P, 256], f32r)
        ukv_lo = place("ukv_lo", [P, KVL // P, 256], f32r)
        mk_hi = place("mk_hi", [QKD, 2, T], f32r)
        mk_lo = place("mk_lo", [QKD, 2, T], f32r)
        mq_hi = place("mq_hi", [QKD, 2, T], f32r)
        mq_lo = place("mq_lo", [QKD, 2, T], f32r)
        mv_hi = place("mv_hi", [P, 4, P], f32r)
        mv_lo = place("mv_lo", [P, 4, P], f32r)
        pl_hi = place("pl_hi", [P, 4, TL], f32r)
        pl_lo = place("pl_lo", [P, 4, TL], f32r)
        assert cursor[0] <= ring1, (cursor[0], ring1)
        cursor[0] = ring0 + SLOTS * SLOT * 4
        gp = place("gp", [P, 3, T])
        gt_hi = place("gt_hi", [P, 4, TL], f32r)
        gt_lo = place("gt_lo", [P, 4, TL], f32r)
        assert cursor[0] <= ring0 + (SLOTS + 2) * SLOT * 4
        cursor[0] = ring0 + 2 * SLOTS * SLOT * 4
        gq_hi = place("gq_hi", [P, 2, TL], f32r)
        gq_lo = place("gq_lo", [P, 2, TL], f32r)
        gq = place("gq", [P, 2, TL])
        g_rot = place("g_rot", [P, 2, TL])
        gk_hi = place("gk_hi", [P, T], f32r)
        gk_lo = place("gk_lo", [P, T], f32r)
        gv_hi = place("gv_hi", [P, 4, P], f32r)
        gv_lo = place("gv_lo", [P, 4, P], f32r)
        assert cursor[0] <= ring0 + (2 * SLOTS + 2) * SLOT * 4, cursor[0]

        cursor[0] = work0
        sq = place("sq", [P, KC, T])
        mla0 = cursor[0]
        qa_hi = place("qa_hi", [P, QL // P, T], f32r)
        qa_lo = place("qa_lo", [P, QL // P, T], f32r)
        ca_hi = place("ca_hi", [P, KVL // P, T], f32r)
        ca_lo = place("ca_lo", [P, KVL // P, T], f32r)
        kr = place("kr", [QKD, T])
        kr_rot = place("kr_rot", [QKD, TL])
        mla1 = cursor[0]
        cursor[0] = work0
        pc_hi = place("pc_hi", [P, 2, TL], f32r)
        pc_lo = place("pc_lo", [P, 2, TL], f32r)
        mp = place("mp", [P, 3, T])
        mq = place("mq", [QKD, 2, T])
        mq_rot = place("mq_rot", [QKD, 2, TL])
        assert cursor[0] <= mla0
        cursor[0] = mla0
        x_rows = place("x_rows", [P, 4, D])
        work_end = max(mla1, cursor[0])
        cursor[0] = work0
        hid_hi = place("hid_hi", [P, 6, T], f32r)
        hid_lo = place("hid_lo", [P, 6, T], f32r)
        sil = place("sil", [P, 2, T])
        hid = place("hid", [P, 2, T])
        cb = place("cb", [P, NEXP, TL])
        comb = place("comb", [P, 2, NEXP])
        comb_rep = place("comb_rep", [P, 2, NEXP, P], at=ring1)
        lg = place("lg", [P, 2, NEXP])
        top = place("top", [P, 2, 8])
        top_i = place("top_i", [P, 2, 8], u32)
        top_f = place("top_f", [P, 2, 8])
        gate = place("gate", [P, 2, 4])
        hot = place("hot", [P, 2, NEXP])
        ffn_end = cursor[0]
        cursor[0] = mla0
        k_hi = place("k_hi", [P, 4, T], f32r)
        k_lo = place("k_lo", [P, 4, T], f32r)
        v_hi = place("v_hi", [P, 4, 256], f32r)
        v_lo = place("v_lo", [P, 4, 256], f32r)
        sink_g = place("sink_g", [P, 4])
        att1_end = cursor[0]
        cursor[0] = work0
        o_hi = place("o_hi", [P, KC, TL], f32r)
        o_lo = place("o_lo", [P, KC, TL], f32r)
        kf = place("kf", [P, 2, T], at=ring1)
        kf_rot = place("kf_rot", [P, 2, TL], at=ring1 + 4096)
        out_rows = place("out_rows", [P, 2, D], at=mla0)
        cursor[0] = max(work_end, ffn_end, att1_end)
        nmax = place("nmax", [P, 3, 2])
        psum_e = place("psum_e", [P, 3, 2])
        rsum = place("rsum", [P, 3, 2])
        esink = place("esink", [P, 3, 2])
        mraw = place("mraw", [P, 3, 2])
        assert cursor[0] <= nc.sbuf_usable_end, (cursor[0], nc.sbuf_usable_end)

        B = [stack.enter_context(nc.psum_tensor(f"bank{i}", [P, 512], f32)) for i in range(8)]
        ADA_BANK = B[7]
        ada_ps = ADA_BANK[:, 0:2 * NMOD].rearrange("p (m v) -> p m v", v=2)

        s_id = sem("ident_in")
        s_const = sem("constants_in")
        s_eps = sem("eps_set")
        s_mark = sem("pool_waited")
        s_vec = sem("vectors_in")
        s_x = sem("x_rows_in")
        s_ones = sem("ones_set")
        s_vecT = sem("vectors_transposed")
        s_cols = sem("vector_columns")
        s_silu = sem("silu_c_done")
        s_xT = sem("x_transposed")
        s_xc = sem("x_columns_even")
        s_xc1 = sem("x_columns_odd")
        s_rwlo = sem("router_w_lo")
        s_cr = sem("constants_rounded")
        ada_full = [sem(f"ada_full{i}") for i in range(2)]
        ada_used = sem("ada_used")
        s_mod = sem("mod_ready")
        raw_full = [sem(f"raw_full{i}") for i in range(SLOTS)]
        split_hi = sem("split_hi")
        split_lo = sem("split_lo")
        norm_sem = {s: sem(f"norm_{s}") for s in ("sq", "sum", "rms", "rstd", "tmp", "hi", "lo")}
        norm_base, total = {}, dict.fromkeys(norm_sem, 0)
        for key, chunks, parts, halves in (("n01", KC, 2, 1), ("nq", 3, 1, 1), ("nc", 2, 1, 1), ("n02", KC, 2, 1),
                                           ("n11", KC, 2, 1), ("n12", KC, 1, 1), ("nf", KC, 1, 0)):
            norm_base[key] = dict(total)
            for step, n in (("sq", chunks), ("sum", 1), ("rms", 1), ("rstd", 1), ("tmp", chunks * parts),
                            ("hi", chunks * parts * halves), ("lo", chunks * parts * halves)):
                total[step] += n

        def normed(key, step, n):
            return norm_sem[step], norm_base[key][step] + n

        s_pj = sem("proj0_done")
        s_pje = sem("proj0_evacuated")
        s_krr = sem("k_rope_rotated")
        s_kr = sem("k_rope_steps")
        s_krhi = sem("k_rope_hi")
        s_krlo = sem("k_rope_lo")
        mraw_in = sem("mla_raw_in")
        m = {s: sem(f"mla_{s}") for s in ("w_hi", "w_lo", "proj", "q_f32", "kv_hi", "kv_lo", "rot", "rope",
                                          "q_hi", "q_lo", "scores", "max", "exp", "rsum", "normed",
                                          "turned", "p_hi", "p_lo", "pv", "o_hi", "o_lo")}
        wo = [{s: sem(f"wo{i}_{s}") for s in ("done", "added")} for i in range(2)]
        ff = [{s: sem(f"ff{i}_{s}") for s in ("pe", "silu", "hid", "hid_w", "hid_hi", "hid_lo", "added")}
              for i in range(2)]
        s_kv1 = sem("kv1_done")
        s_kf = sem("k1_f32")
        s_krot1 = sem("k1_rotated")
        s_krope1 = sem("k1_rope_steps")
        s_kdup_hi = sem("k1_hi")
        s_kdup_lo = sem("k1_lo")
        s_kdup2 = sem("k1_copied")
        s_v1hi = sem("v1_hi")
        s_v1lo = sem("v1_lo")
        qw_full, qw_hi, qw_lo = sem("qw_full"), sem("qw_hi"), sem("qw_lo")
        g = {s: sem(f"gqa_{s}") for s in ("proj", "q_f32", "rot", "rope", "q_hi", "q_lo", "kv_copied", "scores",
                                          "max", "nmax", "exp", "esink", "sum", "rsum", "normed", "turned",
                                          "p_hi", "p_lo", "pv", "o_hi", "o_lo")}
        s_lgp = sem("logits_done")
        s_rt = sem("router_top")
        s_rs = sem("router_steps")
        s_gx = sem("gate_exp")
        s_cbp = sem("combine_turned")
        s_cb = sem("combine_ready")
        s_oT = sem("out_turned")
        s_orow = sem("out_rows_ready")
        s_out = sem("out_written")

        from_one = [m[k] for k in ("exp", "p_lo", "o_lo", "proj")] + [qw_lo]
        from_one += [g[k] for k in ("exp", "turned", "pv", "p_lo", "o_lo", "proj")]
        from_one += [q[k] for q in ff for k in ("pe", "hid", "hid_lo", "added")]

        LAT, CTX = slice(0, TL), slice(TL, T)
        HALVES = (LAT, CTX)

        def norms_of(layer, which):
            return gain[layer][:, which], (lambda kc, v: mod[layer][:, 24 * which + kc, v:v + 1])

        def used(n):
            if n < BASE_WO0:
                return s_pj, (2, 3, 6)[n]
            if n < BASE_FFN0:
                return wo[0]["done"], sum(WO_COLS_0[:n - BASE_WO0 + 1]) // P
            if n < BASE_KV1:
                e, s = divmod(n - BASE_FFN0, NITEMS)
                return ff[0]["pe"], ONE + e * PER_EXP + DONE_BY_ITEM[s + 1]
            if n < BASE_WO1:
                return s_kv1, 2 * (n - BASE_KV1 + 1)
            return wo[1]["done"], sum(WO_COLS_1[:n - BASE_WO1 + 1]) // P

        block = stack.enter_context(nc.Block())

        @block.sync
        def _(sp):
            def load(dst, src, s):
                sp.dma_start(dst, src).then_inc(s, 16)

            def row_chunks(a):
                return a.rearrange("(r p) -> r p", p=P)

            load(ident[:, :], k_ident, s_id)
            for name, src in (("norm_g", norm_g.rearrange("a b (r p) -> (a b r) p", p=P)),
                              ("final_g", row_chunks(final_g)), ("q_norm_g", row_chunks(q_norm_g[0])),
                              ("kv_norm_g", row_chunks(kv_norm_g[0])), ("c", row_chunks(c[0])),
                              ("c_ctx", row_chunks(c_ctx)), ("ada_b0", row_chunks(ada_b[0]))):
                r0, n = ROWS_A[name]
                load(rows_a[r0:r0 + n, :], src, s_vec)
            load(rows_b[:, :], row_chunks(ada_b[1]), s_vec)
            load(x_rows[:, 0:2, :], x[0].rearrange("(t p) d -> p t d", p=P), s_x)
            load(x_rows[:, 2:4, :], ctx_x[0].rearrange("(t p) d -> p t d", p=P), s_x)

            def ada_tile(layer, a, slot, n):
                sp.dma_start(ada_raw[:, slot], ada_w[layer].rearrange("(k p) n -> p k n", p=P)
                             [:, :, bass.ds(a * ADA_W, ADA_W)]).then_inc(ada_full[slot], 16)

            def slot_free(n):
                if n >= SLOTS:
                    sp.wait_ge(split_lo, n - SLOTS + 1)

            def tile_cols(n, w, c0, ncols, nk=KC):
                slot_free(n)
                dst = raw[:, n % SLOTS, 0:nk * ncols].rearrange("p (k n) -> p k n", k=nk)
                src = w.rearrange("(k p) n -> p k n", p=P)
                for a, b in ((0, nk // 2), (nk // 2, nk)):
                    load(dst[:, a:b, :], src[:, a:b, c0:c0 + ncols], raw_full[n % SLOTS])

            ada_tile(0, 0, 0, 0)
            ada_tile(0, 1, 1, 1)
            for dst, src in ((rot_mla[:, :], k_rot_mla), (rot_gqa[:, :], k_rot_gqa),
                             (cs_mla[:, :, :, :], k_cs_mla), (cs_gqa[:, :, :, :], k_cs_gqa),
                             (mask[:, :, :], k_mask), (iota[:, :], k_iota),
                             (sink_b[:, :], sinks.partition_broadcast(P)[:, 0, :]),
                             (rb_b[:, :], router_b.partition_broadcast(P)[:, 0, :]),
                             (rw[:, :, :], router_w[0].rearrange("(k p) e -> p k e", p=P))):
                load(dst, src, s_const)
            tiles0 = [(w_dq[0], 0, 256), (w_dq[0], 256, 128), (w_dkv[0], 0, KVL + ROPE)]
            for a in range(2, ADA_FIRST):
                sp.wait_ge(ada_used, a - 1)
                ada_tile(0, a, a % 2, a)
                if 3 <= a < 6:
                    tile_cols(a - 3, *tiles0[a - 3])
            sp.wait_ge(s_pj, 6)
            load(uq_raw[:, :, :], w_uq[0].rearrange("(k p) n -> p k n", p=P), mraw_in)
            load(ukv_raw[:, :, :], w_ukv[0].rearrange("(k p) n -> p k n", p=P), mraw_in)
            with sp.Fori(0, H // 2) as i:
                for j in range(2):
                    sp.wait_ge(ada_used, i * 2 + (ADA_FIRST + j - 1))
                    ada_tile(0, i * 2 + (ADA_FIRST + j), j, None)
            sp.wait_ge(m["w_lo"], 2 * (H // 2))
            c0 = 0
            for k, cols in enumerate(WO_COLS_0):
                tile_cols(BASE_WO0 + k, w_o0[0], c0, cols)
                c0 += cols

            def ffn_tiles(w_gu, w_dn, width, gu_col, dn_row, first_lo, base, ada=None):
                for s, (kind, gr, k, f0, m0) in enumerate(ITEMS):
                    slot = s % SLOTS
                    sp.wait_ge(split_lo, first_lo + (s - SLOTS + 1))
                    if kind == "up":
                        dst = raw[:, slot, 0:KC * 256].rearrange("p (k n) -> p k n", k=KC)
                        src = w_gu.rearrange("(k p) n -> p k n", p=P)
                        load(dst[:, :, 0:P], src[:, :, bass.ds(gu_col + f0 * P, P)], raw_full[slot])
                        load(dst[:, :, P:2 * P], src[:, :, bass.ds(gu_col + (width + f0 * P), P)], raw_full[slot])
                    else:
                        nf, cols = GROUPS[gr][1], k * P
                        dst = raw[:, slot, 0:nf * cols].rearrange("p (k n) -> p k n", k=nf)
                        for a, b in ((0, nf // 2), (nf // 2, nf)):
                            src = w_dn[bass.ds(dn_row + (f0 + a) * P, (b - a) * P), m0 * P:m0 * P + cols]
                            load(dst[:, a:b, :], src.rearrange("(k p) n -> p k n", p=P), raw_full[slot])
                    if ada is not None and s < ADA_TILES // 2:
                        sp.wait_ge(ada_used, ada + (ADA_TILES + s - 1))
                        ada_tile(1, ada + s, s % 2, None)

            with sp.Fori(0, 2) as e:
                ffn_tiles(ffn_gu[0], ffn_dn[0], DFF, e * EFF, e * EFF, e * NITEMS + BASE_FFN0, BASE_FFN0,
                          ada=e * (ADA_TILES // 2))
            tile_cols(BASE_KV1, w_qkv[0], H * HD, 256)
            tile_cols(BASE_KV1 + 1, w_qkv[0], H * HD + 256, 256)
            sp.wait_ge(split_lo, BASE_KV1)
            with sp.Fori(0, 4) as gi:
                sp.wait_ge(qw_lo, ONE + gi)
                sp.dma_start(raw[:, Q_SLOT, 0:KC * 256].rearrange("p (k n) -> p k n", k=KC),
                             w_qkv[0].rearrange("(k p) n -> p k n", p=P)[:, :, bass.ds(gi * 256, 256)])\
                  .then_inc(qw_full, 16)
            sp.wait_ge(qw_lo, ONE + 4)
            for k, cols in enumerate(WO_COLS_1):
                tile_cols(BASE_WO1 + k, w_o1[0], 256 * k, cols)
            with sp.Fori(0, NEXP) as e:
                ffn_tiles(moe_gu[0, e], moe_dn[0, e], EFF, 0, 0, e * NITEMS + BASE_FFN1, BASE_FFN1)
            for t in range(2):
                sp.wait_ge(s_orow, 4 * (t + 1))
                sp.dma_start(out[0, t * P:(t + 1) * P, :], out_rows[:, t, :]).then_inc(s_out, 16)
            sp.wait_ge(s_out, 32)

        @block.gpsimd
        def _(pool):
            for s in from_one:
                pool.sem_inc(s, ONE)
            pool.memset(ones[:, :], 1.0).then_inc(s_ones, 1)
            pool.wait_ge(s_ones, 1)

            with pool.Fori(0, H // 2) as i:
                for u in range(6):
                    pool.wait_ge(m["rsum"], i * 6 + (u + 1))
                    if u % 3 < 2:
                        pool.tensor_tensor(mp[:, u % 3, :], mp[:, u % 3, :], rsum[:, u % 3, 0:1].to_broadcast([P, T]),
                                           ALU.mult).then_inc(m["normed"], 2)
                    else:
                        for t in range(2):
                            cs = slice(t * TL, (t + 1) * TL)
                            pool.tensor_tensor(mp[:, 2, cs], mp[:, 2, cs], rsum[:, 2, t:t + 1].to_broadcast([P, TL]),
                                               ALU.mult).then_inc(m["normed"], 1)

            def hidden(q, e_gu, f, k, nt):
                pool.wait_ge(q["hid"], ONE + e_gu + (k + 1))
                b = k % 2
                pool.tensor_tensor(hid_hi[:, f, 0:nt], hid[:, b, 0:nt], ones[:, 0:1].to_broadcast([P, nt]), ALU.mult)\
                    .then_inc(q["hid_hi"], 1)
                pool.wait_ge(q["hid_hi"], e_gu + (k + 1))
                pool.tensor_tensor(hid_lo[:, f, 0:nt], hid[:, b, 0:nt], hid_hi[:, f, 0:nt].bitcast(f32),
                                   ALU.subtract).then_inc(q["hid_lo"], 1)

            def ffn(q, e, nt):
                for gr, (f0, nf, parts) in enumerate(GROUPS):
                    if gr == 0:
                        pool.wait_ge(q["pe"], ONE + e * PER_EXP)
                    else:
                        pool.wait_ge(q["pe"], ONE + e * PER_EXP + HALF_EXP)
                    for f in range(nf):
                        hidden(q, e * 11, f, f0 + f, nt)

            with pool.Fori(0, 2) as e:
                ffn(ff[0], e, T)

            with pool.Fori(0, 4) as gi:
                pool.wait_ge(s_kdup2, 8)
                pool.wait_ge(s_v1lo, 2)
                pool.wait_ge(g["pv"], ONE + gi * 4)
                pool.tensor_tensor(pool_mark[:, :], ones[:, 0:1], ones[:, 0:1], ALU.mult).then_inc(s_mark, 1)
                pool.tensor_copy(gk_hi[:, :], k_hi[:, gi, :].bitcast(f32)).then_inc(g["kv_copied"], 1)
                pool.tensor_copy(gk_lo[:, :], k_lo[:, gi, :].bitcast(f32)).then_inc(g["kv_copied"], 1)
                for half in range(2):
                    for dst, src in ((gv_hi, v_hi), (gv_lo, v_lo)):
                        pool.tensor_copy(dst[:, :, half * HD:(half + 1) * HD],
                                         src[:, :, bass.ds(gi * HD, HD)].bitcast(f32)).then_inc(g["kv_copied"], 1)
                pool.tensor_copy(sink_g[:, :], sink_b[:, bass.ds(gi * 4, 4)]).then_inc(g["kv_copied"], 1)
                for u in range(8):
                    pool.wait_ge(g["rsum"], gi * 8 + (u + 1))
                    pool.tensor_tensor(gp[:, u % 3, :], gp[:, u % 3, :], rsum[:, u % 3, 0:1].to_broadcast([P, T]),
                                       ALU.mult).then_inc(g["normed"], 1)

            with pool.Fori(0, NEXP) as e:
                ffn(ff[1], e, TL)

        @block.scalar
        def _(act):
            def split(n, size):
                slot = n % SLOTS
                act.wait_ge(raw_full[slot], 32 * (n // SLOTS + 1))
                if n >= SLOTS:
                    act.wait_ge(*used(n - SLOTS))
                act.copy(w_hi[:, slot, 0:size], raw[:, slot, 0:size]).then_inc(split_hi, 1)

            def norm(key, chunks, width, nt, src, ready, bank, shift, dst_hi, parts):
                for kc in range(chunks):
                    ready(kc)
                    act.activation(sq[:, kc, 0:nt], src(kc), ACT.Square).then_inc(norm_sem["sq"], 1)
                act.wait_ge(*normed(key, "sum", 1))
                act.wait_ge(s_eps, 1)
                act.activation(rstd[:, 0:nt], bank[:, 0:nt], ACT.Sqrt, scale=1.0 / width,
                               bias=eps_col[:, 0:1]).then_inc(norm_sem["rms"], 1)
                if dst_hi is None:
                    return
                for kc in range(chunks):
                    for v in range(parts):
                        cs = HALVES[v] if parts == 2 else slice(0, nt)
                        act.wait_ge(*normed(key, "tmp", parts * kc + v + 1))
                        if shift is None:
                            act.copy(dst_hi[:, kc, cs], sq[:, kc, cs]).then_inc(norm_sem["hi"], 1)
                        else:
                            act.activation(dst_hi[:, kc, cs], sq[:, kc, cs], ACT.Identity,
                                           bias=shift(kc, v)).then_inc(norm_sem["hi"], 1)

            act.wait_ge(s_vecT, 2)
            act.copy(cols_a[:, :], B[0][:, 0:NROWS_A]).then_inc(s_cols, 1)
            act.copy(cols_b[:, :], B[1][:, 0:NMOD]).then_inc(s_cols, 1)
            act.wait_ge(s_cols, 2)
            for v, name in enumerate(("c", "c_ctx")):
                r0, n = ROWS_A[name]
                act.activation(silu_c[:, :, v], cols_a[:, r0:r0 + n], ACT.Silu).then_inc(s_silu, 1)
            for kc in range(1, KC, 2):
                act.wait_ge(s_xT, kc + 1)
                act.copy(x_t[:, kc, :], B[2 + kc % 4][:, :]).then_inc(s_xc1, 1)
            act.wait_ge(s_const, 16 * 9)
            act.wait_ge(s_id, 16)
            act.copy(ident_r[:, :], ident[:, :]).then_inc(s_cr, 1)
            act.copy(mask_r[:, :, :], mask[:, :, :]).then_inc(s_cr, 1)
            act.copy(rw_hi[:, :, :], rw[:, :, :]).then_inc(s_cr, 1)

            def x_ready(kc):
                act.wait_ge(s_xc1 if kc % 2 else s_xc, kc // 2 + 1)
            for n, size in enumerate((2048, 1024, 2304)):
                split(n, size)
            norm("n01", KC, D, T, lambda kc: x_t[:, kc, :], x_ready, B[6],
                 norms_of(0, 0)[1], h_hi, 2)
            act.wait_ge(*normed("n01", "lo", 2 * KC))
            norm("nq", 3, QL, T, lambda kc: B[kc][:, :], lambda kc: act.wait_ge(s_pj, kc + 1), B[6], None, qa_hi, 1)
            act.wait_ge(s_pj, 6)
            act.copy(kr[NOPE:QKD, :], B[5][0:ROPE, :]).then_inc(s_pje, 1)
            act.wait_ge(*normed("nq", "lo", 3))
            norm("nc", 2, KVL, T, lambda kc: B[3 + kc][:, :], lambda kc: act.wait_ge(s_pj, kc + 4), B[6], None,
                 ca_hi, 1)
            act.wait_ge(s_kr, 3)
            for j in range(2):
                act.copy(mk_hi[NOPE:QKD, j, :], kr[NOPE:QKD, :]).then_inc(s_krhi, 1)

            act.wait_ge(mraw_in, 32)
            act.wait_ge(*normed("nc", "lo", 2))

            def mla_exp(i, u):
                act.wait_ge(m["max"], i * 6 + (u + 1))
                if u >= 3:
                    act.wait_ge(m["turned"], i * 6 + (u - 2))
                if u % 3 < 2:
                    act.activation(mp[:, u % 3, :], B[u % 3][:, :], ACT.Exp, bias=nmax[:, u % 3, 0:1],
                                   accum_out=psum_e[:, u % 3, 0:1]).then_inc(m["exp"], 1)
                else:
                    for t in range(2):
                        cs = slice(t * TL, (t + 1) * TL)
                        last = act.activation(mp[:, 2, cs], B[2][:, cs], ACT.Exp, bias=nmax[:, 2, t:t + 1],
                                              accum_out=psum_e[:, 2, t:t + 1])
                    last.then_inc(m["exp"], 1)

            def mla_p_hi(i, u):
                act.wait_ge(m["turned"], i * 6 + (u + 1))
                turned = B[3 + u % 2]
                if u % 3 < 2:
                    act.copy(pl_hi[:, :, (u % 3) * P:(u % 3 + 1) * P],
                             turned[:, :].rearrange("p (c q) -> p c q", c=4)).then_inc(m["p_hi"], 1)
                else:
                    act.copy(pc_hi[:, :, :], turned[:, :].rearrange("p (c q) -> p c q", c=2)).then_inc(m["p_hi"], 1)

            def mla_o_hi(i, j):
                act.wait_ge(m["pv"], i * 2 + (j + 1))
                rows = slice(HD * j, HD * (j + 1))
                act.copy(h_hi[rows, i, :], B[5 + j][rows, :]).then_inc(m["o_hi"], 1)

            with act.Fori(0, H // 2) as i:
                act.wait_ge(m["proj"], ONE + i * 5)
                act.copy(uq_hi[:, :, :], uq_raw[:, :, bass.ds(i * (2 * QKD), 2 * QKD)]).then_inc(m["w_hi"], 1)
                act.copy(ukv_hi[:, :, :], ukv_raw[:, :, bass.ds(i * 256, 256)]).then_inc(m["w_hi"], 1)
                for j in range(2):
                    act.wait_ge(m["proj"], ONE + i * 5 + (j + 1))
                    act.mul(mq[:, j, :], B[j][0:QKD, :], float(QKD) ** -0.5).then_inc(m["q_f32"], 1)
                for j in range(2):
                    act.wait_ge(m["proj"], ONE + i * 5 + (j + 3))
                    act.copy(mk_hi[0:NOPE, j, :], B[2 + j][0:NOPE, :]).then_inc(m["kv_hi"], 1)
                act.wait_ge(m["proj"], ONE + i * 5 + 5)
                act.copy(mv_hi[:, :, :], B[4][:, :].rearrange("p (t n) -> p t n", t=4)).then_inc(m["kv_hi"], 1)
                act.wait_ge(m["rope"], i * 3 + 3)
                act.copy(mq_hi[:, :, :], mq[:, :, :]).then_inc(m["q_hi"], 1)
                mla_exp(i, 0)
                mla_exp(i, 1)
                mla_exp(i, 2)
                mla_p_hi(i, 0)
                mla_exp(i, 3)
                mla_p_hi(i, 1)
                mla_p_hi(i, 2)
                mla_exp(i, 4)
                mla_o_hi(i, 0)
                mla_p_hi(i, 3)
                mla_exp(i, 5)
                mla_p_hi(i, 4)
                mla_p_hi(i, 5)
                mla_o_hi(i, 1)

            act.wait_ge(m["pv"], H)
            for k in range(3):
                split(BASE_WO0 + k, KC * WO_COLS_0[k])
            for k in range(3, len(WO_COLS_0)):
                split(BASE_WO0 + k, KC * WO_COLS_0[k])

            def x_after_wo(layer):
                return lambda kc: act.wait_ge(wo[layer]["added"], KC if layer else kc + 1)

            def ffn_split(q, e, s, base):
                slot = s % SLOTS
                act.wait_ge(raw_full[slot], e * (32 * NITEMS // SLOTS) + 32 * (base // SLOTS + s // SLOTS + 1))
                act.wait_ge(q["pe"], ONE + e * PER_EXP + DONE_BY_ITEM[s - 2])
                act.copy(w_hi[:, slot, 0:item_size(ITEMS[s % NITEMS])],
                         raw[:, slot, 0:item_size(ITEMS[s % NITEMS])]).then_inc(split_hi, 1)

            def ffn_body(q, e, base, nt, last, tail):
                for s, item in enumerate(ITEMS):
                    if s + 2 < NITEMS or not last:
                        ffn_split(q, e, s + 2, base)
                    elif tail:
                        split(*tail[s + 2 - NITEMS])
                    if item[0] == "up":
                        k = item[3]
                        act.wait_ge(q["pe"], ONE + e * PER_EXP + DONE_BY_ITEM[s + 1])
                        if k >= 2:
                            act.wait_ge(q["hid"], ONE + e * 11 + (k - 1))
                        else:
                            act.wait_ge(q["hid"], ONE + e * 11)
                        act.activation(sil[:, k % 2, 0:nt], B[2 * (k % 2)][:, 0:nt], ACT.Silu).then_inc(q["silu"], 1)

            def ffn(q, n_exp, base, nt, tail):
                with act.Fori(0, n_exp - 1) as e:
                    ffn_body(q, e, base, nt, False, None)
                ffn_body(q, n_exp - 1, base, nt, True, tail)

            for s in range(2):
                split(BASE_FFN0 + s, item_size(ITEMS[s]))
            norm("n02", KC, D, T, lambda kc: x_t[:, kc, :], x_after_wo(0), B[6], norms_of(0, 1)[1], h_hi, 2)
            act.wait_ge(*normed("n02", "lo", 2 * KC))
            ffn(ff[0], 2, BASE_FFN0, T, [(BASE_KV1, 2048), (BASE_KV1 + 1, 2048)])

            def x_after_ffn(layer, n_exp):
                return lambda kc: act.wait_ge(ff[layer]["added"], ONE + 16 * n_exp)

            norm("n11", KC, D, T, lambda kc: x_t[:, kc, :], x_after_ffn(0, 2), B[6], norms_of(1, 0)[1], h_hi, 2)
            for c2 in range(2):
                act.wait_ge(s_kv1, c2 + 1)
                act.copy(kf[:, c2, :], B[c2][:, :]).then_inc(s_kf, 1)
            for b in range(2):
                act.wait_ge(s_kv1, b + 3)
                act.copy(v_hi[:, 2 * b:2 * b + 2, :], B[2 + b][:, :].rearrange("p (t n) -> p t n", t=2))\
                   .then_inc(s_v1hi, 1)
            act.wait_ge(s_krope1, 3)
            for gg in range(4):
                rows = slice(HD * (gg % 2), HD * (gg % 2 + 1))
                act.copy(k_hi[rows, gg, :], kf[rows, gg // 2, :]).then_inc(s_kdup_hi, 1)
            for gg in range(4):
                rows = slice(HD * (gg % 2), HD * (gg % 2 + 1))
                other = slice(HD * (1 - gg % 2), HD * (2 - gg % 2))
                act.wait_ge(s_kdup_hi, gg + 1)
                act.copy(k_hi[other, gg, :], k_hi[rows, gg, :].bitcast(f32)).then_inc(s_kdup2, 1)
                act.wait_ge(s_kdup_lo, gg + 1)
                act.copy(k_lo[other, gg, :], k_lo[rows, gg, :].bitcast(f32)).then_inc(s_kdup2, 1)

            def g_exp(gi, u):
                act.wait_ge(g["nmax"], gi * 8 + (u + 1))
                if u >= 3:
                    act.wait_ge(g["turned"], ONE + gi * 8 + (u - 2))
                else:
                    act.wait_ge(g["turned"], ONE + gi * 8)
                act.activation(gp[:, u % 3, :], B[u % 3][:, :], ACT.Exp, bias=nmax[:, u % 3, 0:1],
                               accum_out=psum_e[:, u % 3, 0:1]).then_inc(g["exp"], 1)
                act.activation(esink[:, u % 3, 0:1], sink_g[:, u // 2:u // 2 + 1], ACT.Exp,
                               bias=nmax[:, u % 3, 0:1]).then_inc(g["esink"], 1)

            def g_p_hi(gi, u):
                act.wait_ge(g["turned"], ONE + gi * 8 + (u + 1))
                act.wait_ge(g["pv"], ONE + gi * 4 + u // 2)
                act.copy(gt_hi[:, :, (u % 2) * P:(u % 2 + 1) * P],
                         B[3 + u % 2][:, :].rearrange("p (c q) -> p c q", c=4)).then_inc(g["p_hi"], 1)

            def g_o_hi(gi, j):
                act.wait_ge(g["pv"], ONE + gi * 4 + (j + 1))
                rows = slice(HD * (j % 2), HD * (j % 2 + 1))
                act.copy(o_hi[rows, gi * 2 + j // 2, :], B[5 + j % 2][rows, 0:TL]).then_inc(g["o_hi"], 1)

            act.wait_ge(*normed("n11", "lo", 2 * KC))
            with act.Fori(0, 4) as gi:
                act.wait_ge(qw_full, gi * 16 + 16)
                act.wait_ge(g["proj"], ONE + gi * 2)
                act.copy(w_hi[:, Q_SLOT, 0:2048], raw[:, Q_SLOT, 0:2048]).then_inc(qw_hi, 1)
                for j in range(2):
                    act.wait_ge(g["proj"], ONE + gi * 2 + (j + 1))
                    act.mul(gq[:, j, :], B[j][:, 0:TL], float(HD) ** -0.5).then_inc(g["q_f32"], 1)
                act.wait_ge(g["rope"], gi * 3 + 3)
                act.copy(gq_hi[:, :, :], gq[:, :, :]).then_inc(g["q_hi"], 1)
                act.wait_ge(g["kv_copied"], gi * 7 + 7)
                g_exp(gi, 0)
                g_exp(gi, 1)
                for u in range(8):
                    if u + 2 < 8:
                        g_exp(gi, u + 2)
                    g_p_hi(gi, u)
                    if u % 2 == 0 and u >= 2:
                        g_o_hi(gi, u // 2 - 1)
                g_o_hi(gi, 3)

            act.wait_ge(g["pv"], ONE + H)
            for k in range(len(WO_COLS_1)):
                split(BASE_WO1 + k, KC * WO_COLS_1[k])
            for s in range(2):
                split(BASE_FFN1 + s, item_size(ITEMS[s]))
            norm("n12", KC, D, TL, lambda kc: x_t[:, kc, LAT], x_after_wo(1), B[6], norms_of(1, 1)[1], h_hi, 1)
            act.wait_ge(s_rt, 3)
            act.activation(gate[:, :, 1:2], gate[:, :, 0:1], ACT.Exp).then_inc(s_gx, 1)
            for b in range(4):
                act.wait_ge(s_cbp, b + 1)
                act.copy(cb[:, 2 * b:2 * b + 2, :], B[b][:, :].rearrange("p (e t) -> p e t", e=2)).then_inc(s_cb, 1)
            act.wait_ge(*normed("n12", "lo", KC))
            ffn(ff[1], NEXP, BASE_FFN1, TL, None)
            norm("nf", KC, D, TL, lambda kc: x_t[:, kc, LAT], x_after_ffn(1, NEXP), B[6], None, None, 1)

        @block.vector
        def _(dve):
            def lo_of(slot, size, n_hi):
                dve.wait_ge(split_hi, n_hi)
                dve.tensor_tensor(w_lo[:, slot, 0:size], raw[:, slot, 0:size], w_hi[:, slot, 0:size].bitcast(f32),
                                  ALU.subtract).then_inc(split_lo, 1)

            def norm(key, chunks, nt, src, gains, shift, dst_hi, dst_lo, parts):
                dve.wait_ge(*normed(key, "rms", 1))
                dve.reciprocal(rstd[:, 0:nt], rstd[:, 0:nt]).then_inc(norm_sem["rstd"], 1)
                dve.wait_ge(*normed(key, "rstd", 1))

                def low(kc):
                    for v in range(parts):
                        cs = HALVES[v] if parts == 2 else slice(0, nt)
                        dve.wait_ge(*normed(key, "hi", parts * kc + v + 1))
                        if shift is None:
                            dve.tensor_tensor(dst_lo[:, kc, cs], sq[:, kc, cs], dst_hi[:, kc, cs].bitcast(f32),
                                              ALU.subtract).then_inc(norm_sem["lo"], 1)
                        else:
                            dve.scalar_tensor_tensor(out=dst_lo[:, kc, cs], in0=sq[:, kc, cs], scalar=shift(kc, v),
                                                     in1=dst_hi[:, kc, cs].bitcast(f32), op0=ALU.add,
                                                     op1=ALU.subtract).then_inc(norm_sem["lo"], 1)

                for kc in range(chunks):
                    for v in range(parts):
                        cs = HALVES[v] if parts == 2 else slice(0, nt)
                        dve.scalar_tensor_tensor(out=sq[:, kc, cs], in0=src(kc, cs), scalar=gains(kc, v),
                                                 in1=rstd[:, cs], op0=ALU.mult, op1=ALU.mult).then_inc(norm_sem["tmp"], 1)
                    if kc and dst_hi is not None:
                        low(kc - 1)
                if dst_hi is not None:
                    low(chunks - 1)

            def mod_cols(layer, a, b, bias, parts):
                for v in range(2):
                    dve.tensor_tensor(mod[layer][:, a:b, v], ada_ps[:, a:b, v], bias[:, a:b], ALU.add)\
                       .then_inc(s_mod, 1)

            def gains(layer, which):
                r0 = ROWS_A["norm_g"][0] + (2 * layer + which) * KC
                for v in range(2):
                    dve.scalar_tensor_tensor(out=gain[layer][:, which, :, v],
                                             in0=mod[layer][:, 24 * which + 8:24 * which + 16, v], scalar=1.0,
                                             in1=cols_a[:, r0:r0 + KC], op0=ALU.add, op1=ALU.mult).then_inc(s_mod, 1)

            dve.memset(eps_col[:, :], EPS).then_inc(s_eps, 1)
            for kc in range(0, KC, 2):
                dve.wait_ge(s_xT, kc + 1)
                dve.tensor_copy(x_t[:, kc, :], B[2 + kc % 4][:, :]).then_inc(s_xc, 1)
            dve.wait_ge(s_cr, 3)
            dve.tensor_tensor(rw_lo[:, :, :], rw[:, :, :], rw_hi[:, :, :].bitcast(f32), ALU.subtract)\
               .then_inc(s_rwlo, 1)
            for n, size in enumerate((2048, 1024, 2304)):
                lo_of(n % SLOTS, size, n + 1)
            a0 = ROWS_A["ada_b0"][0]
            bias0 = cols_a[:, a0:a0 + NMOD]
            dve.wait_ge(ada_used, ADA_FIRST)
            dve.wait_ge(s_cols, 2)
            mod_cols(0, 0, 16, bias0, 2)
            dve.wait_ge(s_mod, 2)
            gains(0, 0)
            dve.wait_ge(s_mod, 4)
            ga = [[gain[l][:, w] for w in range(2)] for l in range(2)]
            norm("n01", KC, T, lambda kc, cs: x_t[:, kc, cs], lambda kc, v: ga[0][0][:, kc, v:v + 1],
                 norms_of(0, 0)[1], h_hi, h_lo, 2)
            qg, kvg = ROWS_A["q_norm_g"][0], ROWS_A["kv_norm_g"][0]
            norm("nq", 3, T, lambda kc, cs: B[kc][:, cs], lambda kc, v: cols_a[:, qg + kc:qg + kc + 1],
                 None, qa_hi, qa_lo, 1)
            norm("nc", 2, T, lambda kc, cs: B[3 + kc][:, cs], lambda kc, v: cols_a[:, kvg + kc:kvg + kc + 1],
                 None, ca_hi, ca_lo, 1)
            rr = slice(NOPE, QKD)
            dve.wait_ge(s_krr, 1)
            dve.tensor_tensor(kr_rot[rr, :], B[5][rr, 0:TL], cs_mla[rr, 1, 0, :], ALU.mult).then_inc(s_kr, 1)
            dve.tensor_tensor(kr[rr, LAT], kr[rr, LAT], cs_mla[rr, 0, 0, :], ALU.mult).then_inc(s_kr, 1)
            dve.wait_ge(s_kr, 2)
            dve.tensor_tensor(kr[rr, LAT], kr[rr, LAT], kr_rot[rr, :], ALU.add).then_inc(s_kr, 1)
            dve.wait_ge(s_krhi, 2)
            for j in range(2):
                dve.tensor_tensor(mk_lo[rr, j, :], kr[rr, :], mk_hi[rr, j, :].bitcast(f32), ALU.subtract)\
                   .then_inc(s_krlo, 1)

            def mla_max(i, u):
                dve.wait_ge(m["scores"], i * 6 + (u + 1))
                if u % 3 < 2:
                    dve.tensor_reduce(nmax[:, u % 3, 0:1], B[u % 3][:, :], AX.X, ALU.max, negate=True)\
                       .then_inc(m["max"], 1)
                else:
                    dve.tensor_reduce(nmax[:, 2, :], B[2][:, :].rearrange("p (t k) -> p t k", t=2), AX.X, ALU.max,
                                      negate=True).then_inc(m["max"], 1)

            def mla_rsum(i, u):
                dve.wait_ge(m["exp"], ONE + i * 6 + (u + 1))
                w = 1 if u % 3 < 2 else 2
                dve.reciprocal(rsum[:, u % 3, 0:w], psum_e[:, u % 3, 0:w]).then_inc(m["rsum"], 1)

            def mla_p_lo(i, u):
                dve.wait_ge(m["p_hi"], i * 6 + (u + 1))
                turned = B[3 + u % 2]
                if u % 3 < 2:
                    cs = slice((u % 3) * P, (u % 3 + 1) * P)
                    dve.tensor_tensor(pl_lo[:, :, cs], turned[:, :].rearrange("p (c q) -> p c q", c=4),
                                      pl_hi[:, :, cs].bitcast(f32), ALU.subtract).then_inc(m["p_lo"], 1)
                else:
                    dve.tensor_tensor(pc_lo[:, :, :], turned[:, :].rearrange("p (c q) -> p c q", c=2),
                                      pc_hi[:, :, :].bitcast(f32), ALU.subtract).then_inc(m["p_lo"], 1)

            def mla_o_lo(i, j):
                dve.wait_ge(m["o_hi"], i * 2 + (j + 1))
                rows = slice(HD * j, HD * (j + 1))
                dve.tensor_tensor(h_lo[rows, i, :], B[5 + j][rows, :], h_hi[rows, i, :].bitcast(f32), ALU.subtract)\
                   .then_inc(m["o_lo"], 1)

            with dve.Fori(0, H // 2) as i:
                dve.wait_ge(m["w_hi"], i * 2 + 1)
                dve.tensor_tensor(uq_lo[:, :, :], uq_raw[:, :, bass.ds(i * (2 * QKD), 2 * QKD)],
                                  uq_hi[:, :, :].bitcast(f32), ALU.subtract).then_inc(m["w_lo"], 1)
                dve.wait_ge(m["w_hi"], i * 2 + 2)
                dve.tensor_tensor(ukv_lo[:, :, :], ukv_raw[:, :, bass.ds(i * 256, 256)],
                                  ukv_hi[:, :, :].bitcast(f32), ALU.subtract).then_inc(m["w_lo"], 1)
                for j in range(2):
                    dve.wait_ge(m["kv_hi"], i * 3 + (j + 1))
                    dve.tensor_tensor(mk_lo[0:NOPE, j, :], B[2 + j][0:NOPE, :], mk_hi[0:NOPE, j, :].bitcast(f32),
                                      ALU.subtract).then_inc(m["kv_lo"], 1)
                dve.wait_ge(m["kv_hi"], i * 3 + 3)
                dve.tensor_tensor(mv_lo[:, :, :], B[4][:, :].rearrange("p (t n) -> p t n", t=4),
                                  mv_hi[:, :, :].bitcast(f32), ALU.subtract).then_inc(m["kv_lo"], 1)
                dve.wait_ge(m["rot"], i + 1)
                dve.tensor_tensor(mq_rot[rr, :, :], B[5][rr, :].rearrange("p (j t) -> p j t", j=2),
                                  cs_mla[rr, 1, :, :], ALU.mult).then_inc(m["rope"], 1)
                dve.tensor_tensor(mq[rr, :, LAT], mq[rr, :, LAT], cs_mla[rr, 0, :, :], ALU.mult)\
                   .then_inc(m["rope"], 1)
                dve.wait_ge(m["rope"], i * 3 + 2)
                dve.tensor_tensor(mq[rr, :, LAT], mq[rr, :, LAT], mq_rot[rr, :, :], ALU.add).then_inc(m["rope"], 1)
                dve.wait_ge(m["q_hi"], i + 1)
                dve.tensor_tensor(mq_lo[:, :, :], mq[:, :, :], mq_hi[:, :, :].bitcast(f32), ALU.subtract)\
                   .then_inc(m["q_lo"], 1)
                mla_max(i, 0)
                mla_max(i, 1)
                mla_rsum(i, 0)
                mla_max(i, 2)
                mla_rsum(i, 1)
                mla_p_lo(i, 0)
                mla_rsum(i, 2)
                mla_max(i, 3)
                mla_p_lo(i, 1)
                mla_rsum(i, 3)
                mla_p_lo(i, 2)
                mla_max(i, 4)
                mla_rsum(i, 4)
                mla_o_lo(i, 0)
                mla_p_lo(i, 3)
                mla_max(i, 5)
                mla_rsum(i, 5)
                mla_p_lo(i, 4)
                mla_p_lo(i, 5)
                mla_o_lo(i, 1)

            dve.wait_ge(ada_used, ADA_TILES)
            mod_cols(0, 16, NMOD, bias0, 2)
            dve.wait_ge(s_mod, 6)
            gains(0, 1)
            dve.wait_ge(s_mod, 8)

            def add_out(layer, mc, bank, parts, which, done):
                for v in range(parts):
                    last = dve.scalar_tensor_tensor(out=x_t[:, mc, HALVES[v]], in0=bank[:, HALVES[v]],
                                                    scalar=mod[layer][:, 8 * which + mc, v:v + 1],
                                                    in1=x_t[:, mc, HALVES[v]], op0=ALU.mult, op1=ALU.add)
                last.then_inc(done, 1)

            def wo_phase(layer, base, cols, parts):
                mc = 0
                sizes = [KC * w for w in cols]
                for k in range(min(2, len(cols))):
                    lo_of((base + k) % SLOTS, sizes[k], base + k + 1)
                for k, w in enumerate(cols):
                    if k + 2 < len(cols):
                        lo_of((base + k + 2) % SLOTS, sizes[k + 2], base + k + 3)
                    for j in range(w // P):
                        dve.wait_ge(wo[layer]["done"], mc + 1)
                        add_out(layer, mc, B[mc % 2], parts, 2, wo[layer]["added"])
                        mc += 1

            def ffn_body(q, layer, e, base, nt, parts, last, tail):
                for s, item in enumerate(ITEMS):
                    if s + 2 < NITEMS or not last:
                        s2 = s + 2
                        lo_of(s2 % SLOTS, item_size(ITEMS[s2 % NITEMS]), e * NITEMS + (base + s2 + 1))
                    elif tail:
                        n, size = tail[s + 2 - NITEMS]
                        lo_of(n % SLOTS, size, n + 1)
                    if item[0] == "up":
                        k = item[3]
                        dve.wait_ge(q["silu"], e * 11 + (k + 1))
                        if k >= 2:
                            dve.wait_ge(q["hid_lo"], ONE + e * 11 + (k - 1))
                        else:
                            dve.wait_ge(q["hid_lo"], ONE + e * 11)
                        hb = hid[:, k % 2, 0:nt]
                        formed = dve.tensor_tensor(hb, B[2 * (k % 2) + 1][:, 0:nt], sil[:, k % 2, 0:nt], ALU.mult)
                        if layer == 1:
                            formed.then_inc(q["hid_w"], 1)
                            dve.wait_ge(q["hid_w"], e * 11 + (k + 1))
                            formed = dve.tensor_tensor(hb, hb, cb[:, e, :], ALU.mult)
                        formed.then_inc(q["hid"], 1)
                    else:
                        _, gr, n_out, _, m0 = item
                        for j in range(n_out):
                            dve.wait_ge(q["pe"], ONE + e * PER_EXP + (DONE_BY_ITEM[s] + j + 1))
                            dve.wait_ge(q["added"], ONE + e * 16 + (m0 + j + 1 if gr else 0))
                            add_out(layer, m0 + j, B[4 + (m0 + j) % 3], parts, 5, q["added"])

            def ffn(q, layer, n_exp, base, nt, parts, tail):
                with dve.Fori(0, n_exp - 1) as e:
                    ffn_body(q, layer, e, base, nt, parts, False, None)
                ffn_body(q, layer, n_exp - 1, base, nt, parts, True, tail)

            wo_phase(0, BASE_WO0, WO_COLS_0, 2)
            for s in range(2):
                lo_of((BASE_FFN0 + s) % SLOTS, item_size(ITEMS[s]), BASE_FFN0 + s + 1)
            dve.wait_ge(wo[0]["added"], KC)
            norm("n02", KC, T, lambda kc, cs: x_t[:, kc, cs], lambda kc, v: ga[0][1][:, kc, v:v + 1],
                 norms_of(0, 1)[1], h_hi, h_lo, 2)
            ffn(ff[0], 0, 2, BASE_FFN0, T, 2, [(BASE_KV1, 2048), (BASE_KV1 + 1, 2048)])

            dve.wait_ge(ada_used, 2 * ADA_TILES)
            mod_cols(1, 0, NMOD, cols_b, 2)
            dve.wait_ge(s_mod, 10)
            gains(1, 0)
            gains(1, 1)
            dve.wait_ge(s_mod, 14)
            dve.wait_ge(ff[0]["added"], ONE + 32)
            norm("n11", KC, T, lambda kc, cs: x_t[:, kc, cs], lambda kc, v: ga[1][0][:, kc, v:v + 1],
                 norms_of(1, 0)[1], h_hi, h_lo, 2)
            dve.wait_ge(s_krot1, 1)
            dve.tensor_tensor(kf_rot[:, :, :], B[4][:, :].rearrange("p (c t) -> p c t", c=2), cs_gqa[:, 1],
                              ALU.mult).then_inc(s_krope1, 1)
            dve.tensor_tensor(kf[:, :, LAT], kf[:, :, LAT], cs_gqa[:, 0], ALU.mult).then_inc(s_krope1, 1)
            dve.wait_ge(s_krope1, 2)
            dve.tensor_tensor(kf[:, :, LAT], kf[:, :, LAT], kf_rot[:, :, :], ALU.add).then_inc(s_krope1, 1)
            for b in range(2):
                dve.wait_ge(s_v1hi, b + 1)
                dve.tensor_tensor(v_lo[:, 2 * b:2 * b + 2, :], B[2 + b][:, :].rearrange("p (t n) -> p t n", t=2),
                                  v_hi[:, 2 * b:2 * b + 2, :].bitcast(f32), ALU.subtract).then_inc(s_v1lo, 1)
            for gg in range(4):
                rows = slice(HD * (gg % 2), HD * (gg % 2 + 1))
                dve.wait_ge(s_kdup_hi, gg + 1)
                dve.tensor_tensor(k_lo[rows, gg, :], kf[rows, gg // 2, :], k_hi[rows, gg, :].bitcast(f32),
                                  ALU.subtract).then_inc(s_kdup_lo, 1)

            def g_max(gi, u):
                dve.wait_ge(g["scores"], gi * 8 + (u + 1))
                dve.tensor_reduce(mraw[:, u % 3, 0:1], B[u % 3][:, :], AX.X, ALU.max).then_inc(g["max"], 1)
                dve.wait_ge(g["max"], gi * 8 + (u + 1))
                dve.tensor_scalar(nmax[:, u % 3, 0:1], mraw[:, u % 3, 0:1], sink_g[:, u // 2:u // 2 + 1], -1.0,
                                  ALU.max, ALU.mult).then_inc(g["nmax"], 1)

            def g_rsum(gi, u):
                dve.wait_ge(g["esink"], gi * 8 + (u + 1))
                dve.tensor_tensor(mraw[:, u % 3, 1:2], psum_e[:, u % 3, 0:1], esink[:, u % 3, 0:1], ALU.add)\
                   .then_inc(g["sum"], 1)
                dve.wait_ge(g["sum"], gi * 8 + (u + 1))
                dve.reciprocal(rsum[:, u % 3, 0:1], mraw[:, u % 3, 1:2]).then_inc(g["rsum"], 1)

            def g_p_lo(gi, u):
                dve.wait_ge(g["p_hi"], gi * 8 + (u + 1))
                cs = slice((u % 2) * P, (u % 2 + 1) * P)
                dve.tensor_tensor(gt_lo[:, :, cs], B[3 + u % 2][:, :].rearrange("p (c q) -> p c q", c=4),
                                  gt_hi[:, :, cs].bitcast(f32), ALU.subtract).then_inc(g["p_lo"], 1)

            def g_o_lo(gi, j):
                dve.wait_ge(g["o_hi"], gi * 4 + (j + 1))
                rows = slice(HD * (j % 2), HD * (j % 2 + 1))
                dve.tensor_tensor(o_lo[rows, gi * 2 + j // 2, :], B[5 + j % 2][rows, 0:TL],
                                  o_hi[rows, gi * 2 + j // 2, :].bitcast(f32), ALU.subtract).then_inc(g["o_lo"], 1)

            with dve.Fori(0, 4) as gi:
                dve.wait_ge(qw_hi, gi + 1)
                dve.tensor_tensor(w_lo[:, Q_SLOT, 0:2048], raw[:, Q_SLOT, 0:2048],
                                  w_hi[:, Q_SLOT, 0:2048].bitcast(f32), ALU.subtract).then_inc(qw_lo, 1)
                dve.wait_ge(g["rot"], gi + 1)
                dve.tensor_tensor(g_rot[:, :, :], B[2][:, :].rearrange("p (j t) -> p j t", j=2), cs_gqa[:, 1],
                                  ALU.mult).then_inc(g["rope"], 1)
                dve.tensor_tensor(gq[:, :, :], gq[:, :, :], cs_gqa[:, 0], ALU.mult).then_inc(g["rope"], 1)
                dve.wait_ge(g["rope"], gi * 3 + 2)
                dve.tensor_tensor(gq[:, :, :], gq[:, :, :], g_rot[:, :, :], ALU.add).then_inc(g["rope"], 1)
                dve.wait_ge(g["q_hi"], gi + 1)
                dve.tensor_tensor(gq_lo[:, :, :], gq[:, :, :], gq_hi[:, :, :].bitcast(f32), ALU.subtract)\
                   .then_inc(g["q_lo"], 1)
                dve.wait_ge(g["kv_copied"], gi * 7 + 7)
                g_max(gi, 0)
                g_max(gi, 1)
                g_rsum(gi, 0)
                for u in range(8):
                    if u + 2 < 8:
                        g_max(gi, u + 2)
                    if u + 1 < 8:
                        g_rsum(gi, u + 1)
                    g_p_lo(gi, u)
                    if u % 2 == 0 and u >= 2:
                        g_o_lo(gi, u // 2 - 1)
                g_o_lo(gi, 3)

            wo_phase(1, BASE_WO1, WO_COLS_1, 1)
            for s in range(2):
                lo_of((BASE_FFN1 + s) % SLOTS, item_size(ITEMS[s]), BASE_FFN1 + s + 1)
            dve.wait_ge(wo[1]["added"], KC)
            norm("n12", KC, TL, lambda kc, cs: x_t[:, kc, cs], lambda kc, v: ga[1][1][:, kc, 0:1],
                 norms_of(1, 1)[1], h_hi, h_lo, 1)
            dve.wait_ge(s_lgp, 1)
            for t in range(2):
                dve.tensor_tensor(lg[:, t, :], B[0][:, t * NEXP:(t + 1) * NEXP], rb_b[:, :], ALU.add)\
                   .then_inc(s_rs, 1)
            dve.wait_ge(s_rs, 2)
            for t in range(2):
                dve.max(top[:, t, :], lg[:, t, :]).then_inc(s_rs, 1)
            dve.wait_ge(s_rs, 4)
            for t in range(2):
                dve.max_index(top_i[:, t, :], top[:, t, :], lg[:, t, :]).then_inc(s_rt, 1)
            dve.tensor_tensor(gate[:, :, 0:1], top[:, :, 1:2], top[:, :, 0:1], ALU.subtract).then_inc(s_rt, 1)
            dve.wait_ge(s_rt, 3)
            dve.tensor_copy(top_f[:, :, :], top_i[:, :, :]).then_inc(s_rs, 1)
            dve.wait_ge(s_gx, 1)
            dve.tensor_scalar(gate[:, :, 2:3], gate[:, :, 1:2], 1.0, None, ALU.add).then_inc(s_rs, 1)
            dve.wait_ge(s_rs, 6)
            dve.reciprocal(gate[:, :, 3:4], gate[:, :, 2:3]).then_inc(s_rs, 1)
            dve.wait_ge(s_rs, 7)
            dve.tensor_tensor(gate[:, :, 2:3], gate[:, :, 1:2], gate[:, :, 3:4], ALU.mult).then_inc(s_rs, 1)
            dve.wait_ge(s_rs, 8)
            for t in range(2):
                dve.tensor_scalar(comb[:, t, :], iota[:, :], top_f[:, t, 0:1], gate[:, t, 3:4], ALU.is_equal,
                                  ALU.mult).then_inc(s_rs, 1)
                dve.tensor_scalar(hot[:, t, :], iota[:, :], top_f[:, t, 1:2], gate[:, t, 2:3], ALU.is_equal,
                                  ALU.mult).then_inc(s_rs, 1)
            dve.wait_ge(s_rs, 12)
            dve.tensor_tensor(comb[:, :, :], comb[:, :, :], hot[:, :, :], ALU.add).then_inc(s_rs, 1)
            dve.wait_ge(s_rs, 13)
            for t in range(2):
                for e in range(NEXP):
                    dve.tensor_scalar(comb_rep[:, t, e, :], ones[:, :], comb[:, t, e:e + 1], None, ALU.mult)\
                       .then_inc(s_rs, 1)
            dve.wait_ge(s_cb, 4)
            ffn(ff[1], 1, NEXP, BASE_FFN1, TL, 1, None)
            dve.wait_ge(ff[1]["added"], ONE + 16 * NEXP)
            fg = ROWS_A["final_g"][0]
            norm("nf", KC, TL, lambda kc, cs: x_t[:, kc, cs], lambda kc, v: cols_a[:, fg + kc:fg + kc + 1],
                 None, None, None, 1)
            for t in range(2):
                for b in range(2):
                    dve.wait_ge(s_oT, 2 * t + b + 1)
                    dve.tensor_copy(out_rows[:, t, b * 512:(b + 1) * 512], B[2 * t + b][:, :]).then_inc(s_orow, 2)

        @block.tensor
        def _(pe):
            def mm(out_, lhs, rhs, start, stop):
                return pe.matmul(out_, lhs, rhs, start=start, stop=stop, skip_group_check=True)

            def three(out_, wh, wl, xh, xl, first, last):
                mm(out_, wh, xh, first, False)
                mm(out_, wh, xl, False, False)
                return mm(out_, wl, xh, False, last)

            def slot_view(t, slot, nk, cols):
                return t[:, slot, 0:nk * cols].rearrange("p (k n) -> p k n", k=nk)

            def ada(slot, full, m0):
                pe.wait_ge(ada_full[slot], full)
                for j in range(2):
                    for kc in range(KC):
                        last = mm(ada_ps_at(m0, j), ada_raw[:, slot, kc, j * P:(j + 1) * P], silu_c[:, kc, :],
                                  kc == 0, kc == KC - 1)
                last.then_inc(ada_used, 1)

            def ada_ps_at(m0, j):
                return ADA_BANK[:, bass.ds(m0 * 2 + 2 * j, 2)]

            def norm_sum(key, chunks, nt, bank):
                for kc in range(chunks):
                    pe.wait_ge(*normed(key, "sq", kc + 1))
                    last = mm(bank[:, 0:nt], ones[:, :], sq[:, kc, 0:nt], kc == 0, kc == chunks - 1)
                last.then_inc(norm_sem["sum"], 1)

            def chunk_wait(key, kc, parts):
                pe.wait_ge(*normed(key, "hi", parts * (kc + 1)))
                pe.wait_ge(*normed(key, "lo", parts * (kc + 1)))

            pe.wait_ge(s_id, 16)
            pe.wait_ge(s_vec, 128)
            pe.transpose(B[0][:, 0:NROWS_A], rows_a[0:NROWS_A, :], ident[0:NROWS_A, 0:NROWS_A]).then_inc(s_vecT, 1)
            pe.transpose(B[1][:, 0:NMOD], rows_b[:, :], ident[0:NMOD, 0:NMOD]).then_inc(s_vecT, 1)
            pe.wait_ge(s_x, 32)
            for kc in range(KC):
                if kc >= 4:
                    pe.wait_ge(s_xc1 if kc % 2 else s_xc, kc // 2 - 1)
                for t in range(4):
                    last = pe.transpose(B[2 + kc % 4][:, t * P:(t + 1) * P], x_rows[:, t, kc * P:(kc + 1) * P],
                                        ident[:, :])
                last.then_inc(s_xT, 1)
            pe.wait_ge(s_silu, 2)
            for a in range(ADA_FIRST):
                ada(a % 2, 16 * (a // 2 + 1), 2 * a)
            pe.wait_ge(s_ones, 1)
            norm_sum("n01", KC, T, B[6])

            pe.wait_ge(s_cols, 2)
            pe.wait_ge(s_xc, 4)
            pe.wait_ge(s_xc1, 4)
            bank = 0
            for n, cols in enumerate((256, 128, KVL + ROPE)):
                pe.wait_ge(split_hi, n + 1)
                pe.wait_ge(split_lo, n + 1)
                wh, wl = slot_view(w_hi, n, KC, cols), slot_view(w_lo, n, KC, cols)
                for c0 in range(0, cols, P):
                    c1 = min(c0 + P, cols)
                    for kc in range(KC):
                        if bank == 0:
                            chunk_wait("n01", kc, 2)
                        last = three(B[bank][0:c1 - c0, :], wh[:, kc, c0:c1], wl[:, kc, c0:c1], h_hi[:, kc, :],
                                     h_lo[:, kc, :], kc == 0, kc == KC - 1)
                    last.then_inc(s_pj, 1)
                    bank += 1
            rr = slice(NOPE, QKD)
            norm_sum("nq", 3, T, B[6])
            pe.wait_ge(s_pje, 1)
            pe.wait_ge(s_const, 16 * 9)
            mm(B[5][0:QKD, 0:TL], rot_mla[rr, :], kr[rr, LAT], True, True).then_inc(s_krr, 1)
            pe.wait_ge(*normed("nq", "rms", 1))
            norm_sum("nc", 2, T, B[6])

            chunk_wait("nq", 2, 1)
            chunk_wait("nc", 1, 1)
            pe.wait_ge(s_krhi, 2)
            pe.wait_ge(s_krlo, 2)
            pe.wait_ge(s_mod, 4)

            def mla_scores(i, u):
                j, t = divmod(u, 3)
                if u >= 3:
                    pe.wait_ge(m["exp"], ONE + i * 6 + (u - 2))
                if t < 2:
                    qs = slice(t * P, (t + 1) * P)
                    last = three(B[t][:, :], mq_hi[:, j, qs], mq_lo[:, j, qs], mk_hi[:, j, :], mk_lo[:, j, :],
                                 True, True)
                else:
                    for t2 in range(2):
                        qs = slice(TL + t2 * P, TL + (t2 + 1) * P)
                        last = three(B[2][:, t2 * TL:(t2 + 1) * TL], mq_hi[:, j, qs], mq_lo[:, j, qs],
                                     mk_hi[:, j, CTX], mk_lo[:, j, CTX], True, True)
                last.then_inc(m["scores"], 1)

            def mla_turn(i, u):
                pe.wait_ge(m["normed"], i * 12 + (2 * u + 2))
                if u >= 2:
                    pe.wait_ge(m["p_lo"], ONE + i * 6 + (u - 1))
                for b in range(4):
                    src = b * P if u % 3 < 2 else (b % 2) * TL + (b // 2) * P
                    last = pe.transpose(B[3 + u % 2][:, b * P:(b + 1) * P], mp[:, u % 3, src:src + P], ident[:, :])
                last.then_inc(m["turned"], 1)

            def mla_pv(i, j):
                pe.wait_ge(m["p_hi"], i * 6 + (3 * j + 3))
                pe.wait_ge(m["p_lo"], ONE + i * 6 + (3 * j + 3))
                for b in range(4):
                    three(B[5 + j][:, LAT], mv_hi[:, b, :], mv_lo[:, b, :], pl_hi[:, b, :], pl_lo[:, b, :],
                          b == 0, b == 3)
                for b in range(2):
                    last = three(B[5 + j][:, CTX], mv_hi[:, 2 + b, :], mv_lo[:, 2 + b, :], pc_hi[:, b, :],
                                 pc_lo[:, b, :], b == 0, b == 1)
                last.then_inc(m["pv"], 1)

            with pe.Fori(0, H // 2) as i:
                pe.wait_ge(m["w_hi"], i * 2 + 2)
                pe.wait_ge(m["w_lo"], i * 2 + 2)
                pe.wait_ge(m["exp"], ONE + i * 6)
                pe.wait_ge(m["p_lo"], ONE + i * 6)
                pe.wait_ge(m["o_lo"], ONE + i * 2)
                for j in range(2):
                    for kc in range(QL // P):
                        cs = slice(j * QKD, (j + 1) * QKD)
                        last = three(B[j][0:QKD, :], uq_hi[:, kc, cs], uq_lo[:, kc, cs], qa_hi[:, kc, :],
                                     qa_lo[:, kc, :], kc == 0, kc == QL // P - 1)
                    last.then_inc(m["proj"], 1)
                for j in range(2):
                    for kc in range(KVL // P):
                        cs = slice(j * 128, j * 128 + NOPE)
                        last = three(B[2 + j][0:NOPE, :], ukv_hi[:, kc, cs], ukv_lo[:, kc, cs], ca_hi[:, kc, :],
                                     ca_lo[:, kc, :], kc == 0, kc == KVL // P - 1)
                    last.then_inc(m["proj"], 1)
                for t in range(4):
                    ts = slice(t * P, (t + 1) * P)
                    for kc in range(KVL // P):
                        vh = ukv_hi[:, kc, :].rearrange("p (j n) -> p j n", j=2)[:, :, NOPE:]
                        vl = ukv_lo[:, kc, :].rearrange("p (j n) -> p j n", j=2)[:, :, NOPE:]
                        last = three(B[4][:, ts].rearrange("p (j n) -> p j n", j=2), ca_hi[:, kc, ts],
                                     ca_lo[:, kc, ts], vh, vl, kc == 0, kc == KVL // P - 1)
                last.then_inc(m["proj"], 1)
                ada(0, i * 16 + 16 * (ADA_FIRST // 2 + 1), i * 4 + 2 * ADA_FIRST)
                pe.wait_ge(m["q_f32"], i * 2 + 2)
                mm(B[5][0:QKD, :].rearrange("p (j t) -> p j t", j=2), rot_mla[rr, :], mq[rr, :, LAT], True, True)\
                    .then_inc(m["rot"], 1)
                ada(1, i * 16 + 16 * (ADA_FIRST // 2 + 1), i * 4 + 2 * (ADA_FIRST + 1))
                pe.wait_ge(m["q_hi"], i + 1)
                pe.wait_ge(m["q_lo"], i + 1)
                pe.wait_ge(m["kv_lo"], i * 3 + 3)
                mla_scores(i, 0)
                mla_scores(i, 1)
                mla_scores(i, 2)
                mla_turn(i, 0)
                mla_scores(i, 3)
                mla_turn(i, 1)
                mla_turn(i, 2)
                mla_scores(i, 4)
                mla_pv(i, 0)
                mla_turn(i, 3)
                mla_scores(i, 5)
                mla_turn(i, 4)
                mla_turn(i, 5)
                mla_pv(i, 1)

            def out_proj(layer, base, cols, yh, yl, nt):
                mc = 0
                for k, w in enumerate(cols):
                    n = base + k
                    pe.wait_ge(split_hi, n + 1)
                    pe.wait_ge(split_lo, n + 1)
                    wh, wl = slot_view(w_hi, n % SLOTS, KC, w), slot_view(w_lo, n % SLOTS, KC, w)
                    for j in range(w // P):
                        if mc >= 2:
                            pe.wait_ge(wo[layer]["added"], mc - 1)
                        for kc in range(KC):
                            last = three(B[mc % 2][:, 0:nt], wh[:, kc, j * P:(j + 1) * P],
                                         wl[:, kc, j * P:(j + 1) * P], yh[:, kc, 0:nt], yl[:, kc, 0:nt],
                                         kc == 0, kc == KC - 1)
                        last.then_inc(wo[layer]["done"], 1)
                        mc += 1

            def ffn(q, e, base, nt, with_ada):
                for s, (kind, gr, k, f0, m0) in enumerate(ITEMS):
                    slot = s % SLOTS
                    pe.wait_ge(split_hi, e * NITEMS + (base + s + 1))
                    pe.wait_ge(split_lo, e * NITEMS + (base + s + 1))
                    if kind == "up":
                        pe.wait_ge(q["hid"], ONE + e * 11 + max(f0 - 1, 0))
                        wh, wl = slot_view(w_hi, slot, KC, 256), slot_view(w_lo, slot, KC, 256)
                        for half in range(2):
                            cs = slice(half * P, (half + 1) * P)
                            for kc in range(KC):
                                last = three(B[2 * (f0 % 2) + half][:, 0:nt], wh[:, kc, cs], wl[:, kc, cs],
                                             h_hi[:, kc, 0:nt], h_lo[:, kc, 0:nt], kc == 0, kc == KC - 1)
                        last.then_inc(q["pe"], 1)
                    else:
                        nf = GROUPS[gr][1]
                        wh, wl = slot_view(w_hi, slot, nf, k * P), slot_view(w_lo, slot, nf, k * P)
                        for j in range(k):
                            pe.wait_ge(q["added"], ONE + e * 16 + (8 * gr + max(m0 + j - 2, 0)))
                            if j == 0:
                                pe.wait_ge(q["hid_lo"], ONE + e * 11 + (f0 + nf - 1))
                            for kc in range(nf - 1):
                                three(B[4 + (m0 + j) % 3][:, 0:nt], wh[:, kc, j * P:(j + 1) * P],
                                      wl[:, kc, j * P:(j + 1) * P], hid_hi[:, kc, 0:nt], hid_lo[:, kc, 0:nt],
                                      kc == 0, False)
                        pe.wait_ge(q["hid_lo"], ONE + e * 11 + (f0 + nf))
                        for j in range(k):
                            three(B[4 + (m0 + j) % 3][:, 0:nt], wh[:, nf - 1, j * P:(j + 1) * P],
                                  wl[:, nf - 1, j * P:(j + 1) * P], hid_hi[:, nf - 1, 0:nt],
                                  hid_lo[:, nf - 1, 0:nt], False, True).then_inc(q["pe"], 1)
                    if with_ada and s < ADA_TILES // 2:
                        ada(s % 2, e * (16 * ADA_TILES // 4) + 16 * (ADA_TILES // 2 + s // 2 + 1),
                            e * ADA_TILES + 2 * s)

            pe.wait_ge(m["o_hi"], H)
            pe.wait_ge(m["o_lo"], ONE + H)
            out_proj(0, BASE_WO0, WO_COLS_0, h_hi, h_lo, T)
            norm_sum("n02", KC, T, B[6])
            chunk_wait("n02", KC - 1, 2)
            pe.wait_ge(s_mod, 8)
            with pe.Fori(0, 2) as e:
                ffn(ff[0], e, BASE_FFN0, T, True)

            norm_sum("n11", KC, T, B[6])
            chunk_wait("n11", KC - 1, 2)
            pe.wait_ge(split_hi, BASE_KV1 + 1)
            pe.wait_ge(split_lo, BASE_KV1 + 1)
            kh, kl = slot_view(w_hi, 0, KC, 256), slot_view(w_lo, 0, KC, 256)
            for c2 in range(2):
                cs = slice(c2 * P, (c2 + 1) * P)
                for kc in range(KC):
                    last = three(B[c2][:, :], kh[:, kc, cs], kl[:, kc, cs], h_hi[:, kc, :], h_lo[:, kc, :],
                                 kc == 0, kc == KC - 1)
                last.then_inc(s_kv1, 1)
            pe.wait_ge(split_hi, BASE_KV1 + 2)
            pe.wait_ge(split_lo, BASE_KV1 + 2)
            vh, vl = slot_view(w_hi, 1, KC, 256), slot_view(w_lo, 1, KC, 256)
            for t in range(4):
                ts = slice(t * P, (t + 1) * P)
                for kc in range(KC):
                    last = three(B[2 + t // 2][:, (t % 2) * 256:(t % 2 + 1) * 256], h_hi[:, kc, ts],
                                 h_lo[:, kc, ts], vh[:, kc, :], vl[:, kc, :], kc == 0, kc == KC - 1)
                if t % 2:
                    last.then_inc(s_kv1, 1)
            pe.wait_ge(s_kf, 2)
            mm(B[4][:, :].rearrange("p (c t) -> p c t", c=2), rot_gqa[:, :], kf[:, :, LAT], True, True)\
                .then_inc(s_krot1, 1)
            pe.wait_ge(s_v1lo, 2)
            pe.wait_ge(s_krope1, 3)
            pe.wait_ge(s_cr, 3)

            def g_scores(gi, u):
                j, t = divmod(u, 2)
                if u >= 3:
                    pe.wait_ge(g["exp"], ONE + gi * 8 + (u - 2))
                rows, qs = slice(HD * (j % 2), HD * (j % 2 + 1)), slice(t * P, (t + 1) * P)
                three(B[u % 3][:, :], gq_hi[rows, j // 2, qs], gq_lo[rows, j // 2, qs], gk_hi[rows, :],
                      gk_lo[rows, :], True, False)
                mm(B[u % 3][:, (1 - t) * P:(2 - t) * P], ident_r[:, :], mask_r[:, t, :], False, True)\
                    .then_inc(g["scores"], 1)

            def g_turn(gi, u):
                pe.wait_ge(g["normed"], gi * 8 + (u + 1))
                pe.wait_ge(g["p_lo"], ONE + gi * 8 + max(u - 1, 0))
                for b in range(4):
                    last = pe.transpose(B[3 + u % 2][:, b * P:(b + 1) * P], gp[:, u % 3, b * P:(b + 1) * P],
                                        ident[:, :])
                last.then_inc(g["turned"], 1)

            def g_pv(gi, j):
                pe.wait_ge(g["p_hi"], gi * 8 + (2 * j + 2))
                pe.wait_ge(g["p_lo"], ONE + gi * 8 + (2 * j + 2))
                pe.wait_ge(g["o_lo"], ONE + gi * 4 + max(j - 1, 0))
                for b in range(4):
                    last = three(B[5 + j % 2][:, 0:TL], gv_hi[:, b, :], gv_lo[:, b, :], gt_hi[:, b, :],
                                 gt_lo[:, b, :], b == 0, b == 3)
                last.then_inc(g["pv"], 1)

            with pe.Fori(0, 4) as gi:
                pe.wait_ge(qw_hi, gi + 1)
                pe.wait_ge(qw_lo, ONE + gi + 1)
                pe.wait_ge(g["exp"], ONE + gi * 8)
                for j in range(2):
                    qh, ql = slot_view(w_hi, Q_SLOT, KC, 256), slot_view(w_lo, Q_SLOT, KC, 256)
                    for kc in range(KC):
                        cs = slice(j * P, (j + 1) * P)
                        last = three(B[j][:, 0:TL], qh[:, kc, cs], ql[:, kc, cs], h_hi[:, kc, LAT],
                                     h_lo[:, kc, LAT], kc == 0, kc == KC - 1)
                    last.then_inc(g["proj"], 1)
                pe.wait_ge(g["q_f32"], gi * 2 + 2)
                mm(B[2][:, :].rearrange("p (j t) -> p j t", j=2), rot_gqa[:, :], gq[:, :, :], True, True)\
                    .then_inc(g["rot"], 1)
                pe.wait_ge(g["q_hi"], gi + 1)
                pe.wait_ge(g["q_lo"], gi + 1)
                pe.wait_ge(g["kv_copied"], gi * 7 + 7)
                for u in range(3):
                    g_scores(gi, u)
                for u in range(8):
                    g_turn(gi, u)
                    if u + 3 < 8:
                        g_scores(gi, u + 3)
                    if u % 2 == 0 and u >= 2:
                        g_pv(gi, u // 2 - 1)
                g_pv(gi, 3)

            pe.wait_ge(g["o_hi"], H)
            pe.wait_ge(g["o_lo"], ONE + H)
            out_proj(1, BASE_WO1, WO_COLS_1, o_hi, o_lo, TL)
            norm_sum("n12", KC, TL, B[6])
            chunk_wait("n12", KC - 1, 1)
            pe.wait_ge(s_rwlo, 1)
            for t in range(2):
                ts = slice(t * P, (t + 1) * P)
                for kc in range(KC):
                    last = three(B[0][:, t * NEXP:(t + 1) * NEXP], h_hi[:, kc, ts], h_lo[:, kc, ts],
                                 rw_hi[:, kc, :], rw_lo[:, kc, :], kc == 0, kc == KC - 1)
            last.then_inc(s_lgp, 1)
            pe.wait_ge(s_rs, 13 + 2 * NEXP)
            for e in range(NEXP):
                for t in range(2):
                    last = mm(B[e // 2][:, (e % 2) * TL + t * P:(e % 2) * TL + (t + 1) * P], comb_rep[:, t, e, :],
                              ident[:, :], True, True)
                if e % 2:
                    last.then_inc(s_cbp, 1)
            pe.wait_ge(s_cb, 4)
            with pe.Fori(0, NEXP) as e:
                ffn(ff[1], e, BASE_FFN1, TL, False)

            norm_sum("nf", KC, TL, B[6])
            pe.wait_ge(*normed("nf", "tmp", KC))
            for t in range(2):
                for b in range(2):
                    for k in range(4):
                        last = pe.transpose(B[2 * t + b][:, k * P:(k + 1) * P],
                                            sq[:, 4 * b + k, t * P:(t + 1) * P], ident[:, :])
                    last.then_inc(s_oT, 1)


_NAMES = ("x", "c", "ctx", "c_ctx", "ada_w", "ada_b", "norm_g", "final_norm_g", "mla_w_dq", "mla_q_norm_g",
          "mla_w_uq", "mla_w_dkv", "mla_kv_norm_g", "mla_w_ukv", "mla_w_o", "swa_w_qkv", "swa_sinks", "swa_w_o",
          "ffn_w_gate_up", "ffn_w_down", "moe_router_w", "moe_router_b", "moe_w_gate_up", "moe_w_down")


def constants():
    def angles(rot_dim):
        n = rot_dim // 4
        inv = np.float32(10000.0) ** (-np.arange(n, dtype=np.float32) / np.float32(n))
        rows = np.repeat(np.arange(TL // GRID_W, dtype=np.float32), GRID_W)
        cols = np.tile(np.arange(GRID_W, dtype=np.float32), TL // GRID_W)
        return np.concatenate([rows[:, None] * inv, cols[:, None] * inv], axis=-1).astype(np.float32)

    def table(rot_dim, first, copies):
        a = angles(rot_dim).T
        out = np.zeros((P, 2, 2, TL), np.float32)
        for k in range(copies):
            for half in range(2):
                r = first + k * rot_dim + half * (rot_dim // 2)
                out[r:r + rot_dim // 2, 0] = np.cos(a)[:, None, :]
                out[r:r + rot_dim // 2, 1] = np.sin(a)[:, None, :]
        return out

    def rotation(width, rot_dim, first, copies):
        r = np.zeros((P, width), np.float32)
        half = rot_dim // 2
        for k in range(copies):
            for i in range(half):
                a = first + k * rot_dim + i
                r[a + half, a] = -1.0
                r[a, a + half] = 1.0
        return r

    q, k = np.arange(P)[:, None], np.arange(P)[None, :]
    mask = np.stack([np.where(k <= q, 0.0, NEG), np.where(k >= q, 0.0, NEG)], axis=1).astype(np.float32)
    return {
        "k_ident": np.eye(P, dtype=np.float32),
        "k_rot_mla": rotation(QKD, ROPE, NOPE, 1),
        "k_rot_gqa": rotation(P, HD, 0, 2),
        "k_cs_mla": table(ROPE, NOPE, 1),
        "k_cs_gqa": table(HD, 0, 2),
        "k_mask": mask,
        "k_iota": np.ascontiguousarray(np.broadcast_to(np.arange(NEXP, dtype=np.float32), (P, NEXP))),
    }


def kernel(**inputs):
    import concourse.bacc as bacc
    from concourse.bass_utils import run_bass_kernel_spmd

    nc = bacc.Bacc("TRN2", target_bir_lowering=False, num_devices=1)
    arrays = {f"in_{n}": np.ascontiguousarray(inputs[n]) for n in _NAMES}
    arrays.update(constants())
    args = [nc.dram_tensor(n, a.shape, mybir.dt.from_np(a.dtype), kind="ExternalInput").ap()
            for n, a in arrays.items()]
    args.append(nc.dram_tensor("out", (1, TL, D), mybir.dt.float32, kind="ExternalOutput").ap())
    build(nc, *args)
    r = run_bass_kernel_spmd(nc, [arrays], core_ids=[0])
    return r.results[0]["out"]
```

```python
import numpy as np

import concourse.bass as bass
from concourse import mybir
from contextlib import ExitStack

D = 1024
T = 512
TL = 256
GRID_W = 64
H = 16
HD = 64
QL, KVL, NOPE, ROPE = 384, 256, 64, 32
QKD = NOPE + ROPE
DFF = 2816
NEXP, EFF = 8, 1408
EPS = 1e-6
NEG = -1e30
P = 128
KC = D // P
NMOD = 6 * KC

SLOTS = 3
ONE = 1
SLOT = 2304
ADA_W = 256
ADA_FIRST = 8
ADA_TILES = 6 * D // ADA_W
GROUPS = ((0, 6, (3, 3, 2)), (6, 5, (2, 2, 2, 2)))
WO_COLS_0 = (256, 256, 256, 256)
WO_COLS_1 = (256, 256, 256, 256)


def ffn_items():
    items = []
    for g, (f0, nf, parts) in enumerate(GROUPS):
        items += [("up", g, f, f0 + f, 0) for f in range(nf)]
        m = 0
        for parted in parts:
            items.append(("down", g, parted, f0, m))
            m += parted
    return items


ITEMS = ffn_items()
NITEMS = len(ITEMS)
assert NITEMS % SLOTS == 0


def item_size(item):
    return KC * 256 if item[0] == "up" else GROUPS[item[1]][1] * item[2] * P


DONE_BY_ITEM = [0]
for _kind, _g, _k, _f, _m in ITEMS:
    DONE_BY_ITEM.append(DONE_BY_ITEM[-1] + (1 if _kind == "up" else _k))
PER_EXP = DONE_BY_ITEM[-1]
HALF_EXP = DONE_BY_ITEM[NITEMS // 2]

PROJ0_COLS = (256, 128, 288)
BASE_PROJ0 = ADA_FIRST
BASE_WO0 = BASE_PROJ0 + len(PROJ0_COLS)
BASE_FFN0 = BASE_WO0 + len(WO_COLS_0)
BASE_KV1 = BASE_FFN0 + 2 * NITEMS
BASE_WO1 = BASE_KV1 + 2
BASE_FFN1 = BASE_WO1 + len(WO_COLS_1)
ADA_MLA = ADA_TILES - ADA_FIRST
assert ADA_MLA == H and BASE_FFN0 % SLOTS == 0 and BASE_KV1 % SLOTS == 0 and BASE_FFN1 % SLOTS == 0
Q_SLOT = 2

ROWS_A = {"norm_g": (0, 32), "final_g": (32, 8), "q_norm_g": (40, 3), "kv_norm_g": (43, 2),
          "c": (45, 8), "c_ctx": (53, 8), "ada_b0": (61, NMOD)}
NROWS_A = 61 + NMOD


def build(nc, x, c, ctx_x, c_ctx, ada_w, ada_b, norm_g, final_g, w_dq, q_norm_g, w_uq, w_dkv, kv_norm_g,
          w_ukv, w_o0, w_qkv, sinks, w_o1, ffn_gu, ffn_dn, router_w, router_b, moe_gu, moe_dn,
          k_ident, k_rot_mla, k_rot_gqa, k_cs_mla, k_cs_gqa, k_mask, k_iota, out):
    f32, f32r, u32 = mybir.dt.float32, mybir.dt.float32r, mybir.dt.uint32
    ALU, ACT, AX = mybir.AluOpType, mybir.ActivationFunctionType, mybir.AxisListType
    stack = ExitStack()
    with stack:
        words = {f32: 4, f32r: 4, u32: 4}
        cursor = [16640]

        def place(name, shape, dt=f32, at=None):
            size = int(np.prod(shape[1:])) * words[dt]
            off = cursor[0] if at is None else at
            if at is None:
                cursor[0] = (off + size + 31) // 32 * 32
            return nc.alloc_sbuf_tensor_at(name, shape, dt, offset=off)

        def sem(name):
            return stack.enter_context(nc.semaphore(name))

        x_t = place("x_t", [P, KC, T])
        h_hi = place("h_hi", [P, KC, T], f32r)
        h_lo = place("h_lo", [P, KC, T], f32r)
        ident = place("ident", [P, P])
        ident_r = place("ident_r", [P, P], f32r)
        ones = place("ones", [P, P])
        rot_mla = place("rot_mla", [P, QKD])
        rot_gqa = place("rot_gqa", [P, P])
        cs_mla = place("cs_mla", [P, 2, 2, TL])
        cs_gqa = place("cs_gqa", [P, 2, 2, TL])
        mask = place("mask", [P, 2, P])
        mask_r = place("mask_r", [P, 2, P], f32r)
        iota = place("iota", [P, NEXP])
        sink_b = place("sink_b", [P, H])
        rb_b = place("rb_b", [P, NEXP])
        rw = place("rw", [P, KC, NEXP])
        rw_hi = place("rw_hi", [P, KC, NEXP], f32r)
        rw_lo = place("rw_lo", [P, KC, NEXP], f32r)
        rows_a = place("rows_a", [P, P])
        rows_b = place("rows_b", [NMOD, P])
        cols_a = place("cols_a", [P, NROWS_A])
        cols_b = place("cols_b", [P, NMOD])
        silu_c = place("silu_c", [P, KC, 2])
        c4 = place("c4", [P, KC, 4], f32r)
        mod4 = [place(f"mod4_{i}", [P, NMOD, 4]) for i in range(2)]
        mod = [place(f"mod{i}", [P, NMOD, 2]) for i in range(2)]
        gain = [place(f"gain{i}", [P, 2, KC, 2]) for i in range(2)]
        rstd = place("rstd", [P, T])
        eps_col = place("eps_col", [P, 1])
        pool_mark = place("pool_mark", [P, 1])
        ring0 = cursor[0]
        raw = place("raw", [P, SLOTS, SLOT])
        w_hi = place("w_hi", [P, SLOTS, SLOT], f32r)
        w_lo = place("w_lo", [P, SLOTS, SLOT], f32r)
        ring1 = cursor[0]
        ada_raw = place("ada_raw", [P, 2, KC // 2, ADA_W])
        ada_hi = place("ada_hi", [P, KC // 2, ADA_W], f32r)
        ada_lo = place("ada_lo", [P, KC // 2, ADA_W], f32r)
        ada_rows = place("ada_rows", [4, ADA_W])
        work0 = cursor[0]

        cursor[0] = ring0
        uq_raw = place("uq_raw", [P, QL // P, H * QKD])
        ukv_raw = place("ukv_raw", [P, KVL // P, H * 128])
        uq_hi = place("uq_hi", [P, QL // P, 2 * QKD], f32r)
        uq_lo = place("uq_lo", [P, QL // P, 2 * QKD], f32r)
        ukv_hi = place("ukv_hi", [P, KVL // P, 256], f32r)
        ukv_lo = place("ukv_lo", [P, KVL // P, 256], f32r)
        mk_hi = place("mk_hi", [QKD, 2, T], f32r)
        mk_lo = place("mk_lo", [QKD, 2, T], f32r)
        mq_hi = place("mq_hi", [QKD, 2, T], f32r)
        mq_lo = place("mq_lo", [QKD, 2, T], f32r)
        mv_hi = place("mv_hi", [P, 4, P], f32r)
        mv_lo = place("mv_lo", [P, 4, P], f32r)
        pl_hi = place("pl_hi", [P, 4, TL], f32r)
        pl_lo = place("pl_lo", [P, 4, TL], f32r)
        assert cursor[0] <= ring1, (cursor[0], ring1)
        cursor[0] = ring0 + SLOTS * SLOT * 4
        gp = place("gp", [P, 3, T])
        gt_hi = place("gt_hi", [P, 4, TL], f32r)
        gt_lo = place("gt_lo", [P, 4, TL], f32r)
        assert cursor[0] <= ring0 + (SLOTS + 2) * SLOT * 4
        cursor[0] = ring0 + 2 * SLOTS * SLOT * 4
        gq_hi = place("gq_hi", [P, 2, TL], f32r)
        gq_lo = place("gq_lo", [P, 2, TL], f32r)
        gq = place("gq", [P, 2, TL])
        g_rot = place("g_rot", [P, 2, TL])
        gk_hi = place("gk_hi", [P, T], f32r)
        gk_lo = place("gk_lo", [P, T], f32r)
        gv_hi = place("gv_hi", [P, 4, P], f32r)
        gv_lo = place("gv_lo", [P, 4, P], f32r)
        assert cursor[0] <= ring0 + (2 * SLOTS + 2) * SLOT * 4, cursor[0]

        cursor[0] = work0
        sq = place("sq", [P, KC, T])
        mla0 = cursor[0]
        qa_hi = place("qa_hi", [P, QL // P, T], f32r)
        qa_lo = place("qa_lo", [P, QL // P, T], f32r)
        ca_hi = place("ca_hi", [P, KVL // P, T], f32r)
        ca_lo = place("ca_lo", [P, KVL // P, T], f32r)
        kr = place("kr", [QKD, T])
        kr_rot = place("kr_rot", [QKD, TL])
        mla1 = cursor[0]
        cursor[0] = work0
        pc_hi = place("pc_hi", [P, 2, TL], f32r)
        pc_lo = place("pc_lo", [P, 2, TL], f32r)
        mp = place("mp", [P, 3, T])
        mq = place("mq", [QKD, 2, T])
        mq_rot = place("mq_rot", [QKD, 2, TL])
        assert cursor[0] <= mla0
        cursor[0] = mla0
        x_rows = place("x_rows", [P, 4, D])
        work_end = max(mla1, cursor[0])
        cursor[0] = work0
        hid_hi = place("hid_hi", [P, 6, T], f32r)
        hid_lo = place("hid_lo", [P, 6, T], f32r)
        sil = place("sil", [P, 2, T])
        hid = place("hid", [P, 2, T])
        cb = place("cb", [P, NEXP, TL])
        comb = place("comb", [P, 2, NEXP])
        comb_rep = place("comb_rep", [P, 2, NEXP, P], at=ring1)
        lg = place("lg", [P, 2, NEXP])
        top = place("top", [P, 2, 8])
        top_i = place("top_i", [P, 2, 8], u32)
        top_f = place("top_f", [P, 2, 8])
        gate = place("gate", [P, 2, 4])
        hot = place("hot", [P, 2, NEXP])
        ffn_end = cursor[0]
        cursor[0] = mla0
        k_hi = place("k_hi", [P, 4, T], f32r)
        k_lo = place("k_lo", [P, 4, T], f32r)
        v_hi = place("v_hi", [P, 4, 256], f32r)
        v_lo = place("v_lo", [P, 4, 256], f32r)
        sink_g = place("sink_g", [P, 4])
        att1_end = cursor[0]
        cursor[0] = work0
        o_hi = place("o_hi", [P, KC, TL], f32r)
        o_lo = place("o_lo", [P, KC, TL], f32r)
        kf = place("kf", [P, 2, T], at=ring1)
        kf_rot = place("kf_rot", [P, 2, TL], at=ring1 + 4096)
        out_rows = place("out_rows", [P, 2, D], at=mla0)
        cursor[0] = max(work_end, ffn_end, att1_end)
        nmax = place("nmax", [P, 3, 2])
        psum_e = place("psum_e", [P, 3, 2])
        rsum = place("rsum", [P, 3, 2])
        esink = place("esink", [P, 3, 2])
        mraw = place("mraw", [P, 3, 2])
        assert cursor[0] <= nc.sbuf_usable_end, (cursor[0], nc.sbuf_usable_end)

        B = [stack.enter_context(nc.psum_tensor(f"bank{i}", [P, 512], f32)) for i in range(8)]
        ADA_BANK = B[7]

        s_id = sem("ident_in")
        s_const = sem("constants_in")
        s_eps = sem("eps_set")
        s_mark = sem("pool_waited")
        s_vec = sem("vectors_in")
        s_x = sem("x_rows_in")
        s_ones = sem("ones_set")
        s_vecT = sem("vectors_transposed")
        s_cols = sem("vector_columns")
        s_silu = sem("silu_c_done")
        s_xT = sem("x_transposed")
        s_xc = sem("x_columns_even")
        s_xc1 = sem("x_columns_odd")
        s_rwlo = sem("router_w_lo")
        s_cr = sem("constants_rounded")
        ada_full = [sem(f"ada_full{i}") for i in range(2)]
        ada_first_mm = sem("ada_first_mm")
        ad = {s: sem(f"ada_{s}") for s in ("hi", "lo", "mm", "rows", "turned", "cols")}
        s_mod = sem("mod_ready")
        raw_full = [sem(f"raw_full{i}") for i in range(SLOTS)]
        split_hi = sem("split_hi")
        split_lo = sem("split_lo")
        norm_sem = {s: sem(f"norm_{s}") for s in ("sq", "sum", "rms", "rstd", "tmp", "hi", "lo")}
        norm_base, total = {}, dict.fromkeys(norm_sem, 0)
        for key, chunks, parts, halves in (("n01", KC, 2, 1), ("nq", 3, 1, 1), ("nc", 2, 1, 1), ("n02", KC, 2, 1),
                                           ("n11", KC, 2, 1), ("n12", KC, 1, 1), ("nf", KC, 1, 0)):
            norm_base[key] = dict(total)
            for step, n in (("sq", chunks), ("sum", 1), ("rms", 1), ("rstd", 1), ("tmp", chunks * parts),
                            ("hi", chunks * parts * halves), ("lo", chunks * parts * halves)):
                total[step] += n

        def normed(key, step, n):
            return norm_sem[step], norm_base[key][step] + n

        s_pj = sem("proj0_done")
        s_pje = sem("proj0_evacuated")
        s_krr = sem("k_rope_rotated")
        s_kr = sem("k_rope_steps")
        s_krhi = sem("k_rope_hi")
        s_krlo = sem("k_rope_lo")
        mraw_in = sem("mla_raw_in")
        m = {s: sem(f"mla_{s}") for s in ("w_hi", "w_lo", "proj", "q_f32", "kv_hi", "kv_lo", "rot", "rope",
                                          "q_hi", "q_lo", "scores", "max", "exp", "rsum", "normed",
                                          "turned", "p_hi", "p_lo", "pv", "o_hi", "o_lo")}
        wo = [{s: sem(f"wo{i}_{s}") for s in ("done", "added")} for i in range(2)]
        ff = [{s: sem(f"ff{i}_{s}") for s in ("pe", "silu", "hid", "hid_w", "hid_hi", "hid_lo", "added")}
              for i in range(2)]
        s_kv1 = sem("kv1_done")
        s_kf = sem("k1_f32")
        s_krot1 = sem("k1_rotated")
        s_krope1 = sem("k1_rope_steps")
        s_kdup_hi = sem("k1_hi")
        s_kdup_lo = sem("k1_lo")
        s_kdup2 = sem("k1_copied")
        s_v1hi = sem("v1_hi")
        s_v1lo = sem("v1_lo")
        qw_full, qw_hi, qw_lo = sem("qw_full"), sem("qw_hi"), sem("qw_lo")
        g = {s: sem(f"gqa_{s}") for s in ("proj", "q_f32", "rot", "rope", "q_hi", "q_lo", "kv_copied", "scores",
                                          "max", "nmax", "exp", "esink", "sum", "rsum", "normed", "turned",
                                          "p_hi", "p_lo", "pv", "o_hi", "o_lo")}
        s_lgp = sem("logits_done")
        s_rt = sem("router_top")
        s_rs = sem("router_steps")
        s_gx = sem("gate_exp")
        s_cbp = sem("combine_turned")
        s_cb = sem("combine_ready")
        s_oT = sem("out_turned")
        s_orow = sem("out_rows_ready")
        s_out = sem("out_written")

        from_one = [m[k] for k in ("exp", "p_lo", "o_lo", "proj")] + [qw_lo]
        from_one += [g[k] for k in ("exp", "turned", "pv", "p_lo", "o_lo", "proj")]
        from_one += [ad["lo"], ad["lo"], ad["mm"]]
        from_one += [q[k] for q in ff for k in ("pe", "hid", "hid_lo", "added")]

        K_BANKS = (5, 2)
        LAT, CTX = slice(0, TL), slice(TL, T)
        HALVES = (LAT, CTX)

        def norms_of(layer, which):
            return gain[layer][:, which], (lambda kc, v: mod[layer][:, 24 * which + kc, v:v + 1])

        def used(n):
            if n < BASE_PROJ0:
                return ada_first_mm, n + 1
            if n < BASE_WO0:
                return s_pj, (2, 3, 6)[n - BASE_PROJ0]
            if n < BASE_FFN0:
                return wo[0]["done"], sum(WO_COLS_0[:n - BASE_WO0 + 1]) // P
            if n < BASE_KV1:
                e, s = divmod(n - BASE_FFN0, NITEMS)
                return ff[0]["pe"], ONE + e * PER_EXP + DONE_BY_ITEM[s + 1]
            if n < BASE_WO1:
                return s_kv1, 2 * (n - BASE_KV1 + 1)
            return wo[1]["done"], sum(WO_COLS_1[:n - BASE_WO1 + 1]) // P

        block = stack.enter_context(nc.Block())

        @block.sync
        def _(sp):
            def load(dst, src, s):
                sp.dma_start(dst, src).then_inc(s, 16)

            def row_chunks(a):
                return a.rearrange("(r p) -> r p", p=P)

            load(ident[:, :], k_ident, s_id)
            for name, src in (("norm_g", norm_g.rearrange("a b (r p) -> (a b r) p", p=P)),
                              ("final_g", row_chunks(final_g)), ("q_norm_g", row_chunks(q_norm_g[0])),
                              ("kv_norm_g", row_chunks(kv_norm_g[0])), ("c", row_chunks(c[0])),
                              ("c_ctx", row_chunks(c_ctx)), ("ada_b0", row_chunks(ada_b[0]))):
                r0, n = ROWS_A[name]
                load(rows_a[r0:r0 + n, :], src, s_vec)
            load(rows_b[:, :], row_chunks(ada_b[1]), s_vec)
            load(x_rows[:, 0:2, :], x[0].rearrange("(t p) d -> p t d", p=P), s_x)
            load(x_rows[:, 2:4, :], ctx_x[0].rearrange("(t p) d -> p t d", p=P), s_x)

            def ada_tile(layer, a, n):
                w = ada_w[layer].rearrange("(k p) n -> p k n", p=P)
                for h in range(2):
                    sp.wait_ge(ad["lo"], n * 2 + (h + ONE))
                    sp.dma_start(ada_raw[:, h], w[:, h * (KC // 2):(h + 1) * (KC // 2), bass.ds(a * ADA_W, ADA_W)])\
                      .then_inc(ada_full[h], 16)

            def slot_free(n):
                if n >= SLOTS:
                    sp.wait_ge(split_lo, n - SLOTS + 1)

            def tile_cols(n, w, c0, ncols, nk=KC):
                slot_free(n)
                dst = raw[:, n % SLOTS, 0:nk * ncols].rearrange("p (k n) -> p k n", k=nk)
                src = w.rearrange("(k p) n -> p k n", p=P)
                for a, b in ((0, nk // 2), (nk // 2, nk)):
                    load(dst[:, a:b, :], src[:, a:b, c0:c0 + ncols], raw_full[n % SLOTS])

            for a in range(ADA_FIRST):
                tile_cols(a, ada_w[0], a * ADA_W, ADA_W)
            for dst, src in ((rot_mla[:, :], k_rot_mla), (rot_gqa[:, :], k_rot_gqa),
                             (cs_mla[:, :, :, :], k_cs_mla), (cs_gqa[:, :, :, :], k_cs_gqa),
                             (mask[:, :, :], k_mask), (iota[:, :], k_iota),
                             (sink_b[:, :], sinks.partition_broadcast(P)[:, 0, :]),
                             (rb_b[:, :], router_b.partition_broadcast(P)[:, 0, :]),
                             (rw[:, :, :], router_w[0].rearrange("(k p) e -> p k e", p=P))):
                load(dst, src, s_const)
            for k, tile in enumerate(((w_dq[0], 0, 256), (w_dq[0], 256, 128), (w_dkv[0], 0, KVL + ROPE))):
                tile_cols(BASE_PROJ0 + k, *tile)
            sp.wait_ge(s_pj, 6)
            load(uq_raw[:, :, :], w_uq[0].rearrange("(k p) n -> p k n", p=P), mraw_in)
            load(ukv_raw[:, :, :], w_ukv[0].rearrange("(k p) n -> p k n", p=P), mraw_in)
            with sp.Fori(0, H // 2) as i:
                for j in range(2):
                    ada_tile(0, i * 2 + (ADA_FIRST + j), i * 2 + j)
            sp.wait_ge(m["w_lo"], 2 * (H // 2))
            c0 = 0
            for k, cols in enumerate(WO_COLS_0):
                tile_cols(BASE_WO0 + k, w_o0[0], c0, cols)
                c0 += cols

            def ffn_tiles(w_gu, w_dn, width, gu_col, dn_row, first_lo, base, ada=None):
                for s, (kind, gr, k, f0, m0) in enumerate(ITEMS):
                    slot = s % SLOTS
                    sp.wait_ge(split_lo, first_lo + (s - SLOTS + 1))
                    if kind == "up":
                        dst = raw[:, slot, 0:KC * 256].rearrange("p (k n) -> p k n", k=KC)
                        src = w_gu.rearrange("(k p) n -> p k n", p=P)
                        load(dst[:, :, 0:P], src[:, :, bass.ds(gu_col + f0 * P, P)], raw_full[slot])
                        load(dst[:, :, P:2 * P], src[:, :, bass.ds(gu_col + (width + f0 * P), P)], raw_full[slot])
                    else:
                        nf, cols = GROUPS[gr][1], k * P
                        dst = raw[:, slot, 0:nf * cols].rearrange("p (k n) -> p k n", k=nf)
                        for a, b in ((0, nf // 2), (nf // 2, nf)):
                            src = w_dn[bass.ds(dn_row + (f0 + a) * P, (b - a) * P), m0 * P:m0 * P + cols]
                            load(dst[:, a:b, :], src.rearrange("(k p) n -> p k n", p=P), raw_full[slot])
                    if ada is not None and 2 <= s < 2 + ADA_TILES // 2:
                        ada_tile(1, ada + (s - 2), ada + (ADA_MLA + s - 2))

            with sp.Fori(0, 2) as e:
                ffn_tiles(ffn_gu[0], ffn_dn[0], DFF, e * EFF, e * EFF, e * NITEMS + BASE_FFN0, BASE_FFN0,
                          ada=e * (ADA_TILES // 2))
            tile_cols(BASE_KV1, w_qkv[0], H * HD, 256)
            tile_cols(BASE_KV1 + 1, w_qkv[0], H * HD + 256, 256)
            sp.wait_ge(split_lo, BASE_KV1)
            with sp.Fori(0, 4) as gi:
                sp.wait_ge(qw_lo, ONE + gi)
                sp.dma_start(raw[:, Q_SLOT, 0:KC * 256].rearrange("p (k n) -> p k n", k=KC),
                             w_qkv[0].rearrange("(k p) n -> p k n", p=P)[:, :, bass.ds(gi * 256, 256)])\
                  .then_inc(qw_full, 16)
            sp.wait_ge(qw_lo, ONE + 4)
            for k, cols in enumerate(WO_COLS_1):
                tile_cols(BASE_WO1 + k, w_o1[0], 256 * k, cols)
            with sp.Fori(0, NEXP) as e:
                ffn_tiles(moe_gu[0, e], moe_dn[0, e], EFF, 0, 0, e * NITEMS + BASE_FFN1, BASE_FFN1)
            for t in range(2):
                sp.wait_ge(s_orow, 4 * (t + 1))
                sp.dma_start(out[0, t * P:(t + 1) * P, :], out_rows[:, t, :]).then_inc(s_out, 16)
            sp.wait_ge(s_out, 32)

        @block.gpsimd
        def _(pool):
            for s in from_one:
                pool.sem_inc(s, ONE)
            pool.memset(ones[:, :], 1.0).then_inc(s_ones, 1)
            pool.wait_ge(s_ones, 1)

            with pool.Fori(0, H // 2) as i:
                for u in range(6):
                    pool.wait_ge(m["rsum"], i * 6 + (u + 1))
                    if u % 3 < 2:
                        pool.tensor_tensor(mp[:, u % 3, :], mp[:, u % 3, :], rsum[:, u % 3, 0:1].to_broadcast([P, T]),
                                           ALU.mult).then_inc(m["normed"], 2)
                    else:
                        for t in range(2):
                            cs = slice(t * TL, (t + 1) * TL)
                            pool.tensor_tensor(mp[:, 2, cs], mp[:, 2, cs], rsum[:, 2, t:t + 1].to_broadcast([P, TL]),
                                               ALU.mult).then_inc(m["normed"], 1)

            def hidden(q, e_gu, f, k, nt):
                pool.wait_ge(q["hid"], ONE + e_gu + (k + 1))
                b = k % 2
                pool.tensor_tensor(hid_hi[:, f, 0:nt], hid[:, b, 0:nt], ones[:, 0:1].to_broadcast([P, nt]), ALU.mult)\
                    .then_inc(q["hid_hi"], 1)
                pool.wait_ge(q["hid_hi"], e_gu + (k + 1))
                pool.tensor_tensor(hid_lo[:, f, 0:nt], hid[:, b, 0:nt], hid_hi[:, f, 0:nt].bitcast(f32),
                                   ALU.subtract).then_inc(q["hid_lo"], 1)

            def ffn(q, e, nt):
                for gr, (f0, nf, parts) in enumerate(GROUPS):
                    if gr == 0:
                        pool.wait_ge(q["pe"], ONE + e * PER_EXP)
                    else:
                        pool.wait_ge(q["pe"], ONE + e * PER_EXP + HALF_EXP)
                    for f in range(nf):
                        hidden(q, e * 11, f, f0 + f, nt)

            with pool.Fori(0, 2) as e:
                ffn(ff[0], e, T)

            with pool.Fori(0, 4) as gi:
                pool.wait_ge(s_kdup2, 8)
                pool.wait_ge(s_v1lo, 2)
                pool.wait_ge(g["pv"], ONE + gi * 4)
                pool.tensor_tensor(pool_mark[:, :], ones[:, 0:1], ones[:, 0:1], ALU.mult).then_inc(s_mark, 1)
                pool.tensor_copy(gk_hi[:, :], k_hi[:, gi, :].bitcast(f32)).then_inc(g["kv_copied"], 1)
                pool.tensor_copy(gk_lo[:, :], k_lo[:, gi, :].bitcast(f32)).then_inc(g["kv_copied"], 1)
                for half in range(2):
                    for dst, src in ((gv_hi, v_hi), (gv_lo, v_lo)):
                        pool.tensor_copy(dst[:, :, half * HD:(half + 1) * HD],
                                         src[:, :, bass.ds(gi * HD, HD)].bitcast(f32)).then_inc(g["kv_copied"], 1)
                pool.tensor_copy(sink_g[:, :], sink_b[:, bass.ds(gi * 4, 4)]).then_inc(g["kv_copied"], 1)
                for u in range(8):
                    pool.wait_ge(g["rsum"], gi * 8 + (u + 1))
                    pool.tensor_tensor(gp[:, u % 3, :], gp[:, u % 3, :], rsum[:, u % 3, 0:1].to_broadcast([P, T]),
                                       ALU.mult).then_inc(g["normed"], 1)

            with pool.Fori(0, NEXP) as e:
                ffn(ff[1], e, TL)

        @block.scalar
        def _(act):
            def split(n, size):
                slot = n % SLOTS
                act.wait_ge(raw_full[slot], 32 * (n // SLOTS + 1))
                if n >= SLOTS:
                    act.wait_ge(*used(n - SLOTS))
                act.copy(w_hi[:, slot, 0:size], raw[:, slot, 0:size]).then_inc(split_hi, 1)

            def ada_cols_to(layer, m0):
                act.copy(mod4[layer][:, bass.ds(m0, 2), :], ADA_BANK[:, 256:264].rearrange("p (m v) -> p m v", v=4))\
                    .then_inc(ad["cols"], 1)

            def ada_first_rows(n):
                act.wait_ge(ada_first_mm, n + 1)
                act.copy(ada_rows[:, :], ADA_BANK[0:4, 0:ADA_W]).then_inc(ad["rows"], 1)

            def ada_first_cols(n):
                ada_first_rows(n)
                act.wait_ge(ad["turned"], n + 1)
                ada_cols_to(0, 2 * n)

            def ada_half_hi(n, h):
                act.wait_ge(ada_full[h], n * 16 + 16)
                act.wait_ge(ad["mm"], n * 2 + (h + ONE))
                act.copy(ada_hi[:, :, :], ada_raw[:, h]).then_inc(ad["hi"], 1)

            def ada_tile_rows(n):
                act.wait_ge(ad["mm"], n * 2 + (2 + ONE))
                act.copy(ada_rows[:, :], ADA_BANK[0:4, 0:ADA_W]).then_inc(ad["rows"], 1)

            def ada_tile_cols(n, layer, m0):
                act.wait_ge(ad["turned"], n + (ADA_FIRST + 1))
                ada_cols_to(layer, m0)

            def norm(key, chunks, width, nt, src, ready, bank, shift, dst_hi, parts, between=None):
                for kc in range(chunks):
                    ready(kc)
                    act.activation(sq[:, kc, 0:nt], src(kc), ACT.Square).then_inc(norm_sem["sq"], 1)
                if between:
                    between()
                act.wait_ge(*normed(key, "sum", 1))
                act.wait_ge(s_eps, 1)
                act.activation(rstd[:, 0:nt], bank[:, 0:nt], ACT.Sqrt, scale=1.0 / width,
                               bias=eps_col[:, 0:1]).then_inc(norm_sem["rms"], 1)
                if dst_hi is None:
                    return
                for kc in range(chunks):
                    for v in range(parts):
                        cs = HALVES[v] if parts == 2 else slice(0, nt)
                        act.wait_ge(*normed(key, "tmp", parts * kc + v + 1))
                        if shift is None:
                            act.copy(dst_hi[:, kc, cs], sq[:, kc, cs]).then_inc(norm_sem["hi"], 1)
                        else:
                            act.activation(dst_hi[:, kc, cs], sq[:, kc, cs], ACT.Identity,
                                           bias=shift(kc, v)).then_inc(norm_sem["hi"], 1)

            act.wait_ge(s_vecT, 2)
            act.copy(cols_a[:, :], B[0][:, 0:NROWS_A]).then_inc(s_cols, 1)
            act.copy(cols_b[:, :], B[1][:, 0:NMOD]).then_inc(s_cols, 1)
            act.wait_ge(s_cols, 2)
            for v, name in enumerate(("c", "c_ctx")):
                r0, n = ROWS_A[name]
                act.activation(silu_c[:, :, v], cols_a[:, r0:r0 + n], ACT.Silu).then_inc(s_silu, 1)
            act.wait_ge(s_silu, 2)
            act.copy(c4[:, :, 0:2], silu_c[:, :, :]).then_inc(s_silu, 1)
            split(0, KC * ADA_W)
            split(1, KC * ADA_W)
            for kc in range(1, KC, 2):
                act.wait_ge(s_xT, kc + 1)
                act.copy(x_t[:, kc, :], B[2 + kc % 4][:, :]).then_inc(s_xc1, 1)
            def x_ready(kc):
                act.wait_ge(s_xc1 if kc % 2 else s_xc, kc // 2 + 1)
            def mid_n01():
                for n in range(2, ADA_FIRST):
                    split(n, KC * ADA_W)
                    if n > 2:
                        ada_first_cols(n - 3)
                for n in range(ADA_FIRST - 3, ADA_FIRST):
                    ada_first_cols(n)
                for k, cols in enumerate(PROJ0_COLS):
                    split(BASE_PROJ0 + k, KC * cols)

            norm("n01", KC, D, T, lambda kc: x_t[:, kc, :], x_ready, B[6],
                 norms_of(0, 0)[1], h_hi, 2, mid_n01)
            act.wait_ge(s_const, 16 * 9)
            act.wait_ge(s_id, 16)
            act.copy(ident_r[:, :], ident[:, :]).then_inc(s_cr, 1)
            act.copy(mask_r[:, :, :], mask[:, :, :]).then_inc(s_cr, 1)
            act.copy(rw_hi[:, :, :], rw[:, :, :]).then_inc(s_cr, 1)

            act.wait_ge(*normed("n01", "lo", 2 * KC))
            norm("nq", 3, QL, T, lambda kc: B[kc][:, :], lambda kc: act.wait_ge(s_pj, kc + 1), B[6], None, qa_hi, 1)
            act.wait_ge(s_pj, 6)
            act.copy(kr[NOPE:QKD, :], B[5][0:ROPE, :]).then_inc(s_pje, 1)
            act.wait_ge(*normed("nq", "lo", 3))
            norm("nc", 2, KVL, T, lambda kc: B[3 + kc][:, :], lambda kc: act.wait_ge(s_pj, kc + 4), B[6], None,
                 ca_hi, 1)
            act.wait_ge(s_kr, 3)
            for j in range(2):
                act.copy(mk_hi[NOPE:QKD, j, :], kr[NOPE:QKD, :]).then_inc(s_krhi, 1)

            act.wait_ge(mraw_in, 32)
            act.wait_ge(*normed("nc", "lo", 2))

            def mla_exp(i, u):
                act.wait_ge(m["max"], i * 6 + (u + 1))
                if u >= 3:
                    act.wait_ge(m["turned"], i * 6 + (u - 2))
                if u % 3 < 2:
                    act.activation(mp[:, u % 3, :], B[u % 3][:, :], ACT.Exp, bias=nmax[:, u % 3, 0:1],
                                   accum_out=psum_e[:, u % 3, 0:1]).then_inc(m["exp"], 1)
                else:
                    for t in range(2):
                        cs = slice(t * TL, (t + 1) * TL)
                        last = act.activation(mp[:, 2, cs], B[2][:, cs], ACT.Exp, bias=nmax[:, 2, t:t + 1],
                                              accum_out=psum_e[:, 2, t:t + 1])
                    last.then_inc(m["exp"], 1)

            def mla_p_hi(i, u):
                act.wait_ge(m["turned"], i * 6 + (u + 1))
                turned = B[3 + u % 2]
                if u % 3 < 2:
                    act.copy(pl_hi[:, :, (u % 3) * P:(u % 3 + 1) * P],
                             turned[:, :].rearrange("p (c q) -> p c q", c=4)).then_inc(m["p_hi"], 1)
                else:
                    act.copy(pc_hi[:, :, :], turned[:, :].rearrange("p (c q) -> p c q", c=2)).then_inc(m["p_hi"], 1)

            def mla_o_hi(i, j):
                act.wait_ge(m["pv"], i * 2 + (j + 1))
                rows = slice(HD * j, HD * (j + 1))
                act.copy(h_hi[rows, i, :], B[5 + j][rows, :]).then_inc(m["o_hi"], 1)

            def mla_w_hi(n):
                act.wait_ge(m["proj"], n * 5 + ONE)
                act.copy(uq_hi[:, :, :], uq_raw[:, :, bass.ds(n * (2 * QKD), 2 * QKD)]).then_inc(m["w_hi"], 1)
                act.copy(ukv_hi[:, :, :], ukv_raw[:, :, bass.ds(n * 256, 256)]).then_inc(m["w_hi"], 1)

            def mla_q_copy(n, j):
                act.wait_ge(m["proj"], n * 5 + (j + 1 + ONE))
                act.mul(mq[:, j, :], B[j][0:QKD, :], float(QKD) ** -0.5).then_inc(m["q_f32"], 1)

            def mla_k_hi(n, j):
                act.wait_ge(m["proj"], n * 5 + (j + 3 + ONE))
                act.copy(mk_hi[0:NOPE, j, :], B[K_BANKS[j]][0:NOPE, :]).then_inc(m["kv_hi"], 1)

            def mla_q_hi(n):
                act.wait_ge(m["rope"], n * 3 + 3)
                act.copy(mq_hi[:, :, :], mq[:, :, :]).then_inc(m["q_hi"], 1)

            def mla_v_hi(n):
                act.wait_ge(m["proj"], n * 5 + (5 + ONE))
                act.copy(mv_hi[:, :, :], B[3][:, :].rearrange("p (t n) -> p t n", t=4)).then_inc(m["kv_hi"], 1)

            def mla_body(i, n):
                a, b = i * 2, i * 2 + 1
                ma, mb = i * 4 + 2 * ADA_FIRST, i * 4 + (2 * ADA_FIRST + 2)
                more = n is not None
                ada_half_hi(a, 0)
                mla_exp(i, 0)
                mla_exp(i, 1)
                mla_exp(i, 2)
                mla_p_hi(i, 0)
                ada_half_hi(a, 1)
                mla_exp(i, 3)
                if more:
                    mla_w_hi(n)
                mla_p_hi(i, 1)
                mla_p_hi(i, 2)
                mla_exp(i, 4)
                ada_tile_rows(a)
                ada_half_hi(b, 0)
                mla_o_hi(i, 0)
                mla_p_hi(i, 3)
                ada_tile_cols(a, 0, ma)
                mla_exp(i, 5)
                if more:
                    mla_q_copy(n, 0)
                    mla_q_copy(n, 1)
                ada_half_hi(b, 1)
                mla_p_hi(i, 4)
                if more:
                    mla_k_hi(n, 0)
                mla_p_hi(i, 5)
                if more:
                    mla_k_hi(n, 1)
                ada_tile_rows(b)
                if more:
                    mla_q_hi(n)
                mla_o_hi(i, 1)
                if more:
                    mla_v_hi(n)
                ada_tile_cols(b, 0, mb)

            mla_w_hi(0)
            mla_q_copy(0, 0)
            mla_q_copy(0, 1)
            mla_k_hi(0, 0)
            mla_k_hi(0, 1)
            mla_q_hi(0)
            mla_v_hi(0)
            with act.Fori(0, H // 2 - 1) as i:
                mla_body(i, i + 1)
            mla_body(H // 2 - 1, None)

            act.wait_ge(m["pv"], H)
            for k in range(len(WO_COLS_0)):
                split(BASE_WO0 + k, KC * WO_COLS_0[k])

            def x_after_wo(layer):
                return lambda kc: act.wait_ge(wo[layer]["added"], KC if layer else kc + 1)

            def ffn_split(q, e, s, base):
                slot = s % SLOTS
                act.wait_ge(raw_full[slot], e * (32 * NITEMS // SLOTS) + 32 * (base // SLOTS + s // SLOTS + 1))
                act.wait_ge(q["pe"], ONE + e * PER_EXP + DONE_BY_ITEM[s - 2])
                act.copy(w_hi[:, slot, 0:item_size(ITEMS[s % NITEMS])],
                         raw[:, slot, 0:item_size(ITEMS[s % NITEMS])]).then_inc(split_hi, 1)

            def ffn_body(q, e, base, nt, last, tail, with_ada):
                for s, item in enumerate(ITEMS):
                    if s + 2 < NITEMS or not last:
                        ffn_split(q, e, s + 2, base)
                    elif tail:
                        split(*tail[s + 2 - NITEMS])
                    if with_ada and 1 <= s <= ADA_TILES // 2:
                        ada_tile_cols(e * (ADA_TILES // 2) + (ADA_MLA + s - 1), 1, e * ADA_TILES + 2 * (s - 1))
                    if with_ada and s < ADA_TILES // 2:
                        n = e * (ADA_TILES // 2) + (ADA_MLA + s)
                        ada_half_hi(n, 0)
                        ada_half_hi(n, 1)
                    if item[0] == "up":
                        k = item[3]
                        act.wait_ge(q["pe"], ONE + e * PER_EXP + DONE_BY_ITEM[s + 1])
                        if k >= 2:
                            act.wait_ge(q["hid"], ONE + e * 11 + (k - 1))
                        else:
                            act.wait_ge(q["hid"], ONE + e * 11)
                        act.activation(sil[:, k % 2, 0:nt], B[2 * (k % 2)][:, 0:nt], ACT.Silu).then_inc(q["silu"], 1)
                    if with_ada and s < ADA_TILES // 2:
                        ada_tile_rows(n)

            def ffn(q, n_exp, base, nt, tail, with_ada):
                with act.Fori(0, n_exp - 1) as e:
                    ffn_body(q, e, base, nt, False, None, with_ada)
                ffn_body(q, n_exp - 1, base, nt, True, tail, with_ada)

            for s in range(2):
                split(BASE_FFN0 + s, item_size(ITEMS[s]))
            norm("n02", KC, D, T, lambda kc: x_t[:, kc, :], x_after_wo(0), B[6], norms_of(0, 1)[1], h_hi, 2)
            act.wait_ge(*normed("n02", "lo", 2 * KC))
            ffn(ff[0], 2, BASE_FFN0, T, [(BASE_KV1, 2048), (BASE_KV1 + 1, 2048)], True)

            def x_after_ffn(layer, n_exp):
                return lambda kc: act.wait_ge(ff[layer]["added"], ONE + 16 * n_exp)

            norm("n11", KC, D, T, lambda kc: x_t[:, kc, :], x_after_ffn(0, 2), B[6], norms_of(1, 0)[1], h_hi, 2)
            for c2 in range(2):
                act.wait_ge(s_kv1, c2 + 1)
                act.copy(kf[:, c2, :], B[c2][:, :]).then_inc(s_kf, 1)
            for b in range(2):
                act.wait_ge(s_kv1, b + 3)
                act.copy(v_hi[:, 2 * b:2 * b + 2, :], B[2 + b][:, :].rearrange("p (t n) -> p t n", t=2))\
                   .then_inc(s_v1hi, 1)
            act.wait_ge(s_krope1, 3)
            for gg in range(4):
                rows = slice(HD * (gg % 2), HD * (gg % 2 + 1))
                act.copy(k_hi[rows, gg, :], kf[rows, gg // 2, :]).then_inc(s_kdup_hi, 1)
            for gg in range(4):
                rows = slice(HD * (gg % 2), HD * (gg % 2 + 1))
                other = slice(HD * (1 - gg % 2), HD * (2 - gg % 2))
                act.wait_ge(s_kdup_hi, gg + 1)
                act.copy(k_hi[other, gg, :], k_hi[rows, gg, :].bitcast(f32)).then_inc(s_kdup2, 1)
                act.wait_ge(s_kdup_lo, gg + 1)
                act.copy(k_lo[other, gg, :], k_lo[rows, gg, :].bitcast(f32)).then_inc(s_kdup2, 1)

            def g_exp(gi, u):
                act.wait_ge(g["nmax"], gi * 8 + (u + 1))
                if u >= 3:
                    act.wait_ge(g["turned"], ONE + gi * 8 + (u - 2))
                else:
                    act.wait_ge(g["turned"], ONE + gi * 8)
                act.activation(gp[:, u % 3, :], B[u % 3][:, :], ACT.Exp, bias=nmax[:, u % 3, 0:1],
                               accum_out=psum_e[:, u % 3, 0:1]).then_inc(g["exp"], 1)
                act.activation(esink[:, u % 3, 0:1], sink_g[:, u // 2:u // 2 + 1], ACT.Exp,
                               bias=nmax[:, u % 3, 0:1]).then_inc(g["esink"], 1)

            def g_p_hi(gi, u):
                act.wait_ge(g["turned"], ONE + gi * 8 + (u + 1))
                act.wait_ge(g["pv"], ONE + gi * 4 + u // 2)
                act.copy(gt_hi[:, :, (u % 2) * P:(u % 2 + 1) * P],
                         B[3 + u % 2][:, :].rearrange("p (c q) -> p c q", c=4)).then_inc(g["p_hi"], 1)

            def g_o_hi(gi, j):
                act.wait_ge(g["pv"], ONE + gi * 4 + (j + 1))
                rows = slice(HD * (j % 2), HD * (j % 2 + 1))
                act.copy(o_hi[rows, gi * 2 + j // 2, :], B[5 + j % 2][rows, 0:TL]).then_inc(g["o_hi"], 1)

            act.wait_ge(*normed("n11", "lo", 2 * KC))
            with act.Fori(0, 4) as gi:
                act.wait_ge(qw_full, gi * 16 + 16)
                act.wait_ge(g["proj"], ONE + gi * 2)
                act.copy(w_hi[:, Q_SLOT, 0:2048], raw[:, Q_SLOT, 0:2048]).then_inc(qw_hi, 1)
                for j in range(2):
                    act.wait_ge(g["proj"], ONE + gi * 2 + (j + 1))
                    act.mul(gq[:, j, :], B[j][:, 0:TL], float(HD) ** -0.5).then_inc(g["q_f32"], 1)
                act.wait_ge(g["rope"], gi * 3 + 3)
                act.copy(gq_hi[:, :, :], gq[:, :, :]).then_inc(g["q_hi"], 1)
                act.wait_ge(g["kv_copied"], gi * 7 + 7)
                g_exp(gi, 0)
                g_exp(gi, 1)
                for u in range(8):
                    if u + 2 < 8:
                        g_exp(gi, u + 2)
                    g_p_hi(gi, u)
                    if u % 2 == 0 and u >= 2:
                        g_o_hi(gi, u // 2 - 1)
                g_o_hi(gi, 3)

            act.wait_ge(g["pv"], ONE + H)
            for k in range(len(WO_COLS_1)):
                split(BASE_WO1 + k, KC * WO_COLS_1[k])
            for s in range(2):
                split(BASE_FFN1 + s, item_size(ITEMS[s]))
            norm("n12", KC, D, TL, lambda kc: x_t[:, kc, LAT], x_after_wo(1), B[6], norms_of(1, 1)[1], h_hi, 1)
            act.wait_ge(s_rt, 3)
            act.activation(gate[:, :, 1:2], gate[:, :, 0:1], ACT.Exp).then_inc(s_gx, 1)
            for b in range(4):
                act.wait_ge(s_cbp, b + 1)
                act.copy(cb[:, 2 * b:2 * b + 2, :], B[b][:, :].rearrange("p (e t) -> p e t", e=2)).then_inc(s_cb, 1)
            act.wait_ge(*normed("n12", "lo", KC))
            ffn(ff[1], NEXP, BASE_FFN1, TL, None, False)
            norm("nf", KC, D, TL, lambda kc: x_t[:, kc, LAT], x_after_ffn(1, NEXP), B[6], None, None, 1)

        @block.vector
        def _(dve):
            def lo_of(slot, size, n_hi):
                dve.wait_ge(split_hi, n_hi)
                dve.tensor_tensor(w_lo[:, slot, 0:size], raw[:, slot, 0:size], w_hi[:, slot, 0:size].bitcast(f32),
                                  ALU.subtract).then_inc(split_lo, 1)

            def norm(key, chunks, nt, src, gains, shift, dst_hi, dst_lo, parts):
                dve.wait_ge(*normed(key, "rms", 1))
                dve.reciprocal(rstd[:, 0:nt], rstd[:, 0:nt]).then_inc(norm_sem["rstd"], 1)
                dve.wait_ge(*normed(key, "rstd", 1))

                def low(kc):
                    for v in range(parts):
                        cs = HALVES[v] if parts == 2 else slice(0, nt)
                        dve.wait_ge(*normed(key, "hi", parts * kc + v + 1))
                        if shift is None:
                            dve.tensor_tensor(dst_lo[:, kc, cs], sq[:, kc, cs], dst_hi[:, kc, cs].bitcast(f32),
                                              ALU.subtract).then_inc(norm_sem["lo"], 1)
                        else:
                            dve.scalar_tensor_tensor(out=dst_lo[:, kc, cs], in0=sq[:, kc, cs], scalar=shift(kc, v),
                                                     in1=dst_hi[:, kc, cs].bitcast(f32), op0=ALU.add,
                                                     op1=ALU.subtract).then_inc(norm_sem["lo"], 1)

                for kc in range(chunks):
                    for v in range(parts):
                        cs = HALVES[v] if parts == 2 else slice(0, nt)
                        dve.scalar_tensor_tensor(out=sq[:, kc, cs], in0=src(kc, cs), scalar=gains(kc, v),
                                                 in1=rstd[:, cs], op0=ALU.mult, op1=ALU.mult).then_inc(norm_sem["tmp"], 1)
                    if kc and dst_hi is not None:
                        low(kc - 1)
                if dst_hi is not None:
                    low(chunks - 1)

            def mod_cols(layer, a, b, bias, done):
                for v in range(2):
                    dve.tensor_tensor(mod[layer][:, a:b, v], mod4[layer][:, a:b, 2 + v], bias[:, a:b], ALU.add)\
                       .then_inc(s_mod, 1)
                dve.wait_ge(s_mod, done + 2)
                for v in range(2):
                    dve.tensor_tensor(mod[layer][:, a:b, v], mod[layer][:, a:b, v], mod4[layer][:, a:b, v], ALU.add)\
                       .then_inc(s_mod, 1)
                dve.wait_ge(s_mod, done + 4)

            def ada_half_lo(n, h):
                dve.wait_ge(ad["hi"], n * 2 + (h + 1))
                dve.tensor_tensor(ada_lo[:, :, :], ada_raw[:, h], ada_hi[:, :, :].bitcast(f32), ALU.subtract)\
                   .then_inc(ad["lo"], 1)

            def gains(layer, which):
                r0 = ROWS_A["norm_g"][0] + (2 * layer + which) * KC
                for v in range(2):
                    dve.scalar_tensor_tensor(out=gain[layer][:, which, :, v],
                                             in0=mod[layer][:, 24 * which + 8:24 * which + 16, v], scalar=1.0,
                                             in1=cols_a[:, r0:r0 + KC], op0=ALU.add, op1=ALU.mult).then_inc(s_mod, 1)

            dve.memset(eps_col[:, :], EPS).then_inc(s_eps, 1)
            dve.wait_ge(s_silu, 3)
            dve.tensor_tensor(c4[:, :, 2:4], silu_c[:, :, :], c4[:, :, 0:2].bitcast(f32), ALU.subtract)\
               .then_inc(s_silu, 1)
            for n in range(2):
                lo_of(n, KC * ADA_W, n + 1)
            for kc in range(0, KC, 2):
                dve.wait_ge(s_xT, kc + 1)
                dve.tensor_copy(x_t[:, kc, :], B[2 + kc % 4][:, :]).then_inc(s_xc, 1)
            for n in range(2, ADA_FIRST):
                lo_of(n % SLOTS, KC * ADA_W, n + 1)
            for k, cols in enumerate(PROJ0_COLS):
                lo_of((BASE_PROJ0 + k) % SLOTS, KC * cols, BASE_PROJ0 + k + 1)
            a0 = ROWS_A["ada_b0"][0]
            bias0 = cols_a[:, a0:a0 + NMOD]
            dve.wait_ge(ad["cols"], ADA_FIRST)
            dve.wait_ge(s_cols, 2)
            mod_cols(0, 0, 16, bias0, 0)
            gains(0, 0)
            dve.wait_ge(s_mod, 6)
            ga = [[gain[l][:, w] for w in range(2)] for l in range(2)]
            norm("n01", KC, T, lambda kc, cs: x_t[:, kc, cs], lambda kc, v: ga[0][0][:, kc, v:v + 1],
                 norms_of(0, 0)[1], h_hi, h_lo, 2)
            dve.wait_ge(s_cr, 3)
            dve.tensor_tensor(rw_lo[:, :, :], rw[:, :, :], rw_hi[:, :, :].bitcast(f32), ALU.subtract)\
               .then_inc(s_rwlo, 1)
            qg, kvg = ROWS_A["q_norm_g"][0], ROWS_A["kv_norm_g"][0]
            norm("nq", 3, T, lambda kc, cs: B[kc][:, cs], lambda kc, v: cols_a[:, qg + kc:qg + kc + 1],
                 None, qa_hi, qa_lo, 1)
            norm("nc", 2, T, lambda kc, cs: B[3 + kc][:, cs], lambda kc, v: cols_a[:, kvg + kc:kvg + kc + 1],
                 None, ca_hi, ca_lo, 1)
            rr = slice(NOPE, QKD)
            dve.wait_ge(s_krr, 1)
            dve.tensor_tensor(kr_rot[rr, :], B[5][rr, 0:TL], cs_mla[rr, 1, 0, :], ALU.mult).then_inc(s_kr, 1)
            dve.tensor_tensor(kr[rr, LAT], kr[rr, LAT], cs_mla[rr, 0, 0, :], ALU.mult).then_inc(s_kr, 1)
            dve.wait_ge(s_kr, 2)
            dve.tensor_tensor(kr[rr, LAT], kr[rr, LAT], kr_rot[rr, :], ALU.add).then_inc(s_kr, 1)
            dve.wait_ge(s_krhi, 2)
            for j in range(2):
                dve.tensor_tensor(mk_lo[rr, j, :], kr[rr, :], mk_hi[rr, j, :].bitcast(f32), ALU.subtract)\
                   .then_inc(s_krlo, 1)

            def mla_max(i, u):
                dve.wait_ge(m["scores"], i * 6 + (u + 1))
                if u % 3 < 2:
                    dve.tensor_reduce(nmax[:, u % 3, 0:1], B[u % 3][:, :], AX.X, ALU.max, negate=True)\
                       .then_inc(m["max"], 1)
                else:
                    dve.tensor_reduce(nmax[:, 2, :], B[2][:, :].rearrange("p (t k) -> p t k", t=2), AX.X, ALU.max,
                                      negate=True).then_inc(m["max"], 1)

            def mla_rsum(i, u):
                dve.wait_ge(m["exp"], ONE + i * 6 + (u + 1))
                w = 1 if u % 3 < 2 else 2
                dve.reciprocal(rsum[:, u % 3, 0:w], psum_e[:, u % 3, 0:w]).then_inc(m["rsum"], 1)

            def mla_p_lo(i, u):
                dve.wait_ge(m["p_hi"], i * 6 + (u + 1))
                turned = B[3 + u % 2]
                if u % 3 < 2:
                    cs = slice((u % 3) * P, (u % 3 + 1) * P)
                    dve.tensor_tensor(pl_lo[:, :, cs], turned[:, :].rearrange("p (c q) -> p c q", c=4),
                                      pl_hi[:, :, cs].bitcast(f32), ALU.subtract).then_inc(m["p_lo"], 1)
                else:
                    dve.tensor_tensor(pc_lo[:, :, :], turned[:, :].rearrange("p (c q) -> p c q", c=2),
                                      pc_hi[:, :, :].bitcast(f32), ALU.subtract).then_inc(m["p_lo"], 1)

            def mla_o_lo(i, j):
                dve.wait_ge(m["o_hi"], i * 2 + (j + 1))
                rows = slice(HD * j, HD * (j + 1))
                dve.tensor_tensor(h_lo[rows, i, :], B[5 + j][rows, :], h_hi[rows, i, :].bitcast(f32), ALU.subtract)\
                   .then_inc(m["o_lo"], 1)

            def mla_w_lo(n):
                dve.wait_ge(m["w_hi"], n * 2 + 1)
                dve.tensor_tensor(uq_lo[:, :, :], uq_raw[:, :, bass.ds(n * (2 * QKD), 2 * QKD)],
                                  uq_hi[:, :, :].bitcast(f32), ALU.subtract).then_inc(m["w_lo"], 1)
                dve.wait_ge(m["w_hi"], n * 2 + 2)
                dve.tensor_tensor(ukv_lo[:, :, :], ukv_raw[:, :, bass.ds(n * 256, 256)],
                                  ukv_hi[:, :, :].bitcast(f32), ALU.subtract).then_inc(m["w_lo"], 1)

            def mla_k_lo(n, j):
                dve.wait_ge(m["kv_hi"], n * 3 + (j + 1))
                dve.tensor_tensor(mk_lo[0:NOPE, j, :], B[K_BANKS[j]][0:NOPE, :], mk_hi[0:NOPE, j, :].bitcast(f32),
                                  ALU.subtract).then_inc(m["kv_lo"], 1)

            def mla_v_lo(n):
                dve.wait_ge(m["kv_hi"], n * 3 + 3)
                dve.tensor_tensor(mv_lo[:, :, :], B[3][:, :].rearrange("p (t n) -> p t n", t=4),
                                  mv_hi[:, :, :].bitcast(f32), ALU.subtract).then_inc(m["kv_lo"], 1)

            def mla_rope(n):
                dve.wait_ge(m["rot"], n + 1)
                dve.tensor_tensor(mq_rot[rr, :, :], B[0][rr, :].rearrange("p (j t) -> p j t", j=2),
                                  cs_mla[rr, 1, :, :], ALU.mult).then_inc(m["rope"], 1)
                dve.tensor_tensor(mq[rr, :, LAT], mq[rr, :, LAT], cs_mla[rr, 0, :, :], ALU.mult)\
                   .then_inc(m["rope"], 1)
                dve.wait_ge(m["rope"], n * 3 + 2)
                dve.tensor_tensor(mq[rr, :, LAT], mq[rr, :, LAT], mq_rot[rr, :, :], ALU.add).then_inc(m["rope"], 1)

            def mla_q_lo(n):
                dve.wait_ge(m["q_hi"], n + 1)
                dve.tensor_tensor(mq_lo[:, :, :], mq[:, :, :], mq_hi[:, :, :].bitcast(f32), ALU.subtract)\
                   .then_inc(m["q_lo"], 1)

            def mla_body(i, n):
                more = n is not None
                ada_half_lo(i * 2, 0)
                mla_max(i, 0)
                mla_max(i, 1)
                mla_rsum(i, 0)
                mla_max(i, 2)
                mla_rsum(i, 1)
                mla_p_lo(i, 0)
                mla_rsum(i, 2)
                ada_half_lo(i * 2, 1)
                mla_max(i, 3)
                mla_p_lo(i, 1)
                mla_rsum(i, 3)
                if more:
                    mla_w_lo(n)
                mla_p_lo(i, 2)
                mla_max(i, 4)
                mla_rsum(i, 4)
                ada_half_lo(i * 2 + 1, 0)
                mla_o_lo(i, 0)
                mla_p_lo(i, 3)
                mla_max(i, 5)
                mla_rsum(i, 5)
                ada_half_lo(i * 2 + 1, 1)
                mla_p_lo(i, 4)
                if more:
                    mla_k_lo(n, 0)
                mla_p_lo(i, 5)
                if more:
                    mla_k_lo(n, 1)
                    mla_rope(n)
                    mla_q_lo(n)
                mla_o_lo(i, 1)
                if more:
                    mla_v_lo(n)

            mla_w_lo(0)
            mla_k_lo(0, 0)
            mla_k_lo(0, 1)
            mla_rope(0)
            mla_q_lo(0)
            mla_v_lo(0)
            with dve.Fori(0, H // 2 - 1) as i:
                mla_body(i, i + 1)
            mla_body(H // 2 - 1, None)

            dve.wait_ge(ad["cols"], ADA_TILES)
            mod_cols(0, 16, NMOD, bias0, 6)
            gains(0, 1)
            dve.wait_ge(s_mod, 12)

            def add_out(layer, mc, bank, parts, which, done):
                for v in range(parts):
                    last = dve.scalar_tensor_tensor(out=x_t[:, mc, HALVES[v]], in0=bank[:, HALVES[v]],
                                                    scalar=mod[layer][:, 8 * which + mc, v:v + 1],
                                                    in1=x_t[:, mc, HALVES[v]], op0=ALU.mult, op1=ALU.add)
                last.then_inc(done, 1)

            def wo_phase(layer, base, cols, parts):
                mc = 0
                sizes = [KC * w for w in cols]
                for k in range(min(2, len(cols))):
                    lo_of((base + k) % SLOTS, sizes[k], base + k + 1)
                for k, w in enumerate(cols):
                    if k + 2 < len(cols):
                        lo_of((base + k + 2) % SLOTS, sizes[k + 2], base + k + 3)
                    for j in range(w // P):
                        dve.wait_ge(wo[layer]["done"], mc + 1)
                        add_out(layer, mc, B[mc % 2], parts, 2, wo[layer]["added"])
                        mc += 1

            def ffn_body(q, layer, e, base, nt, parts, last, tail):
                for s, item in enumerate(ITEMS):
                    if layer == 0 and s < ADA_TILES // 2:
                        ada_half_lo(e * (ADA_TILES // 2) + (ADA_MLA + s), 0)
                    if s + 2 < NITEMS or not last:
                        s2 = s + 2
                        lo_of(s2 % SLOTS, item_size(ITEMS[s2 % NITEMS]), e * NITEMS + (base + s2 + 1))
                    elif tail:
                        n, size = tail[s + 2 - NITEMS]
                        lo_of(n % SLOTS, size, n + 1)
                    if layer == 0 and s < ADA_TILES // 2:
                        ada_half_lo(e * (ADA_TILES // 2) + (ADA_MLA + s), 1)
                    if item[0] == "up":
                        k = item[3]
                        dve.wait_ge(q["silu"], e * 11 + (k + 1))
                        if k >= 2:
                            dve.wait_ge(q["hid_lo"], ONE + e * 11 + (k - 1))
                        else:
                            dve.wait_ge(q["hid_lo"], ONE + e * 11)
                        hb = hid[:, k % 2, 0:nt]
                        formed = dve.tensor_tensor(hb, B[2 * (k % 2) + 1][:, 0:nt], sil[:, k % 2, 0:nt], ALU.mult)
                        if layer == 1:
                            formed.then_inc(q["hid_w"], 1)
                            dve.wait_ge(q["hid_w"], e * 11 + (k + 1))
                            formed = dve.tensor_tensor(hb, hb, cb[:, e, :], ALU.mult)
                        formed.then_inc(q["hid"], 1)
                    else:
                        _, gr, n_out, _, m0 = item
                        for j in range(n_out):
                            dve.wait_ge(q["pe"], ONE + e * PER_EXP + (DONE_BY_ITEM[s] + j + 1))
                            dve.wait_ge(q["added"], ONE + e * 16 + (m0 + j + 1 if gr else 0))
                            add_out(layer, m0 + j, B[4 + (m0 + j) % 3], parts, 5, q["added"])

            def ffn(q, layer, n_exp, base, nt, parts, tail):
                with dve.Fori(0, n_exp - 1) as e:
                    ffn_body(q, layer, e, base, nt, parts, False, None)
                ffn_body(q, layer, n_exp - 1, base, nt, parts, True, tail)

            wo_phase(0, BASE_WO0, WO_COLS_0, 2)
            for s in range(2):
                lo_of((BASE_FFN0 + s) % SLOTS, item_size(ITEMS[s]), BASE_FFN0 + s + 1)
            dve.wait_ge(wo[0]["added"], KC)
            norm("n02", KC, T, lambda kc, cs: x_t[:, kc, cs], lambda kc, v: ga[0][1][:, kc, v:v + 1],
                 norms_of(0, 1)[1], h_hi, h_lo, 2)
            ffn(ff[0], 0, 2, BASE_FFN0, T, 2, [(BASE_KV1, 2048), (BASE_KV1 + 1, 2048)])

            dve.wait_ge(ad["cols"], 2 * ADA_TILES)
            mod_cols(1, 0, NMOD, cols_b, 12)
            gains(1, 0)
            gains(1, 1)
            dve.wait_ge(s_mod, 20)
            dve.wait_ge(ff[0]["added"], ONE + 32)
            norm("n11", KC, T, lambda kc, cs: x_t[:, kc, cs], lambda kc, v: ga[1][0][:, kc, v:v + 1],
                 norms_of(1, 0)[1], h_hi, h_lo, 2)
            dve.wait_ge(s_krot1, 1)
            dve.tensor_tensor(kf_rot[:, :, :], B[4][:, :].rearrange("p (c t) -> p c t", c=2), cs_gqa[:, 1],
                              ALU.mult).then_inc(s_krope1, 1)
            dve.tensor_tensor(kf[:, :, LAT], kf[:, :, LAT], cs_gqa[:, 0], ALU.mult).then_inc(s_krope1, 1)
            dve.wait_ge(s_krope1, 2)
            dve.tensor_tensor(kf[:, :, LAT], kf[:, :, LAT], kf_rot[:, :, :], ALU.add).then_inc(s_krope1, 1)
            for b in range(2):
                dve.wait_ge(s_v1hi, b + 1)
                dve.tensor_tensor(v_lo[:, 2 * b:2 * b + 2, :], B[2 + b][:, :].rearrange("p (t n) -> p t n", t=2),
                                  v_hi[:, 2 * b:2 * b + 2, :].bitcast(f32), ALU.subtract).then_inc(s_v1lo, 1)
            for gg in range(4):
                rows = slice(HD * (gg % 2), HD * (gg % 2 + 1))
                dve.wait_ge(s_kdup_hi, gg + 1)
                dve.tensor_tensor(k_lo[rows, gg, :], kf[rows, gg // 2, :], k_hi[rows, gg, :].bitcast(f32),
                                  ALU.subtract).then_inc(s_kdup_lo, 1)

            def g_max(gi, u):
                dve.wait_ge(g["scores"], gi * 8 + (u + 1))
                dve.tensor_reduce(mraw[:, u % 3, 0:1], B[u % 3][:, :], AX.X, ALU.max).then_inc(g["max"], 1)
                dve.wait_ge(g["max"], gi * 8 + (u + 1))
                dve.tensor_scalar(nmax[:, u % 3, 0:1], mraw[:, u % 3, 0:1], sink_g[:, u // 2:u // 2 + 1], -1.0,
                                  ALU.max, ALU.mult).then_inc(g["nmax"], 1)

            def g_rsum(gi, u):
                dve.wait_ge(g["esink"], gi * 8 + (u + 1))
                dve.tensor_tensor(mraw[:, u % 3, 1:2], psum_e[:, u % 3, 0:1], esink[:, u % 3, 0:1], ALU.add)\
                   .then_inc(g["sum"], 1)
                dve.wait_ge(g["sum"], gi * 8 + (u + 1))
                dve.reciprocal(rsum[:, u % 3, 0:1], mraw[:, u % 3, 1:2]).then_inc(g["rsum"], 1)

            def g_p_lo(gi, u):
                dve.wait_ge(g["p_hi"], gi * 8 + (u + 1))
                cs = slice((u % 2) * P, (u % 2 + 1) * P)
                dve.tensor_tensor(gt_lo[:, :, cs], B[3 + u % 2][:, :].rearrange("p (c q) -> p c q", c=4),
                                  gt_hi[:, :, cs].bitcast(f32), ALU.subtract).then_inc(g["p_lo"], 1)

            def g_o_lo(gi, j):
                dve.wait_ge(g["o_hi"], gi * 4 + (j + 1))
                rows = slice(HD * (j % 2), HD * (j % 2 + 1))
                dve.tensor_tensor(o_lo[rows, gi * 2 + j // 2, :], B[5 + j % 2][rows, 0:TL],
                                  o_hi[rows, gi * 2 + j // 2, :].bitcast(f32), ALU.subtract).then_inc(g["o_lo"], 1)

            with dve.Fori(0, 4) as gi:
                dve.wait_ge(qw_hi, gi + 1)
                dve.tensor_tensor(w_lo[:, Q_SLOT, 0:2048], raw[:, Q_SLOT, 0:2048],
                                  w_hi[:, Q_SLOT, 0:2048].bitcast(f32), ALU.subtract).then_inc(qw_lo, 1)
                dve.wait_ge(g["rot"], gi + 1)
                dve.tensor_tensor(g_rot[:, :, :], B[2][:, :].rearrange("p (j t) -> p j t", j=2), cs_gqa[:, 1],
                                  ALU.mult).then_inc(g["rope"], 1)
                dve.tensor_tensor(gq[:, :, :], gq[:, :, :], cs_gqa[:, 0], ALU.mult).then_inc(g["rope"], 1)
                dve.wait_ge(g["rope"], gi * 3 + 2)
                dve.tensor_tensor(gq[:, :, :], gq[:, :, :], g_rot[:, :, :], ALU.add).then_inc(g["rope"], 1)
                dve.wait_ge(g["q_hi"], gi + 1)
                dve.tensor_tensor(gq_lo[:, :, :], gq[:, :, :], gq_hi[:, :, :].bitcast(f32), ALU.subtract)\
                   .then_inc(g["q_lo"], 1)
                dve.wait_ge(g["kv_copied"], gi * 7 + 7)
                g_max(gi, 0)
                g_max(gi, 1)
                g_rsum(gi, 0)
                for u in range(8):
                    if u + 2 < 8:
                        g_max(gi, u + 2)
                    if u + 1 < 8:
                        g_rsum(gi, u + 1)
                    g_p_lo(gi, u)
                    if u % 2 == 0 and u >= 2:
                        g_o_lo(gi, u // 2 - 1)
                g_o_lo(gi, 3)

            wo_phase(1, BASE_WO1, WO_COLS_1, 1)
            for s in range(2):
                lo_of((BASE_FFN1 + s) % SLOTS, item_size(ITEMS[s]), BASE_FFN1 + s + 1)
            dve.wait_ge(wo[1]["added"], KC)
            norm("n12", KC, TL, lambda kc, cs: x_t[:, kc, cs], lambda kc, v: ga[1][1][:, kc, 0:1],
                 norms_of(1, 1)[1], h_hi, h_lo, 1)
            dve.wait_ge(s_lgp, 1)
            for t in range(2):
                dve.tensor_tensor(lg[:, t, :], B[0][:, t * NEXP:(t + 1) * NEXP], rb_b[:, :], ALU.add)\
                   .then_inc(s_rs, 1)
            dve.wait_ge(s_rs, 2)
            for t in range(2):
                dve.max(top[:, t, :], lg[:, t, :]).then_inc(s_rs, 1)
            dve.wait_ge(s_rs, 4)
            for t in range(2):
                dve.max_index(top_i[:, t, :], top[:, t, :], lg[:, t, :]).then_inc(s_rt, 1)
            dve.tensor_tensor(gate[:, :, 0:1], top[:, :, 1:2], top[:, :, 0:1], ALU.subtract).then_inc(s_rt, 1)
            dve.wait_ge(s_rt, 3)
            dve.tensor_copy(top_f[:, :, :], top_i[:, :, :]).then_inc(s_rs, 1)
            dve.wait_ge(s_gx, 1)
            dve.tensor_scalar(gate[:, :, 2:3], gate[:, :, 1:2], 1.0, None, ALU.add).then_inc(s_rs, 1)
            dve.wait_ge(s_rs, 6)
            dve.reciprocal(gate[:, :, 3:4], gate[:, :, 2:3]).then_inc(s_rs, 1)
            dve.wait_ge(s_rs, 7)
            dve.tensor_tensor(gate[:, :, 2:3], gate[:, :, 1:2], gate[:, :, 3:4], ALU.mult).then_inc(s_rs, 1)
            dve.wait_ge(s_rs, 8)
            for t in range(2):
                dve.tensor_scalar(comb[:, t, :], iota[:, :], top_f[:, t, 0:1], gate[:, t, 3:4], ALU.is_equal,
                                  ALU.mult).then_inc(s_rs, 1)
                dve.tensor_scalar(hot[:, t, :], iota[:, :], top_f[:, t, 1:2], gate[:, t, 2:3], ALU.is_equal,
                                  ALU.mult).then_inc(s_rs, 1)
            dve.wait_ge(s_rs, 12)
            dve.tensor_tensor(comb[:, :, :], comb[:, :, :], hot[:, :, :], ALU.add).then_inc(s_rs, 1)
            dve.wait_ge(s_rs, 13)
            for t in range(2):
                for e in range(NEXP):
                    dve.tensor_scalar(comb_rep[:, t, e, :], ones[:, :], comb[:, t, e:e + 1], None, ALU.mult)\
                       .then_inc(s_rs, 1)
            dve.wait_ge(s_cb, 4)
            ffn(ff[1], 1, NEXP, BASE_FFN1, TL, 1, None)
            dve.wait_ge(ff[1]["added"], ONE + 16 * NEXP)
            fg = ROWS_A["final_g"][0]
            norm("nf", KC, TL, lambda kc, cs: x_t[:, kc, cs], lambda kc, v: cols_a[:, fg + kc:fg + kc + 1],
                 None, None, None, 1)
            for t in range(2):
                for b in range(2):
                    dve.wait_ge(s_oT, 2 * t + b + 1)
                    dve.tensor_copy(out_rows[:, t, b * 512:(b + 1) * 512], B[2 * t + b][:, :]).then_inc(s_orow, 2)

        @block.tensor
        def _(pe):
            def mm(out_, lhs, rhs, start, stop):
                return pe.matmul(out_, lhs, rhs, start=start, stop=stop, skip_group_check=True)

            def three(out_, wh, wl, xh, xl, first, last):
                mm(out_, wh, xh, first, False)
                mm(out_, wh, xl, False, False)
                return mm(out_, wl, xh, False, last)

            def slot_view(t, slot, nk, cols):
                return t[:, slot, 0:nk * cols].rearrange("p (k n) -> p k n", k=nk)

            def ada_mms(wh, wl, k0, k1):
                for kc in range(k0, k1):
                    mm(ADA_BANK[0:4, 0:ADA_W], c4[:, kc, :], wh[:, kc - k0, :], kc == 0, False)
                    last = mm(ADA_BANK[0:4, 0:ADA_W], c4[:, kc, :], wl[:, kc - k0, :], False, kc == KC - 1)
                return last

            def ada_half(n, h):
                pe.wait_ge(ad["lo"], n * 2 + (h + 2 + ONE))
                if h == 0:
                    pe.wait_ge(ad["cols"], n + ADA_FIRST)
                ada_mms(ada_hi, ada_lo, h * (KC // 2), (h + 1) * (KC // 2)).then_inc(ad["mm"], 1)

            def ada_turn(n):
                pe.wait_ge(ad["rows"], n + 1)
                for j in range(2):
                    last = mm(ADA_BANK[:, 256 + 4 * j:260 + 4 * j], ada_rows[:, j * P:(j + 1) * P],
                              ident[0:4, 0:4], True, True)
                last.then_inc(ad["turned"], 1)

            def norm_sum(key, chunks, nt, bank):
                for kc in range(chunks):
                    pe.wait_ge(*normed(key, "sq", kc + 1))
                    last = mm(bank[:, 0:nt], ones[:, :], sq[:, kc, 0:nt], kc == 0, kc == chunks - 1)
                last.then_inc(norm_sem["sum"], 1)

            def chunk_wait(key, kc, parts):
                pe.wait_ge(*normed(key, "hi", parts * (kc + 1)))
                pe.wait_ge(*normed(key, "lo", parts * (kc + 1)))

            pe.wait_ge(s_id, 16)
            pe.wait_ge(s_vec, 128)
            pe.transpose(B[0][:, 0:NROWS_A], rows_a[0:NROWS_A, :], ident[0:NROWS_A, 0:NROWS_A]).then_inc(s_vecT, 1)
            pe.transpose(B[1][:, 0:NMOD], rows_b[:, :], ident[0:NMOD, 0:NMOD]).then_inc(s_vecT, 1)
            pe.wait_ge(s_x, 32)
            for kc in range(KC):
                if kc >= 4:
                    pe.wait_ge(s_xc1 if kc % 2 else s_xc, kc // 2 - 1)
                for t in range(4):
                    last = pe.transpose(B[2 + kc % 4][:, t * P:(t + 1) * P], x_rows[:, t, kc * P:(kc + 1) * P],
                                        ident[:, :])
                last.then_inc(s_xT, 1)
            pe.wait_ge(s_ones, 1)
            norm_sum("n01", KC, T, B[6])
            pe.wait_ge(s_silu, 4)
            for a in range(ADA_FIRST):
                pe.wait_ge(split_hi, a + 1)
                pe.wait_ge(split_lo, a + 1)
                if a:
                    pe.wait_ge(ad["cols"], a)
                ada_mms(slot_view(w_hi, a % SLOTS, KC, ADA_W), slot_view(w_lo, a % SLOTS, KC, ADA_W), 0, KC)\
                    .then_inc(ada_first_mm, 1)
                ada_turn(a)

            pe.wait_ge(s_cols, 2)
            pe.wait_ge(s_xc, 4)
            pe.wait_ge(s_xc1, 4)
            bank = 0
            for k, cols in enumerate(PROJ0_COLS):
                n = BASE_PROJ0 + k
                pe.wait_ge(split_hi, n + 1)
                pe.wait_ge(split_lo, n + 1)
                wh, wl = slot_view(w_hi, n % SLOTS, KC, cols), slot_view(w_lo, n % SLOTS, KC, cols)
                for c0 in range(0, cols, P):
                    c1 = min(c0 + P, cols)
                    for kc in range(KC):
                        if bank == 0:
                            chunk_wait("n01", kc, 2)
                        last = three(B[bank][0:c1 - c0, :], wh[:, kc, c0:c1], wl[:, kc, c0:c1], h_hi[:, kc, :],
                                     h_lo[:, kc, :], kc == 0, kc == KC - 1)
                    last.then_inc(s_pj, 1)
                    bank += 1
            rr = slice(NOPE, QKD)
            norm_sum("nq", 3, T, B[6])
            pe.wait_ge(s_pje, 1)
            pe.wait_ge(s_const, 16 * 9)
            mm(B[5][0:QKD, 0:TL], rot_mla[rr, :], kr[rr, LAT], True, True).then_inc(s_krr, 1)
            pe.wait_ge(*normed("nq", "rms", 1))
            norm_sum("nc", 2, T, B[6])

            chunk_wait("nq", 2, 1)
            chunk_wait("nc", 1, 1)
            pe.wait_ge(s_krhi, 2)
            pe.wait_ge(s_krlo, 2)

            def mla_scores(i, u):
                j, t = divmod(u, 3)
                if u >= 3:
                    pe.wait_ge(m["exp"], ONE + i * 6 + (u - 2))
                if t < 2:
                    qs = slice(t * P, (t + 1) * P)
                    last = three(B[t][:, :], mq_hi[:, j, qs], mq_lo[:, j, qs], mk_hi[:, j, :], mk_lo[:, j, :],
                                 True, True)
                else:
                    for t2 in range(2):
                        qs = slice(TL + t2 * P, TL + (t2 + 1) * P)
                        last = three(B[2][:, t2 * TL:(t2 + 1) * TL], mq_hi[:, j, qs], mq_lo[:, j, qs],
                                     mk_hi[:, j, CTX], mk_lo[:, j, CTX], True, True)
                last.then_inc(m["scores"], 1)

            def mla_turn(i, u):
                pe.wait_ge(m["normed"], i * 12 + (2 * u + 2))
                if u >= 2:
                    pe.wait_ge(m["p_lo"], ONE + i * 6 + (u - 1))
                for b in range(4):
                    src = b * P if u % 3 < 2 else (b % 2) * TL + (b // 2) * P
                    last = pe.transpose(B[3 + u % 2][:, b * P:(b + 1) * P], mp[:, u % 3, src:src + P], ident[:, :])
                last.then_inc(m["turned"], 1)

            def mla_pv(i, j):
                pe.wait_ge(m["p_hi"], i * 6 + (3 * j + 3))
                pe.wait_ge(m["p_lo"], ONE + i * 6 + (3 * j + 3))
                for b in range(4):
                    three(B[5 + j][:, LAT], mv_hi[:, b, :], mv_lo[:, b, :], pl_hi[:, b, :], pl_lo[:, b, :],
                          b == 0, b == 3)
                for b in range(2):
                    last = three(B[5 + j][:, CTX], mv_hi[:, 2 + b, :], mv_lo[:, 2 + b, :], pc_hi[:, b, :],
                                 pc_lo[:, b, :], b == 0, b == 1)
                last.then_inc(m["pv"], 1)

            def mla_q_proj(n, j, i):
                if i is not None:
                    pe.wait_ge(m["exp"], i * 6 + (4 + j + ONE))
                for kc in range(QL // P):
                    cs = slice(j * QKD, (j + 1) * QKD)
                    last = three(B[j][0:QKD, :], uq_hi[:, kc, cs], uq_lo[:, kc, cs], qa_hi[:, kc, :],
                                 qa_lo[:, kc, :], kc == 0, kc == QL // P - 1)
                last.then_inc(m["proj"], 1)

            def mla_k_proj(n, j, i):
                if i is not None and j == 0:
                    pe.wait_ge(m["o_lo"], i * 2 + (1 + ONE))
                if i is not None and j == 1:
                    pe.wait_ge(m["exp"], i * 6 + (6 + ONE))
                for kc in range(KVL // P):
                    cs = slice(j * 128, j * 128 + NOPE)
                    last = three(B[K_BANKS[j]][0:NOPE, :], ukv_hi[:, kc, cs], ukv_lo[:, kc, cs], ca_hi[:, kc, :],
                                 ca_lo[:, kc, :], kc == 0, kc == KVL // P - 1)
                last.then_inc(m["proj"], 1)

            def mla_v_proj(n, i):
                if i is not None:
                    pe.wait_ge(m["p_lo"], i * 6 + (5 + ONE))
                for t in range(4):
                    ts = slice(t * P, (t + 1) * P)
                    for kc in range(KVL // P):
                        vh = ukv_hi[:, kc, :].rearrange("p (j n) -> p j n", j=2)[:, :, NOPE:]
                        vl = ukv_lo[:, kc, :].rearrange("p (j n) -> p j n", j=2)[:, :, NOPE:]
                        last = three(B[3][:, ts].rearrange("p (j n) -> p j n", j=2), ca_hi[:, kc, ts],
                                     ca_lo[:, kc, ts], vh, vl, kc == 0, kc == KVL // P - 1)
                last.then_inc(m["proj"], 1)

            def mla_rot(n):
                pe.wait_ge(m["q_f32"], n * 2 + 2)
                mm(B[0][0:QKD, :].rearrange("p (j t) -> p j t", j=2), rot_mla[rr, :], mq[rr, :, LAT], True, True)\
                    .then_inc(m["rot"], 1)

            def mla_body(i, n):
                more = n is not None
                pe.wait_ge(m["q_hi"], i + 1)
                pe.wait_ge(m["q_lo"], i + 1)
                pe.wait_ge(m["kv_lo"], i * 3 + 2)
                mla_scores(i, 0)
                mla_scores(i, 1)
                mla_scores(i, 2)
                ada_half(i * 2, 0)
                pe.wait_ge(m["kv_lo"], i * 3 + 3)
                mla_turn(i, 0)
                mla_scores(i, 3)
                mla_turn(i, 1)
                mla_turn(i, 2)
                mla_scores(i, 4)
                ada_half(i * 2, 1)
                mla_pv(i, 0)
                ada_turn(i * 2 + ADA_FIRST)
                mla_turn(i, 3)
                mla_scores(i, 5)
                if more:
                    pe.wait_ge(m["w_hi"], n * 2 + 2)
                    pe.wait_ge(m["w_lo"], n * 2 + 2)
                    mla_q_proj(n, 0, i)
                    mla_q_proj(n, 1, i)
                ada_half(i * 2 + 1, 0)
                mla_turn(i, 4)
                if more:
                    mla_k_proj(n, 0, i)
                mla_turn(i, 5)
                if more:
                    mla_k_proj(n, 1, i)
                ada_half(i * 2 + 1, 1)
                if more:
                    mla_rot(n)
                mla_pv(i, 1)
                if more:
                    mla_v_proj(n, i)
                ada_turn(i * 2 + (ADA_FIRST + 1))

            pe.wait_ge(m["w_hi"], 2)
            pe.wait_ge(m["w_lo"], 2)
            for j in range(2):
                mla_q_proj(0, j, None)
            for j in range(2):
                mla_k_proj(0, j, None)
            mla_rot(0)
            mla_v_proj(0, None)
            with pe.Fori(0, H // 2 - 1) as i:
                mla_body(i, i + 1)
            mla_body(H // 2 - 1, None)

            def out_proj(layer, base, cols, yh, yl, nt):
                mc = 0
                for k, w in enumerate(cols):
                    n = base + k
                    pe.wait_ge(split_hi, n + 1)
                    pe.wait_ge(split_lo, n + 1)
                    wh, wl = slot_view(w_hi, n % SLOTS, KC, w), slot_view(w_lo, n % SLOTS, KC, w)
                    for j in range(w // P):
                        if mc >= 2:
                            pe.wait_ge(wo[layer]["added"], mc - 1)
                        for kc in range(KC):
                            last = three(B[mc % 2][:, 0:nt], wh[:, kc, j * P:(j + 1) * P],
                                         wl[:, kc, j * P:(j + 1) * P], yh[:, kc, 0:nt], yl[:, kc, 0:nt],
                                         kc == 0, kc == KC - 1)
                        last.then_inc(wo[layer]["done"], 1)
                        mc += 1

            def ffn(q, e, base, nt, with_ada):
                for s, (kind, gr, k, f0, m0) in enumerate(ITEMS):
                    slot = s % SLOTS
                    if with_ada and 1 <= s <= ADA_TILES // 2:
                        ada_turn(e * (ADA_TILES // 2) + (ADA_TILES + s - 1))
                    with_half = with_ada and s < ADA_TILES // 2
                    n_ada = e * (ADA_TILES // 2) + (ADA_MLA + s)
                    pe.wait_ge(split_hi, e * NITEMS + (base + s + 1))
                    pe.wait_ge(split_lo, e * NITEMS + (base + s + 1))
                    if kind == "up":
                        pe.wait_ge(q["hid"], ONE + e * 11 + max(f0 - 1, 0))
                        wh, wl = slot_view(w_hi, slot, KC, 256), slot_view(w_lo, slot, KC, 256)
                        for half in range(2):
                            cs = slice(half * P, (half + 1) * P)
                            if half and with_half:
                                ada_half(n_ada, 0)
                            for kc in range(KC):
                                last = three(B[2 * (f0 % 2) + half][:, 0:nt], wh[:, kc, cs], wl[:, kc, cs],
                                             h_hi[:, kc, 0:nt], h_lo[:, kc, 0:nt], kc == 0, kc == KC - 1)
                        last.then_inc(q["pe"], 1)
                    else:
                        nf = GROUPS[gr][1]
                        wh, wl = slot_view(w_hi, slot, nf, k * P), slot_view(w_lo, slot, nf, k * P)
                        for j in range(k):
                            pe.wait_ge(q["added"], ONE + e * 16 + (8 * gr + max(m0 + j - 2, 0)))
                            if j == 0:
                                pe.wait_ge(q["hid_lo"], ONE + e * 11 + (f0 + nf - 1))
                            for kc in range(nf - 1):
                                three(B[4 + (m0 + j) % 3][:, 0:nt], wh[:, kc, j * P:(j + 1) * P],
                                      wl[:, kc, j * P:(j + 1) * P], hid_hi[:, kc, 0:nt], hid_lo[:, kc, 0:nt],
                                      kc == 0, False)
                        if with_half:
                            ada_half(n_ada, 0)
                        pe.wait_ge(q["hid_lo"], ONE + e * 11 + (f0 + nf))
                        for j in range(k):
                            three(B[4 + (m0 + j) % 3][:, 0:nt], wh[:, nf - 1, j * P:(j + 1) * P],
                                  wl[:, nf - 1, j * P:(j + 1) * P], hid_hi[:, nf - 1, 0:nt],
                                  hid_lo[:, nf - 1, 0:nt], False, True).then_inc(q["pe"], 1)
                    if with_half:
                        ada_half(n_ada, 1)

            pe.wait_ge(m["o_hi"], H)
            pe.wait_ge(m["o_lo"], ONE + H)
            out_proj(0, BASE_WO0, WO_COLS_0, h_hi, h_lo, T)
            norm_sum("n02", KC, T, B[6])
            chunk_wait("n02", KC - 1, 2)
            with pe.Fori(0, 2) as e:
                ffn(ff[0], e, BASE_FFN0, T, True)

            norm_sum("n11", KC, T, B[6])
            chunk_wait("n11", KC - 1, 2)
            pe.wait_ge(split_hi, BASE_KV1 + 1)
            pe.wait_ge(split_lo, BASE_KV1 + 1)
            kh, kl = slot_view(w_hi, 0, KC, 256), slot_view(w_lo, 0, KC, 256)
            for c2 in range(2):
                cs = slice(c2 * P, (c2 + 1) * P)
                for kc in range(KC):
                    last = three(B[c2][:, :], kh[:, kc, cs], kl[:, kc, cs], h_hi[:, kc, :], h_lo[:, kc, :],
                                 kc == 0, kc == KC - 1)
                last.then_inc(s_kv1, 1)
            pe.wait_ge(split_hi, BASE_KV1 + 2)
            pe.wait_ge(split_lo, BASE_KV1 + 2)
            vh, vl = slot_view(w_hi, 1, KC, 256), slot_view(w_lo, 1, KC, 256)
            for t in range(4):
                ts = slice(t * P, (t + 1) * P)
                for kc in range(KC):
                    last = three(B[2 + t // 2][:, (t % 2) * 256:(t % 2 + 1) * 256], h_hi[:, kc, ts],
                                 h_lo[:, kc, ts], vh[:, kc, :], vl[:, kc, :], kc == 0, kc == KC - 1)
                if t % 2:
                    last.then_inc(s_kv1, 1)
            pe.wait_ge(s_kf, 2)
            mm(B[4][:, :].rearrange("p (c t) -> p c t", c=2), rot_gqa[:, :], kf[:, :, LAT], True, True)\
                .then_inc(s_krot1, 1)
            pe.wait_ge(s_v1lo, 2)
            pe.wait_ge(s_krope1, 3)
            pe.wait_ge(s_cr, 3)

            def g_scores(gi, u):
                j, t = divmod(u, 2)
                if u >= 3:
                    pe.wait_ge(g["exp"], ONE + gi * 8 + (u - 2))
                rows, qs = slice(HD * (j % 2), HD * (j % 2 + 1)), slice(t * P, (t + 1) * P)
                three(B[u % 3][:, :], gq_hi[rows, j // 2, qs], gq_lo[rows, j // 2, qs], gk_hi[rows, :],
                      gk_lo[rows, :], True, False)
                mm(B[u % 3][:, (1 - t) * P:(2 - t) * P], ident_r[:, :], mask_r[:, t, :], False, True)\
                    .then_inc(g["scores"], 1)

            def g_turn(gi, u):
                pe.wait_ge(g["normed"], gi * 8 + (u + 1))
                pe.wait_ge(g["p_lo"], ONE + gi * 8 + max(u - 1, 0))
                for b in range(4):
                    last = pe.transpose(B[3 + u % 2][:, b * P:(b + 1) * P], gp[:, u % 3, b * P:(b + 1) * P],
                                        ident[:, :])
                last.then_inc(g["turned"], 1)

            def g_pv(gi, j):
                pe.wait_ge(g["p_hi"], gi * 8 + (2 * j + 2))
                pe.wait_ge(g["p_lo"], ONE + gi * 8 + (2 * j + 2))
                pe.wait_ge(g["o_lo"], ONE + gi * 4 + max(j - 1, 0))
                for b in range(4):
                    last = three(B[5 + j % 2][:, 0:TL], gv_hi[:, b, :], gv_lo[:, b, :], gt_hi[:, b, :],
                                 gt_lo[:, b, :], b == 0, b == 3)
                last.then_inc(g["pv"], 1)

            with pe.Fori(0, 4) as gi:
                pe.wait_ge(qw_hi, gi + 1)
                pe.wait_ge(qw_lo, ONE + gi + 1)
                pe.wait_ge(g["exp"], ONE + gi * 8)
                for j in range(2):
                    qh, ql = slot_view(w_hi, Q_SLOT, KC, 256), slot_view(w_lo, Q_SLOT, KC, 256)
                    for kc in range(KC):
                        cs = slice(j * P, (j + 1) * P)
                        last = three(B[j][:, 0:TL], qh[:, kc, cs], ql[:, kc, cs], h_hi[:, kc, LAT],
                                     h_lo[:, kc, LAT], kc == 0, kc == KC - 1)
                    last.then_inc(g["proj"], 1)
                pe.wait_ge(g["q_f32"], gi * 2 + 2)
                mm(B[2][:, :].rearrange("p (j t) -> p j t", j=2), rot_gqa[:, :], gq[:, :, :], True, True)\
                    .then_inc(g["rot"], 1)
                pe.wait_ge(g["q_hi"], gi + 1)
                pe.wait_ge(g["q_lo"], gi + 1)
                pe.wait_ge(g["kv_copied"], gi * 7 + 7)
                for u in range(3):
                    g_scores(gi, u)
                for u in range(8):
                    g_turn(gi, u)
                    if u + 3 < 8:
                        g_scores(gi, u + 3)
                    if u % 2 == 0 and u >= 2:
                        g_pv(gi, u // 2 - 1)
                g_pv(gi, 3)

            pe.wait_ge(g["o_hi"], H)
            pe.wait_ge(g["o_lo"], ONE + H)
            out_proj(1, BASE_WO1, WO_COLS_1, o_hi, o_lo, TL)
            norm_sum("n12", KC, TL, B[6])
            chunk_wait("n12", KC - 1, 1)
            pe.wait_ge(s_rwlo, 1)
            for t in range(2):
                ts = slice(t * P, (t + 1) * P)
                for kc in range(KC):
                    last = three(B[0][:, t * NEXP:(t + 1) * NEXP], h_hi[:, kc, ts], h_lo[:, kc, ts],
                                 rw_hi[:, kc, :], rw_lo[:, kc, :], kc == 0, kc == KC - 1)
            last.then_inc(s_lgp, 1)
            pe.wait_ge(s_rs, 13 + 2 * NEXP)
            for e in range(NEXP):
                for t in range(2):
                    last = mm(B[e // 2][:, (e % 2) * TL + t * P:(e % 2) * TL + (t + 1) * P], comb_rep[:, t, e, :],
                              ident[:, :], True, True)
                if e % 2:
                    last.then_inc(s_cbp, 1)
            pe.wait_ge(s_cb, 4)
            with pe.Fori(0, NEXP) as e:
                ffn(ff[1], e, BASE_FFN1, TL, False)

            norm_sum("nf", KC, TL, B[6])
            pe.wait_ge(*normed("nf", "tmp", KC))
            for t in range(2):
                for b in range(2):
                    for k in range(4):
                        last = pe.transpose(B[2 * t + b][:, k * P:(k + 1) * P],
                                            sq[:, 4 * b + k, t * P:(t + 1) * P], ident[:, :])
                    last.then_inc(s_oT, 1)


_NAMES = ("x", "c", "ctx", "c_ctx", "ada_w", "ada_b", "norm_g", "final_norm_g", "mla_w_dq", "mla_q_norm_g",
          "mla_w_uq", "mla_w_dkv", "mla_kv_norm_g", "mla_w_ukv", "mla_w_o", "swa_w_qkv", "swa_sinks", "swa_w_o",
          "ffn_w_gate_up", "ffn_w_down", "moe_router_w", "moe_router_b", "moe_w_gate_up", "moe_w_down")


def constants():
    def angles(rot_dim):
        n = rot_dim // 4
        inv = np.float32(10000.0) ** (-np.arange(n, dtype=np.float32) / np.float32(n))
        rows = np.repeat(np.arange(TL // GRID_W, dtype=np.float32), GRID_W)
        cols = np.tile(np.arange(GRID_W, dtype=np.float32), TL // GRID_W)
        return np.concatenate([rows[:, None] * inv, cols[:, None] * inv], axis=-1).astype(np.float32)

    def table(rot_dim, first, copies):
        a = angles(rot_dim).T
        out = np.zeros((P, 2, 2, TL), np.float32)
        for k in range(copies):
            for half in range(2):
                r = first + k * rot_dim + half * (rot_dim // 2)
                out[r:r + rot_dim // 2, 0] = np.cos(a)[:, None, :]
                out[r:r + rot_dim // 2, 1] = np.sin(a)[:, None, :]
        return out

    def rotation(width, rot_dim, first, copies):
        r = np.zeros((P, width), np.float32)
        half = rot_dim // 2
        for k in range(copies):
            for i in range(half):
                a = first + k * rot_dim + i
                r[a + half, a] = -1.0
                r[a, a + half] = 1.0
        return r

    q, k = np.arange(P)[:, None], np.arange(P)[None, :]
    mask = np.stack([np.where(k <= q, 0.0, NEG), np.where(k >= q, 0.0, NEG)], axis=1).astype(np.float32)
    return {
        "k_ident": np.eye(P, dtype=np.float32),
        "k_rot_mla": rotation(QKD, ROPE, NOPE, 1),
        "k_rot_gqa": rotation(P, HD, 0, 2),
        "k_cs_mla": table(ROPE, NOPE, 1),
        "k_cs_gqa": table(HD, 0, 2),
        "k_mask": mask,
        "k_iota": np.ascontiguousarray(np.broadcast_to(np.arange(NEXP, dtype=np.float32), (P, NEXP))),
    }


def kernel(**inputs):
    import concourse.bacc as bacc
    from concourse.bass_utils import run_bass_kernel_spmd

    nc = bacc.Bacc("TRN2", target_bir_lowering=False, num_devices=1)
    arrays = {f"in_{n}": np.ascontiguousarray(inputs[n]) for n in _NAMES}
    arrays.update(constants())
    args = [nc.dram_tensor(n, a.shape, mybir.dt.from_np(a.dtype), kind="ExternalInput").ap()
            for n, a in arrays.items()]
    args.append(nc.dram_tensor("out", (1, TL, D), mybir.dt.float32, kind="ExternalOutput").ap())
    build(nc, *args)
    r = run_bass_kernel_spmd(nc, [arrays], core_ids=[0])
    return r.results[0]["out"]
```

```python
import numpy as np

import concourse.bass as bass
from concourse import mybir
from contextlib import ExitStack

D = 1024
T = 512
TL = 256
GRID_W = 64
H = 16
HD = 64
QL, KVL, NOPE, ROPE = 384, 256, 64, 32
QKD = NOPE + ROPE
DFF = 2816
NEXP, EFF = 8, 1408
EPS = 1e-6
NEG = -1e30
P = 128
KC = D // P
NMOD = 6 * KC

SLOTS = 3
ONE = 1
SLOT = 2304
ADA_W = 256
ADA_FIRST = 8
ADA_TILES = 6 * D // ADA_W
GROUPS = ((0, 6, (3, 3, 2)), (6, 5, (2, 2, 2, 2)))
WO_COLS_0 = (256, 256, 256, 256)
WO_COLS_1 = (256, 256, 256, 256)


def ffn_items():
    items = []
    for g, (f0, nf, parts) in enumerate(GROUPS):
        items += [("up", g, f, f0 + f, 0) for f in range(nf)]
        m = 0
        for parted in parts:
            items.append(("down", g, parted, f0, m))
            m += parted
    return items


ITEMS = ffn_items()
NITEMS = len(ITEMS)
assert NITEMS % SLOTS == 0


def item_size(item):
    return KC * 256 if item[0] == "up" else GROUPS[item[1]][1] * item[2] * P


DONE_BY_ITEM = [0]
for _kind, _g, _k, _f, _m in ITEMS:
    DONE_BY_ITEM.append(DONE_BY_ITEM[-1] + (1 if _kind == "up" else _k))
PER_EXP = DONE_BY_ITEM[-1]
HALF_EXP = DONE_BY_ITEM[NITEMS // 2]

PROJ0_COLS = (256, 128, 288)
BASE_PROJ0 = ADA_FIRST
BASE_WO0 = BASE_PROJ0 + len(PROJ0_COLS)
BASE_FFN0 = BASE_WO0 + len(WO_COLS_0)
BASE_KV1 = BASE_FFN0 + 2 * NITEMS
BASE_WO1 = BASE_KV1 + 2
BASE_FFN1 = BASE_WO1 + len(WO_COLS_1)
ADA_MLA = ADA_TILES - ADA_FIRST
assert ADA_MLA == H and BASE_FFN0 % SLOTS == 0 and BASE_KV1 % SLOTS == 0 and BASE_FFN1 % SLOTS == 0
Q_SLOT = 2

ROWS_A = {"norm_g": (0, 32), "final_g": (32, 8), "q_norm_g": (40, 3), "kv_norm_g": (43, 2),
          "c": (45, 8), "c_ctx": (53, 8), "ada_b0": (61, NMOD)}
NROWS_A = 61 + NMOD


def build(nc, x, c, ctx_x, c_ctx, ada_w, ada_b, norm_g, final_g, w_dq, q_norm_g, w_uq, w_dkv, kv_norm_g,
          w_ukv, w_o0, w_qkv, sinks, w_o1, ffn_gu, ffn_dn, router_w, router_b, moe_gu, moe_dn,
          k_ident, k_rot_mla, k_rot_gqa, k_cs_mla, k_cs_gqa, k_mask, k_iota, k_tri, out):
    f32, f32r, u32, i32 = mybir.dt.float32, mybir.dt.float32r, mybir.dt.uint32, mybir.dt.int32
    ALU, ACT, AX = mybir.AluOpType, mybir.ActivationFunctionType, mybir.AxisListType
    stack = ExitStack()
    with stack:
        words = {f32: 4, f32r: 4, u32: 4, i32: 4}
        cursor = [16640]

        def place(name, shape, dt=f32, at=None):
            size = int(np.prod(shape[1:])) * words[dt]
            off = cursor[0] if at is None else at
            if at is None:
                cursor[0] = (off + size + 31) // 32 * 32
            return nc.alloc_sbuf_tensor_at(name, shape, dt, offset=off)

        def sem(name):
            return stack.enter_context(nc.semaphore(name))

        x_t_at = cursor[0]
        x_t = place("x_t", [P, KC, T])
        h_hi = place("h_hi", [P, KC, T], f32r)
        h_lo = place("h_lo", [P, KC, T], f32r)
        ident = place("ident", [P, P])
        ident_r = place("ident_r", [P, P], f32r)
        ones = place("ones", [P, P])
        tables0 = cursor[0]
        rot_mla = place("rot_mla", [P, QKD])
        rot_gqa = place("rot_gqa", [P, P])
        cs_mla = place("cs_mla", [P, 2, 2, TL])
        cs_gqa = place("cs_gqa", [P, 2, 2, TL])
        mask = place("mask", [P, 2, P])
        mask_r = place("mask_r", [P, 2, P], f32r)
        tables1 = cursor[0]
        iota = place("iota", [P, P])
        tri = place("tri", [P, P])
        sink_b = place("sink_b", [P, H])
        rb_b = place("rb_b", [P, NEXP])
        rw = place("rw", [P, KC, NEXP])
        rw_hi = place("rw_hi", [P, KC, NEXP], f32r)
        rw_lo = place("rw_lo", [P, KC, NEXP], f32r)
        rows_a = place("rows_a", [P, P])
        rows_b = place("rows_b", [NMOD, P])
        cols_a = place("cols_a", [P, NROWS_A])
        cols_b = place("cols_b", [P, NMOD])
        silu_c = place("silu_c", [P, KC, 2])
        c4 = place("c4", [P, KC, 4], f32r)
        mod4 = [place(f"mod4_{i}", [P, NMOD, 4]) for i in range(2)]
        mod = [place(f"mod{i}", [P, NMOD, 2]) for i in range(2)]
        gain = [place(f"gain{i}", [P, 2, KC, 2]) for i in range(2)]
        rstd = place("rstd", [P, T])
        eps_col = place("eps_col", [P, 1])
        pool_mark = place("pool_mark", [P, 2])
        ring0 = cursor[0]
        raw = place("raw", [P, SLOTS, SLOT])
        w_hi = place("w_hi", [P, SLOTS, SLOT], f32r)
        w_lo = place("w_lo", [P, SLOTS, SLOT], f32r)
        ring1 = cursor[0]
        ada_raw = place("ada_raw", [P, 2, KC // 2, ADA_W])
        ada_hi = place("ada_hi", [P, KC // 2, ADA_W], f32r)
        ada_lo = place("ada_lo", [P, KC // 2, ADA_W], f32r)
        ada_rows = place("ada_rows", [4, ADA_W])
        work0 = cursor[0]

        cursor[0] = ring0
        uq_raw = place("uq_raw", [P, QL // P, H * QKD])
        ukv_raw = place("ukv_raw", [P, KVL // P, H * 128])
        uq_hi = place("uq_hi", [P, QL // P, 2 * QKD], f32r)
        uq_lo = place("uq_lo", [P, QL // P, 2 * QKD], f32r)
        ukv_hi = place("ukv_hi", [P, KVL // P, 256], f32r)
        ukv_lo = place("ukv_lo", [P, KVL // P, 256], f32r)
        mk_hi = place("mk_hi", [QKD, 2, T], f32r)
        mk_lo = place("mk_lo", [QKD, 2, T], f32r)
        mq_hi = place("mq_hi", [QKD, 2, T], f32r)
        mq_lo = place("mq_lo", [QKD, 2, T], f32r)
        mv_hi = place("mv_hi", [P, 4, P], f32r)
        mv_lo = place("mv_lo", [P, 4, P], f32r)
        pl_hi = place("pl_hi", [P, 4, TL], f32r)
        pl_lo = place("pl_lo", [P, 4, TL], f32r)
        assert cursor[0] <= ring1, (cursor[0], ring1)
        cursor[0] = ring0 + SLOTS * SLOT * 4
        gp = place("gp", [P, 3, T])
        gt_hi = place("gt_hi", [P, 4, TL], f32r)
        gt_lo = place("gt_lo", [P, 4, TL], f32r)
        assert cursor[0] <= ring0 + (SLOTS + 2) * SLOT * 4
        cursor[0] = ring0 + 2 * SLOTS * SLOT * 4
        gq_hi = place("gq_hi", [P, 2, TL], f32r)
        gq_lo = place("gq_lo", [P, 2, TL], f32r)
        gq = place("gq", [P, 2, TL])
        g_rot = place("g_rot", [P, 2, TL])
        gk_hi = place("gk_hi", [P, T], f32r)
        gk_lo = place("gk_lo", [P, T], f32r)
        gv_hi = place("gv_hi", [P, 4, P], f32r)
        gv_lo = place("gv_lo", [P, 4, P], f32r)
        assert cursor[0] <= ring0 + (2 * SLOTS + 2) * SLOT * 4, cursor[0]

        cursor[0] = work0
        sq = place("sq", [P, KC, T])
        mla0 = cursor[0]
        qa_hi = place("qa_hi", [P, QL // P, T], f32r)
        qa_lo = place("qa_lo", [P, QL // P, T], f32r)
        ca_hi = place("ca_hi", [P, KVL // P, T], f32r)
        ca_lo = place("ca_lo", [P, KVL // P, T], f32r)
        kr = place("kr", [QKD, T])
        kr_rot = place("kr_rot", [QKD, TL])
        mla1 = cursor[0]
        cursor[0] = work0
        pc_hi = place("pc_hi", [P, 2, TL], f32r)
        pc_lo = place("pc_lo", [P, 2, TL], f32r)
        mp = place("mp", [P, 3, T])
        mq = place("mq", [QKD, 2, T])
        mq_rot = place("mq_rot", [QKD, 2, TL])
        assert cursor[0] <= mla0
        cursor[0] = mla0
        x_rows = place("x_rows", [P, 4, D])
        work_end = max(mla1, cursor[0])
        cursor[0] = work0
        hid_hi = place("hid_hi", [P, 6, T], f32r)
        hid_lo = place("hid_lo", [P, 6, T], f32r)
        sil = place("sil", [P, 2, T])
        hid = place("hid", [P, 2, T])
        ffn_end = cursor[0]
        cursor[0] = mla0
        k_hi = place("k_hi", [P, 4, T], f32r)
        k_lo = place("k_lo", [P, 4, T], f32r)
        v_hi = place("v_hi", [P, 4, 256], f32r)
        v_lo = place("v_lo", [P, 4, 256], f32r)
        sink_g = place("sink_g", [P, 4])
        att1_end = cursor[0]
        cursor[0] = work0
        o_hi = place("o_hi", [P, KC, TL], f32r)
        o_lo = place("o_lo", [P, KC, TL], f32r)
        kf = place("kf", [P, 2, T], at=ring1)
        kf_rot = place("kf_rot", [P, 2, TL], at=ring1 + 4096)
        out_rows = place("out_rows", [P, 2, D], at=mla0)
        tok_hi = place("tok_hi", [P, 2, D], f32r, at=ring1)
        tok_lo = place("tok_lo", [P, 2, D], f32r, at=ring1 + 2 * D * 4)
        assert ring1 + 4 * D * 4 <= work0
        pick = place("pick", [P, NEXP, T], f32r, at=x_t_at)
        put_hi, put_lo = h_hi, h_lo
        cb = place("cb", [P, NEXP, TL], at=tables0)
        s_sil = place("s_sil", [P, 2, TL], at=tables0 + NEXP * TL * 4)
        assert tables0 + (NEXP + 2) * TL * 4 <= tables1
        cursor[0] = work0
        xg_hi = place("xg_hi", [P, KC, P], f32r)
        xg_lo = place("xg_lo", [P, KC, P], f32r)
        comb_rep = place("comb_rep", [P, 2, NEXP, P], at=cursor[0])
        sh_hi = place("sh_hi", [P, 11, TL], f32r)
        sh_lo = place("sh_lo", [P, 11, TL], f32r)
        s_hid = place("s_hid", [P, 2, TL])
        put_tok = place("put_tok", [P, NEXP, TL], at=cursor[0])
        y_tmp = place("y_tmp", [P, 4, T], at=cursor[0])
        y_hi = place("y_hi", [P, D], f32r)
        y_lo = place("y_lo", [P, D], f32r)
        comb = place("comb", [P, 2, NEXP])
        lg = place("lg", [P, 2, NEXP])
        top = place("top", [P, 2, 8])
        top_i = place("top_i", [P, 2, 8], u32)
        top_f = place("top_f", [P, 2, 8])
        gate = place("gate", [P, 2, 4])
        hot = place("hot", [P, 2, NEXP])
        sel = place("sel", [P, 2, NEXP])
        sel_b = place("sel_b", [P, 2, NEXP])
        slot_no = place("slot_no", [P, 2, NEXP])
        most = place("most", [P, 1])
        wide = place("wide", [P, NEXP], i32)
        any_wide = place("any_wide", [P, 1], i32)
        moe_end = cursor[0]
        cursor[0] = max(work_end, ffn_end, att1_end, moe_end)
        nmax = place("nmax", [P, 3, 2])
        psum_e = place("psum_e", [P, 3, 2])
        rsum = place("rsum", [P, 3, 2])
        esink = place("esink", [P, 3, 2])
        mraw = place("mraw", [P, 3, 2])
        assert cursor[0] <= nc.sbuf_usable_end, (cursor[0], nc.sbuf_usable_end)

        B = [stack.enter_context(nc.psum_tensor(f"bank{i}", [P, 512], f32)) for i in range(8)]
        ADA_BANK = B[7]
        FIRST_BANKS = (B[7], B[0])
        first_rows = (ada_rows, place("first_rows", [4, ADA_W], at=ring1))

        s_id = sem("ident_in")
        s_const = sem("constants_in")
        s_eps = sem("eps_set")
        s_mark = sem("pool_waited")
        s_vec = sem("vectors_in")
        s_x = sem("x_rows_in")
        s_ones = sem("ones_set")
        s_vecT = sem("vectors_transposed")
        s_cols = sem("vector_columns")
        s_silu = sem("silu_c_done")
        s_xT = sem("x_transposed")
        s_xc = sem("x_columns_even")
        s_xc1 = sem("x_columns_odd")
        s_rwlo = sem("router_w_lo")
        s_cr = sem("constants_rounded")
        ada_full = [sem(f"ada_full{i}") for i in range(2)]
        ada_first_mm = sem("ada_first_mm")
        ad = {s: sem(f"ada_{s}") for s in ("hi", "lo", "mm", "rows", "turned", "cols")}
        s_mod = sem("mod_ready")
        raw_full = [sem(f"raw_full{i}") for i in range(SLOTS)]
        split_hi = sem("split_hi")
        split_lo = sem("split_lo")
        norm_sem = {s: sem(f"norm_{s}") for s in ("sq", "sum", "rms", "rstd", "tmp", "hi", "lo")}
        norm_base, total = {}, dict.fromkeys(norm_sem, 0)
        for key, chunks, parts, halves in (("n01", KC, 2, 1), ("nq", 3, 1, 1), ("nc", 2, 1, 1), ("n02", KC, 2, 1),
                                           ("n11", KC, 2, 1), ("n12", KC, 1, 1), ("nf", KC, 1, 0)):
            norm_base[key] = dict(total)
            for step, n in (("sq", chunks), ("sum", 1), ("rms", 1), ("rstd", 1), ("tmp", chunks * parts),
                            ("hi", chunks * parts * halves), ("lo", chunks * parts * halves)):
                total[step] += n

        def normed(key, step, n):
            return norm_sem[step], norm_base[key][step] + n

        s_pj = sem("proj0_done")
        s_pje = sem("proj0_evacuated")
        s_krr = sem("k_rope_rotated")
        s_kr = sem("k_rope_steps")
        s_krhi = sem("k_rope_hi")
        s_krlo = sem("k_rope_lo")
        mraw_in = sem("mla_raw_in")
        m = {s: sem(f"mla_{s}") for s in ("w_hi", "w_lo", "proj", "q_f32", "kv_hi", "kv_lo", "rot", "rope",
                                          "q_hi", "q_lo", "scores", "max", "exp", "rsum", "normed",
                                          "turned", "p_hi", "p_lo", "pv", "o_hi", "o_lo")}
        wo = [{s: sem(f"wo{i}_{s}") for s in ("done", "added")} for i in range(2)]
        ff = {s: sem(f"ffn_{s}") for s in ("pe", "silu", "hid", "hid_hi", "hid_lo", "added")}
        s_kv1 = sem("kv1_done")
        s_kf = sem("k1_f32")
        s_krot1 = sem("k1_rotated")
        s_krope1 = sem("k1_rope_steps")
        s_kdup_hi = sem("k1_hi")
        s_kdup_lo = sem("k1_lo")
        s_kdup2 = sem("k1_copied")
        s_v1hi = sem("v1_hi")
        s_v1lo = sem("v1_lo")
        qw_full, qw_hi, qw_lo = sem("qw_full"), sem("qw_hi"), sem("qw_lo")
        g = {s: sem(f"gqa_{s}") for s in ("proj", "q_f32", "rot", "rope", "q_hi", "q_lo", "k_copied", "v_copied", "sinks", "scores",
                                          "max", "nmax", "exp", "esink", "sum", "rsum", "normed", "turned",
                                          "p_hi", "p_lo", "pv", "o_hi", "o_lo")}
        s_lgp = sem("logits_done")
        s_rt = sem("router_top")
        s_rs = sem("router_steps")
        s_gx = sem("gate_exp")
        s_cbp = sem("combine_turned")
        s_cb = sem("combine_ready")
        mo = {s: sem(f"moe_{s}") for s in ("rank", "tok_turned", "tok", "fits", "pick", "put_tok", "put_turned",
                                           "put_hi", "put_lo", "gathered", "xg", "pe", "silu", "hid", "hid_turned",
                                           "hid_hi",
                                           "hid_lo", "y_hi", "y_lo", "scattered", "weighted", "added")}
        s_sel = sem("selected")
        s_oT = sem("out_turned")
        s_orow = sem("out_rows_ready")
        s_out = sem("out_written")

        from_one = [m[k] for k in ("exp", "p_lo", "o_lo", "proj")] + [qw_lo]
        from_one += [g[k] for k in ("exp", "turned", "pv", "p_lo", "o_lo", "proj")]
        from_one += [ad["lo"], ad["lo"], ad["mm"]]
        from_one += [mo[k] for k in ("pe", "hid", "hid_lo", "y_lo")]
        from_one += [ff[k] for k in ("pe", "hid", "hid_lo", "added")]

        K_BANKS = (5, 2)
        LAT, CTX = slice(0, TL), slice(TL, T)
        HALVES = (LAT, CTX)

        def norms_of(layer, which):
            return gain[layer][:, which], (lambda kc, v: mod[layer][:, 24 * which + kc, v:v + 1])

        def used(n):
            if n < BASE_PROJ0:
                return ada_first_mm, n + 1
            if n < BASE_WO0:
                return s_pj, (2, 3, 6)[n - BASE_PROJ0]
            if n < BASE_FFN0:
                return wo[0]["done"], sum(WO_COLS_0[:n - BASE_WO0 + 1]) // P
            if n < BASE_KV1:
                e, s = divmod(n - BASE_FFN0, NITEMS)
                return ff["pe"], ONE + e * PER_EXP + DONE_BY_ITEM[s + 1]
            if n < BASE_WO1:
                return s_kv1, 2 * (n - BASE_KV1 + 1)
            return wo[1]["done"], sum(WO_COLS_1[:n - BASE_WO1 + 1]) // P

        AUX = (0, 1, 2, 0)
        OUT = (0, 1, 2, 3)
        AUX_WIDE = (3, 4, 3, 4)
        OUT_WIDE = (0, 1, 2, 5)
        GATHERS = ((tok_hi, xg_hi, 0), (tok_hi, xg_hi, 4), (tok_lo, xg_lo, 0), (tok_lo, xg_lo, 4))

        def y_runs(m, k):
            cut = min(max(4 - m, 0), k)
            return [r for r in ((3, m * P, 0, cut), (4, max(m - 4, 0) * P, cut, k - cut)) if r[3]]

        block = stack.enter_context(nc.Block())

        @block.sync
        def _(sp):
            def load(dst, src, s):
                sp.dma_start(dst, src).then_inc(s, 16)

            def row_chunks(a):
                return a.rearrange("(r p) -> r p", p=P)

            load(ident[:, :], k_ident, s_id)
            for name, src in (("norm_g", norm_g.rearrange("a b (r p) -> (a b r) p", p=P)),
                              ("final_g", row_chunks(final_g)), ("q_norm_g", row_chunks(q_norm_g[0])),
                              ("kv_norm_g", row_chunks(kv_norm_g[0])), ("c", row_chunks(c[0])),
                              ("c_ctx", row_chunks(c_ctx)), ("ada_b0", row_chunks(ada_b[0]))):
                r0, n = ROWS_A[name]
                load(rows_a[r0:r0 + n, :], src, s_vec)
            load(rows_b[:, :], row_chunks(ada_b[1]), s_vec)
            load(x_rows[:, 0:2, :], x[0].rearrange("(t p) d -> p t d", p=P), s_x)
            load(x_rows[:, 2:4, :], ctx_x[0].rearrange("(t p) d -> p t d", p=P), s_x)

            def ada_tile(layer, a, n):
                w = ada_w[layer].rearrange("(k p) n -> p k n", p=P)
                for h in range(2):
                    sp.wait_ge(ad["lo"], n * 2 + (h + ONE))
                    sp.dma_start(ada_raw[:, h], w[:, h * (KC // 2):(h + 1) * (KC // 2), bass.ds(a * ADA_W, ADA_W)])\
                      .then_inc(ada_full[h], 16)

            def slot_free(n):
                if n >= SLOTS:
                    sp.wait_ge(split_lo, n - SLOTS + 1)

            def tile_cols(n, w, c0, ncols, nk=KC):
                slot_free(n)
                dst = raw[:, n % SLOTS, 0:nk * ncols].rearrange("p (k n) -> p k n", k=nk)
                src = w.rearrange("(k p) n -> p k n", p=P)
                for a, b in ((0, nk // 2), (nk // 2, nk)):
                    load(dst[:, a:b, :], src[:, a:b, c0:c0 + ncols], raw_full[n % SLOTS])

            for a in range(ADA_FIRST):
                tile_cols(a, ada_w[0], a * ADA_W, ADA_W)
            for dst, src in ((rot_mla[:, :], k_rot_mla), (rot_gqa[:, :], k_rot_gqa),
                             (cs_mla[:, :, :, :], k_cs_mla), (cs_gqa[:, :, :, :], k_cs_gqa),
                             (mask[:, :, :], k_mask), (iota[:, :], k_iota), (tri[:, :], k_tri),
                             (sink_b[:, :], sinks.partition_broadcast(P)[:, 0, :]),
                             (rb_b[:, :], router_b.partition_broadcast(P)[:, 0, :]),
                             (rw[:, :, :], router_w[0].rearrange("(k p) e -> p k e", p=P))):
                load(dst, src, s_const)
            for k, tile in enumerate(((w_dq[0], 0, 256), (w_dq[0], 256, 128), (w_dkv[0], 0, KVL + ROPE))):
                tile_cols(BASE_PROJ0 + k, *tile)
            sp.wait_ge(s_pj, 6)
            load(uq_raw[:, :, :], w_uq[0].rearrange("(k p) n -> p k n", p=P), mraw_in)
            load(ukv_raw[:, :, :], w_ukv[0].rearrange("(k p) n -> p k n", p=P), mraw_in)
            sp.wait_ge(ad["turned"], ADA_FIRST)
            with sp.Fori(0, H // 2) as i:
                for j in range(2):
                    ada_tile(0, i * 2 + (ADA_FIRST + j), i * 2 + j)
            sp.wait_ge(m["w_lo"], 2 * (H // 2))
            c0 = 0
            for k, cols in enumerate(WO_COLS_0):
                tile_cols(BASE_WO0 + k, w_o0[0], c0, cols)
                c0 += cols

            def ffn_tiles(w_gu, w_dn, width, gu_col, dn_row, first_lo, base, ada=None):
                for s, (kind, gr, k, f0, m0) in enumerate(ITEMS):
                    slot = s % SLOTS
                    sp.wait_ge(split_lo, first_lo + (s - SLOTS + 1))
                    if kind == "up":
                        dst = raw[:, slot, 0:KC * 256].rearrange("p (k n) -> p k n", k=KC)
                        src = w_gu.rearrange("(k p) n -> p k n", p=P)
                        load(dst[:, :, 0:P], src[:, :, bass.ds(gu_col + f0 * P, P)], raw_full[slot])
                        load(dst[:, :, P:2 * P], src[:, :, bass.ds(gu_col + (width + f0 * P), P)], raw_full[slot])
                    else:
                        nf, cols = GROUPS[gr][1], k * P
                        dst = raw[:, slot, 0:nf * cols].rearrange("p (k n) -> p k n", k=nf)
                        for a, b in ((0, nf // 2), (nf // 2, nf)):
                            src = w_dn[bass.ds(dn_row + (f0 + a) * P, (b - a) * P), m0 * P:m0 * P + cols]
                            load(dst[:, a:b, :], src.rearrange("(k p) n -> p k n", p=P), raw_full[slot])
                    if ada is not None and 2 <= s < 2 + ADA_TILES // 2:
                        ada_tile(1, ada + (s - 2), ada + (ADA_MLA + s - 2))

            with sp.Fori(0, 2) as e:
                ffn_tiles(ffn_gu[0], ffn_dn[0], DFF, e * EFF, e * EFF, e * NITEMS + BASE_FFN0, BASE_FFN0,
                          ada=e * (ADA_TILES // 2))
            tile_cols(BASE_KV1, w_qkv[0], H * HD, 256)
            tile_cols(BASE_KV1 + 1, w_qkv[0], H * HD + 256, 256)
            sp.wait_ge(split_lo, BASE_KV1)
            with sp.Fori(0, 4) as gi:
                sp.wait_ge(qw_lo, ONE + gi)
                sp.dma_start(raw[:, Q_SLOT, 0:KC * 256].rearrange("p (k n) -> p k n", k=KC),
                             w_qkv[0].rearrange("(k p) n -> p k n", p=P)[:, :, bass.ds(gi * 256, 256)])\
                  .then_inc(qw_full, 16)
            sp.wait_ge(qw_lo, ONE + 4)
            for k, cols in enumerate(WO_COLS_1):
                tile_cols(BASE_WO1 + k, w_o1[0], 256 * k, cols)
            with sp.Fori(0, NEXP) as e:
                ffn_tiles(moe_gu[0, e], moe_dn[0, e], EFF, 0, 0, e * NITEMS + BASE_FFN1, BASE_FFN1)
            for t in range(2):
                sp.wait_ge(s_orow, 4 * (t + 1))
                sp.dma_start(out[0, t * P:(t + 1) * P, :], out_rows[:, t, :]).then_inc(s_out, 16)
            sp.wait_ge(s_out, 32)

        @block.gpsimd
        def _(pool):
            for s in from_one:
                pool.sem_inc(s, ONE)
            pool.memset(ones[:, :], 1.0).then_inc(s_ones, 1)
            pool.wait_ge(s_ones, 1)

            with pool.Fori(0, H // 2) as i:
                for u in range(6):
                    pool.wait_ge(m["rsum"], i * 6 + (u + 1))
                    if u % 3 < 2:
                        pool.tensor_tensor(mp[:, u % 3, :], mp[:, u % 3, :], rsum[:, u % 3, 0:1].to_broadcast([P, T]),
                                           ALU.mult).then_inc(m["normed"], 2)
                    else:
                        for t in range(2):
                            cs = slice(t * TL, (t + 1) * TL)
                            pool.tensor_tensor(mp[:, 2, cs], mp[:, 2, cs], rsum[:, 2, t:t + 1].to_broadcast([P, TL]),
                                               ALU.mult).then_inc(m["normed"], 1)

            def hidden(q, e_gu, f, k, nt):
                pool.wait_ge(q["hid"], ONE + e_gu + (k + 1))
                b = k % 2
                pool.tensor_tensor(hid_hi[:, f, 0:nt], hid[:, b, 0:nt], ones[:, 0:1].to_broadcast([P, nt]), ALU.mult)\
                    .then_inc(q["hid_hi"], 1)
                pool.wait_ge(q["hid_hi"], e_gu + (k + 1))
                pool.tensor_tensor(hid_lo[:, f, 0:nt], hid[:, b, 0:nt], hid_hi[:, f, 0:nt].bitcast(f32),
                                   ALU.subtract).then_inc(q["hid_lo"], 1)

            def ffn(q, e, nt):
                for gr, (f0, nf, parts) in enumerate(GROUPS):
                    if gr == 0:
                        pool.wait_ge(q["pe"], ONE + e * PER_EXP)
                    else:
                        pool.wait_ge(q["pe"], ONE + e * PER_EXP + HALF_EXP)
                    for f in range(nf):
                        hidden(q, e * 11, f, f0 + f, nt)

            with pool.Fori(0, 2) as e:
                ffn(ff, e, T)

            def k_copies(gi):
                pool.tensor_tensor(pool_mark[:, 0:1], ones[:, 0:1], ones[:, 0:1], ALU.mult).then_inc(s_mark, 1)
                pool.tensor_copy(gk_hi[:, :], k_hi[:, gi, :].bitcast(f32)).then_inc(g["k_copied"], 1)
                pool.tensor_copy(gk_lo[:, :], k_lo[:, gi, :].bitcast(f32)).then_inc(g["k_copied"], 1)

            def v_copies(gi):
                pool.tensor_tensor(pool_mark[:, 1:2], ones[:, 0:1], ones[:, 0:1], ALU.mult).then_inc(s_mark, 1)
                for half in range(2):
                    for dst, src in ((gv_hi, v_hi), (gv_lo, v_lo)):
                        pool.tensor_copy(dst[:, :, half * HD:(half + 1) * HD],
                                         src[:, :, bass.ds(gi * HD, HD)].bitcast(f32)).then_inc(g["v_copied"], 1)

            def g_body(gi, following):
                for u in range(8):
                    pool.wait_ge(g["rsum"], gi * 8 + (u + 1))
                    pool.tensor_tensor(gp[:, u % 3, :], gp[:, u % 3, :], rsum[:, u % 3, 0:1].to_broadcast([P, T]),
                                       ALU.mult).then_inc(g["normed"], 1)
                    if u == 6 and following:
                        pool.wait_ge(g["scores"], gi * 8 + 8)
                        k_copies(gi + 1)
                if following:
                    pool.wait_ge(g["pv"], ONE + gi * 4 + 4)
                    v_copies(gi + 1)

            pool.wait_ge(s_kdup2, 8)
            pool.wait_ge(s_v1lo, 2)
            k_copies(0)
            v_copies(0)
            with pool.Fori(0, 3) as gi:
                g_body(gi, True)
            g_body(3, False)

            def moe_hidden(e, n):
                for k in range(11):
                    pool.wait_ge(mo["hid"], ONE + e * 11 + (k + 1))
                    pool.tensor_tensor(sh_hi[:, k, 0:n], s_hid[:, k % 2, 0:n], ones[:, 0:1].to_broadcast([P, n]),
                                       ALU.mult).then_inc(mo["hid_hi"], 1)
                    pool.wait_ge(mo["hid_hi"], e * 11 + (k + 1))
                    pool.tensor_tensor(sh_lo[:, k, 0:n], s_hid[:, k % 2, 0:n], sh_hi[:, k, 0:n].bitcast(f32),
                                       ALU.subtract).then_inc(mo["hid_lo"], 1)

            pool.wait_ge(mo["fits"], 2)
            with pool.Fori(0, NEXP) as e:
                with pool.If(pool.value_load(wide[0:1, bass.ds(e, 1)], min_val=0, max_val=1) > 0):
                    moe_hidden(e, TL)

        @block.scalar
        def _(act):
            def split(n, size):
                slot = n % SLOTS
                act.wait_ge(raw_full[slot], 32 * (n // SLOTS + 1))
                if n >= SLOTS:
                    act.wait_ge(*used(n - SLOTS))
                act.copy(w_hi[:, slot, 0:size], raw[:, slot, 0:size]).then_inc(split_hi, 1)

            def ada_cols_to(layer, m0, bank=ADA_BANK):
                act.copy(mod4[layer][:, bass.ds(m0, 2), :], bank[:, 256:264].rearrange("p (m v) -> p m v", v=4))\
                    .then_inc(ad["cols"], 1)

            def ada_first_rows(n):
                act.wait_ge(ada_first_mm, n + 1)
                act.copy(first_rows[n % 2][:, :], FIRST_BANKS[n % 2][0:4, 0:ADA_W]).then_inc(ad["rows"], 1)

            def ada_first_cols(n):
                act.wait_ge(ad["turned"], n + 1)
                ada_cols_to(0, 2 * n, FIRST_BANKS[n % 2])

            def ada_half_hi(n, h):
                act.wait_ge(ada_full[h], n * 16 + 16)
                act.wait_ge(ad["mm"], n * 2 + (h + ONE))
                act.copy(ada_hi[:, :, :], ada_raw[:, h]).then_inc(ad["hi"], 1)

            def ada_tile_rows(n):
                act.wait_ge(ad["mm"], n * 2 + (2 + ONE))
                act.copy(ada_rows[:, :], ADA_BANK[0:4, 0:ADA_W]).then_inc(ad["rows"], 1)

            def ada_tile_cols(n, layer, m0):
                act.wait_ge(ad["turned"], n + (ADA_FIRST + 1))
                ada_cols_to(layer, m0)

            def norm(key, chunks, width, nt, src, ready, bank, shift, dst_hi, parts, between=None):
                for kc in range(chunks):
                    ready(kc)
                    act.activation(sq[:, kc, 0:nt], src(kc), ACT.Square).then_inc(norm_sem["sq"], 1)
                act.wait_ge(*normed(key, "sum", 1))
                act.wait_ge(s_eps, 1)
                act.activation(rstd[:, 0:nt], bank[:, 0:nt], ACT.Sqrt, scale=1.0 / width,
                               bias=eps_col[:, 0:1]).then_inc(norm_sem["rms"], 1)
                if between:
                    between()
                if dst_hi is None:
                    return
                for kc in range(chunks):
                    for v in range(parts):
                        cs = HALVES[v] if parts == 2 else slice(0, nt)
                        act.wait_ge(*normed(key, "tmp", parts * kc + v + 1))
                        if shift is None:
                            act.copy(dst_hi[:, kc, cs], sq[:, kc, cs]).then_inc(norm_sem["hi"], 1)
                        else:
                            act.activation(dst_hi[:, kc, cs], sq[:, kc, cs], ACT.Identity,
                                           bias=shift(kc, v)).then_inc(norm_sem["hi"], 1)

            act.wait_ge(s_vecT, 2)
            act.copy(cols_a[:, :], B[0][:, 0:NROWS_A]).then_inc(s_cols, 1)
            act.copy(cols_b[:, :], B[1][:, 0:NMOD]).then_inc(s_cols, 1)
            act.wait_ge(s_cols, 2)
            for v, name in enumerate(("c", "c_ctx")):
                r0, n = ROWS_A[name]
                act.activation(silu_c[:, :, v], cols_a[:, r0:r0 + n], ACT.Silu).then_inc(s_silu, 1)
            act.wait_ge(s_silu, 2)
            act.copy(c4[:, :, 0:2], silu_c[:, :, :]).then_inc(s_silu, 1)
            split(0, KC * ADA_W)
            split(1, KC * ADA_W)
            for kc in range(1, KC, 2):
                act.wait_ge(s_xT, kc + 1)
                act.copy(x_t[:, kc, :], B[2 + kc % 4][:, :]).then_inc(s_xc1, 1)
            def x_ready(kc):
                act.wait_ge(s_xc1 if kc % 2 else s_xc, kc // 2 + 1)
            def mid_n01():
                split(2, KC * ADA_W)
                for n in range(ADA_FIRST):
                    ada_first_rows(n)
                    if n + 3 < ADA_FIRST:
                        split(n + 3, KC * ADA_W)
                    ada_first_cols(n)
                for k, cols in enumerate(PROJ0_COLS):
                    split(BASE_PROJ0 + k, KC * cols)

            norm("n01", KC, D, T, lambda kc: x_t[:, kc, :], x_ready, B[6],
                 norms_of(0, 0)[1], h_hi, 2, mid_n01)
            act.wait_ge(s_const, 16 * 10)
            act.wait_ge(s_id, 16)
            act.copy(ident_r[:, :], ident[:, :]).then_inc(s_cr, 1)
            act.copy(mask_r[:, :, :], mask[:, :, :]).then_inc(s_cr, 1)
            act.copy(rw_hi[:, :, :], rw[:, :, :]).then_inc(s_cr, 1)

            act.wait_ge(*normed("n01", "lo", 2 * KC))
            norm("nq", 3, QL, T, lambda kc: B[kc][:, :], lambda kc: act.wait_ge(s_pj, kc + 1), B[6], None, qa_hi, 1)
            act.wait_ge(s_pj, 6)
            act.copy(kr[NOPE:QKD, :], B[5][0:ROPE, :]).then_inc(s_pje, 1)
            act.wait_ge(*normed("nq", "lo", 3))
            norm("nc", 2, KVL, T, lambda kc: B[3 + kc][:, :], lambda kc: act.wait_ge(s_pj, kc + 4), B[6], None,
                 ca_hi, 1)
            act.wait_ge(s_kr, 3)
            for j in range(2):
                act.copy(mk_hi[NOPE:QKD, j, :], kr[NOPE:QKD, :]).then_inc(s_krhi, 1)

            act.wait_ge(mraw_in, 32)
            act.wait_ge(*normed("nc", "lo", 2))

            def mla_exp(i, u):
                act.wait_ge(m["max"], i * 6 + (u + 1))
                if u >= 3:
                    act.wait_ge(m["turned"], i * 6 + (u - 2))
                if u % 3 < 2:
                    act.activation(mp[:, u % 3, :], B[u % 3][:, :], ACT.Exp, bias=nmax[:, u % 3, 0:1],
                                   accum_out=psum_e[:, u % 3, 0:1]).then_inc(m["exp"], 1)
                else:
                    for t in range(2):
                        cs = slice(t * TL, (t + 1) * TL)
                        last = act.activation(mp[:, 2, cs], B[2][:, cs], ACT.Exp, bias=nmax[:, 2, t:t + 1],
                                              accum_out=psum_e[:, 2, t:t + 1])
                    last.then_inc(m["exp"], 1)

            def mla_p_hi(i, u):
                act.wait_ge(m["turned"], i * 6 + (u + 1))
                turned = B[3 + u % 2]
                if u % 3 < 2:
                    act.copy(pl_hi[:, :, (u % 3) * P:(u % 3 + 1) * P],
                             turned[:, :].rearrange("p (c q) -> p c q", c=4)).then_inc(m["p_hi"], 1)
                else:
                    act.copy(pc_hi[:, :, :], turned[:, :].rearrange("p (c q) -> p c q", c=2)).then_inc(m["p_hi"], 1)

            def mla_o_hi(i, j):
                act.wait_ge(m["pv"], i * 2 + (j + 1))
                rows = slice(HD * j, HD * (j + 1))
                act.copy(h_hi[rows, i, :], B[5 + j][rows, :]).then_inc(m["o_hi"], 1)

            def mla_w_hi(n):
                act.wait_ge(m["proj"], n * 5 + ONE)
                act.copy(uq_hi[:, :, :], uq_raw[:, :, bass.ds(n * (2 * QKD), 2 * QKD)]).then_inc(m["w_hi"], 1)
                act.copy(ukv_hi[:, :, :], ukv_raw[:, :, bass.ds(n * 256, 256)]).then_inc(m["w_hi"], 1)

            def mla_q_copy(n, j):
                act.wait_ge(m["proj"], n * 5 + (j + 1 + ONE))
                act.mul(mq[:, j, :], B[j][0:QKD, :], float(QKD) ** -0.5).then_inc(m["q_f32"], 1)

            def mla_k_hi(n, j):
                act.wait_ge(m["proj"], n * 5 + (j + 3 + ONE))
                act.copy(mk_hi[0:NOPE, j, :], B[K_BANKS[j]][0:NOPE, :]).then_inc(m["kv_hi"], 1)

            def mla_q_hi(n):
                act.wait_ge(m["rope"], n * 3 + 3)
                act.copy(mq_hi[:, :, :], mq[:, :, :]).then_inc(m["q_hi"], 1)

            def mla_v_hi(n):
                act.wait_ge(m["proj"], n * 5 + (5 + ONE))
                act.copy(mv_hi[:, :, :], B[3][:, :].rearrange("p (t n) -> p t n", t=4)).then_inc(m["kv_hi"], 1)

            def mla_body(i, n):
                a, b = i * 2, i * 2 + 1
                ma, mb = i * 4 + 2 * ADA_FIRST, i * 4 + (2 * ADA_FIRST + 2)
                more = n is not None
                ada_half_hi(a, 0)
                mla_exp(i, 0)
                mla_exp(i, 1)
                mla_exp(i, 2)
                mla_p_hi(i, 0)
                ada_half_hi(a, 1)
                mla_exp(i, 3)
                if more:
                    mla_w_hi(n)
                mla_p_hi(i, 1)
                mla_p_hi(i, 2)
                mla_exp(i, 4)
                ada_tile_rows(a)
                ada_half_hi(b, 0)
                mla_o_hi(i, 0)
                mla_p_hi(i, 3)
                ada_tile_cols(a, 0, ma)
                mla_exp(i, 5)
                if more:
                    mla_q_copy(n, 0)
                    mla_q_copy(n, 1)
                ada_half_hi(b, 1)
                mla_p_hi(i, 4)
                if more:
                    mla_k_hi(n, 0)
                mla_p_hi(i, 5)
                if more:
                    mla_k_hi(n, 1)
                ada_tile_rows(b)
                if more:
                    mla_q_hi(n)
                mla_o_hi(i, 1)
                if more:
                    mla_v_hi(n)
                ada_tile_cols(b, 0, mb)

            mla_w_hi(0)
            mla_q_copy(0, 0)
            mla_q_copy(0, 1)
            mla_k_hi(0, 0)
            mla_k_hi(0, 1)
            mla_q_hi(0)
            mla_v_hi(0)
            with act.Fori(0, H // 2 - 1) as i:
                mla_body(i, i + 1)
            mla_body(H // 2 - 1, None)

            act.wait_ge(m["pv"], H)
            for k in range(len(WO_COLS_0)):
                split(BASE_WO0 + k, KC * WO_COLS_0[k])

            def x_after_wo(layer):
                return lambda kc: act.wait_ge(wo[layer]["added"], KC if layer else kc + 1)

            def ffn_split(q, e, s, base):
                slot = s % SLOTS
                act.wait_ge(raw_full[slot], e * (32 * NITEMS // SLOTS) + 32 * (base // SLOTS + s // SLOTS + 1))
                act.wait_ge(q["pe"], ONE + e * PER_EXP + DONE_BY_ITEM[s - 2])
                act.copy(w_hi[:, slot, 0:item_size(ITEMS[s % NITEMS])],
                         raw[:, slot, 0:item_size(ITEMS[s % NITEMS])]).then_inc(split_hi, 1)

            def ffn_body(q, e, base, nt, last, tail, with_ada):
                for s, item in enumerate(ITEMS):
                    if s + 2 < NITEMS or not last:
                        ffn_split(q, e, s + 2, base)
                    elif tail:
                        split(*tail[s + 2 - NITEMS])
                    if with_ada and 1 <= s <= ADA_TILES // 2:
                        ada_tile_cols(e * (ADA_TILES // 2) + (ADA_MLA + s - 1), 1, e * ADA_TILES + 2 * (s - 1))
                    if with_ada and s < ADA_TILES // 2:
                        n = e * (ADA_TILES // 2) + (ADA_MLA + s)
                        ada_half_hi(n, 0)
                        ada_half_hi(n, 1)
                    if item[0] == "up":
                        k = item[3]
                        act.wait_ge(q["pe"], ONE + e * PER_EXP + DONE_BY_ITEM[s + 1])
                        if k >= 2:
                            act.wait_ge(q["hid"], ONE + e * 11 + (k - 1))
                        else:
                            act.wait_ge(q["hid"], ONE + e * 11)
                        act.activation(sil[:, k % 2, 0:nt], B[2 * (k % 2)][:, 0:nt], ACT.Silu).then_inc(q["silu"], 1)
                    if with_ada and s < ADA_TILES // 2:
                        ada_tile_rows(n)

            def ffn(q, n_exp, base, nt, tail, with_ada):
                with act.Fori(0, n_exp - 1) as e:
                    ffn_body(q, e, base, nt, False, None, with_ada)
                ffn_body(q, n_exp - 1, base, nt, True, tail, with_ada)

            for s in range(2):
                split(BASE_FFN0 + s, item_size(ITEMS[s]))
            norm("n02", KC, D, T, lambda kc: x_t[:, kc, :], x_after_wo(0), B[6], norms_of(0, 1)[1], h_hi, 2)
            act.wait_ge(*normed("n02", "lo", 2 * KC))
            ffn(ff, 2, BASE_FFN0, T, [(BASE_KV1, 2048), (BASE_KV1 + 1, 2048)], True)

            def x_after_ffn(layer, n_exp):
                return lambda kc: act.wait_ge(ff["added"], ONE + 16 * n_exp)

            norm("n11", KC, D, T, lambda kc: x_t[:, kc, :], x_after_ffn(0, 2), B[6], norms_of(1, 0)[1], h_hi, 2)
            for c2 in range(2):
                act.wait_ge(s_kv1, c2 + 1)
                act.copy(kf[:, c2, :], B[c2][:, :]).then_inc(s_kf, 1)
            for b in range(2):
                act.wait_ge(s_kv1, b + 3)
                act.copy(v_hi[:, 2 * b:2 * b + 2, :], B[2 + b][:, :].rearrange("p (t n) -> p t n", t=2))\
                   .then_inc(s_v1hi, 1)
            act.wait_ge(s_krope1, 3)
            for gg in range(4):
                rows = slice(HD * (gg % 2), HD * (gg % 2 + 1))
                act.copy(k_hi[rows, gg, :], kf[rows, gg // 2, :]).then_inc(s_kdup_hi, 1)
            for gg in range(4):
                rows = slice(HD * (gg % 2), HD * (gg % 2 + 1))
                other = slice(HD * (1 - gg % 2), HD * (2 - gg % 2))
                act.wait_ge(s_kdup_hi, gg + 1)
                act.copy(k_hi[other, gg, :], k_hi[rows, gg, :].bitcast(f32)).then_inc(s_kdup2, 1)
                act.wait_ge(s_kdup_lo, gg + 1)
                act.copy(k_lo[other, gg, :], k_lo[rows, gg, :].bitcast(f32)).then_inc(s_kdup2, 1)

            def g_exp(gi, u):
                act.wait_ge(g["nmax"], gi * 8 + (u + 1))
                if u >= 3:
                    act.wait_ge(g["turned"], ONE + gi * 8 + (u - 2))
                else:
                    act.wait_ge(g["turned"], ONE + gi * 8)
                act.activation(gp[:, u % 3, :], B[u % 3][:, :], ACT.Exp, bias=nmax[:, u % 3, 0:1],
                               accum_out=psum_e[:, u % 3, 0:1]).then_inc(g["exp"], 1)
                act.activation(esink[:, u % 3, 0:1], sink_g[:, u // 2:u // 2 + 1], ACT.Exp,
                               bias=nmax[:, u % 3, 0:1]).then_inc(g["esink"], 1)

            def g_p_hi(gi, u):
                act.wait_ge(g["turned"], ONE + gi * 8 + (u + 1))
                act.wait_ge(g["pv"], ONE + gi * 4 + u // 2)
                act.copy(gt_hi[:, :, (u % 2) * P:(u % 2 + 1) * P],
                         B[3 + u % 2][:, :].rearrange("p (c q) -> p c q", c=4)).then_inc(g["p_hi"], 1)

            def g_o_hi(gi, j):
                act.wait_ge(g["pv"], ONE + gi * 4 + (j + 1))
                rows = slice(HD * (j % 2), HD * (j % 2 + 1))
                act.copy(o_hi[rows, gi * 2 + j // 2, :], B[5 + j % 2][rows, 0:TL]).then_inc(g["o_hi"], 1)

            act.wait_ge(*normed("n11", "lo", 2 * KC))

            def q_split(n):
                act.wait_ge(qw_full, n * 16 + 16)
                act.wait_ge(g["proj"], ONE + n * 2)
                act.copy(w_hi[:, Q_SLOT, 0:2048], raw[:, Q_SLOT, 0:2048]).then_inc(qw_hi, 1)

            def q_scale(n):
                act.wait_ge(g["proj"], ONE + n * 2 + 2)
                act.mul(gq[:, :, :], B[7][:, :].rearrange("p (j t) -> p j t", j=2), float(HD) ** -0.5)\
                   .then_inc(g["q_f32"], 1)

            def q_hi(n):
                act.wait_ge(g["rope"], n * 3 + 3)
                act.copy(gq_hi[:, :, :], gq[:, :, :]).then_inc(g["q_hi"], 1)

            def g_body(gi, following):
                act.copy(sink_g[:, :], sink_b[:, bass.ds(gi * 4, 4)]).then_inc(g["sinks"], 1)
                act.wait_ge(g["sinks"], gi + 1)
                g_exp(gi, 0)
                g_exp(gi, 1)
                for u in range(8):
                    if u + 2 < 8:
                        g_exp(gi, u + 2)
                    g_p_hi(gi, u)
                    if u % 2 == 0 and u >= 2:
                        g_o_hi(gi, u // 2 - 1)
                    if following:
                        if u == 0:
                            q_split(gi + 1)
                        elif u == 3:
                            act.wait_ge(g["q_lo"], gi + 1)
                            q_scale(gi + 1)
                        elif u == 6:
                            act.wait_ge(g["scores"], gi * 8 + 8)
                            q_hi(gi + 1)
                g_o_hi(gi, 3)

            q_split(0)
            q_scale(0)
            q_hi(0)
            with act.Fori(0, 3) as gi:
                g_body(gi, True)
            g_body(3, False)

            act.wait_ge(g["pv"], ONE + H)
            for k in range(len(WO_COLS_1)):
                split(BASE_WO1 + k, KC * WO_COLS_1[k])
            for s in range(2):
                split(BASE_FFN1 + s, item_size(ITEMS[s]))
            norm("n12", KC, D, TL, lambda kc: x_t[:, kc, LAT], x_after_wo(1), B[6], norms_of(1, 1)[1], h_hi, 1)
            for k in range(8):
                if k == 3:
                    act.wait_ge(s_rt, 3)
                    act.activation(gate[:, :, 1:2], gate[:, :, 0:1], ACT.Exp).then_inc(s_gx, 1)
                act.wait_ge(mo["tok_turned"], k + 1)
                act.copy((tok_hi, tok_lo)[k // 4][:, (k // 2) % 2, (k % 2) * 512:(k % 2 + 1) * 512],
                         B[2 + k % 6][:, :]).then_inc(mo["tok"], 1)
            act.wait_ge(*normed("n12", "lo", KC))

            def xg_copies(done, banks):
                for j, (_, dst, kc) in enumerate(GATHERS):
                    act.wait_ge(mo["gathered"], done + (j + 1))
                    act.copy(dst[:, kc:kc + 4, :], B[banks[j]][:, :].rearrange("p (k n) -> p k n", k=4))\
                       .then_inc(mo["xg"], 1)

            def turned_hi(e, k):
                act.wait_ge(mo["hid_turned"], e * 11 + (k + 1))
                act.copy(sh_hi[:, k, 0:P], B[5][:, 0:P]).then_inc(mo["hid_hi"], 1)

            def moe_body(e, first, last, is_wide):
                n = TL if is_wide else P
                for s, item in enumerate(ITEMS):
                    if s == 14 and not last:
                        xg_copies(e * 4 + 4, AUX_WIDE if is_wide else AUX)
                    if s in (6, 14) and not is_wide:
                        turned_hi(e, 5 if s == 6 else 10)
                    if s + 2 < NITEMS or not last:
                        s2, slot = s + 2, (s + 2) % SLOTS
                        act.wait_ge(raw_full[slot],
                                    e * (32 * NITEMS // SLOTS) + 32 * (BASE_FFN1 // SLOTS + s2 // SLOTS + 1))
                        act.wait_ge(mo["pe"], ONE + e * NITEMS + s)
                        act.copy(w_hi[:, slot, 0:item_size(ITEMS[s2 % NITEMS])],
                                 raw[:, slot, 0:item_size(ITEMS[s2 % NITEMS])]).then_inc(split_hi, 1)
                    if item[0] == "up":
                        k = item[3]
                        act.wait_ge(mo["pe"], ONE + e * NITEMS + (s + 1))
                        act.wait_ge(mo["hid"], ONE + e * 11 + max(k - 1, 0))
                        act.activation(s_sil[:, k % 2, 0:n], B[6 + k % 2][:, 0:n], ACT.Silu).then_inc(mo["silu"], 1)
                        if not is_wide and item[2]:
                            turned_hi(e, k - 1)
                    if s in (16, 17) and not is_wide:
                        h = s - 16
                        if h == 0 and not first:
                            act.wait_ge(mo["added"], e * 4)
                        act.wait_ge(mo["pe"], ONE + e * NITEMS + (16 + 2 * h))
                        act.copy(y_hi[:, h * 512:(h + 1) * 512], B[3 + h][:, :]).then_inc(mo["y_hi"], 1)
                if is_wide:
                    act.sem_inc(mo["y_hi"], 2)

            def expert(e, first, last):
                with act.If(act.value_load(wide[0:1, bass.ds(e, 1)], min_val=0, max_val=1) > 0):
                    moe_body(e, first, last, True)
                with act.Else():
                    moe_body(e, first, last, False)

            act.wait_ge(mo["fits"], 2)
            xg_copies(0, AUX)
            for b in range(4):
                act.wait_ge(mo["put_turned"], b + 1)
                act.copy(put_hi[:, 2 * b:2 * b + 2, CTX],
                         B[(3, 4, 6, 7)[b]][:, :].rearrange("p (e t) -> p e t", e=2)).then_inc(mo["put_hi"], 1)
            with act.If(act.value_load(any_wide[0:1, 0:1], min_val=0, max_val=1) > 0):
                for b in range(4):
                    act.wait_ge(s_cbp, b + 1)
                    act.copy(cb[:, 2 * b:2 * b + 2, :], B[(3, 4, 6, 7)[b]][:, :].rearrange("p (e t) -> p e t", e=2))\
                       .then_inc(s_cb, 1)
            expert(0, True, False)
            with act.Fori(1, NEXP - 1) as e:
                expert(e, False, False)
            expert(NEXP - 1, False, True)
            act.wait_ge(mo["added"], 4 * NEXP)
            norm("nf", KC, D, TL, lambda kc: x_t[:, kc, LAT], lambda kc: None, B[6], None, None, 1)

        @block.vector
        def _(dve):
            def lo_of(slot, size, n_hi):
                dve.wait_ge(split_hi, n_hi)
                dve.tensor_tensor(w_lo[:, slot, 0:size], raw[:, slot, 0:size], w_hi[:, slot, 0:size].bitcast(f32),
                                  ALU.subtract).then_inc(split_lo, 1)

            def root(key, nt):
                dve.wait_ge(*normed(key, "rms", 1))
                dve.reciprocal(rstd[:, 0:nt], rstd[:, 0:nt]).then_inc(norm_sem["rstd"], 1)

            def norm(key, chunks, nt, src, gains, shift, dst_hi, dst_lo, parts, rooted=False):
                if not rooted:
                    root(key, nt)
                dve.wait_ge(*normed(key, "rstd", 1))

                def low(kc):
                    for v in range(parts):
                        cs = HALVES[v] if parts == 2 else slice(0, nt)
                        dve.wait_ge(*normed(key, "hi", parts * kc + v + 1))
                        if shift is None:
                            dve.tensor_tensor(dst_lo[:, kc, cs], sq[:, kc, cs], dst_hi[:, kc, cs].bitcast(f32),
                                              ALU.subtract).then_inc(norm_sem["lo"], 1)
                        else:
                            dve.scalar_tensor_tensor(out=dst_lo[:, kc, cs], in0=sq[:, kc, cs], scalar=shift(kc, v),
                                                     in1=dst_hi[:, kc, cs].bitcast(f32), op0=ALU.add,
                                                     op1=ALU.subtract).then_inc(norm_sem["lo"], 1)

                for kc in range(chunks):
                    for v in range(parts):
                        cs = HALVES[v] if parts == 2 else slice(0, nt)
                        dve.scalar_tensor_tensor(out=sq[:, kc, cs], in0=src(kc, cs), scalar=gains(kc, v),
                                                 in1=rstd[:, cs], op0=ALU.mult, op1=ALU.mult).then_inc(norm_sem["tmp"], 1)
                    if kc and dst_hi is not None:
                        low(kc - 1)
                if dst_hi is not None:
                    low(chunks - 1)

            def mod_cols(layer, a, b, bias, done):
                for v in range(2):
                    dve.tensor_tensor(mod[layer][:, a:b, v], mod4[layer][:, a:b, 2 + v], bias[:, a:b], ALU.add)\
                       .then_inc(s_mod, 1)
                dve.wait_ge(s_mod, done + 2)
                for v in range(2):
                    dve.tensor_tensor(mod[layer][:, a:b, v], mod[layer][:, a:b, v], mod4[layer][:, a:b, v], ALU.add)\
                       .then_inc(s_mod, 1)
                dve.wait_ge(s_mod, done + 4)

            def ada_half_lo(n, h):
                dve.wait_ge(ad["hi"], n * 2 + (h + 1))
                dve.tensor_tensor(ada_lo[:, :, :], ada_raw[:, h], ada_hi[:, :, :].bitcast(f32), ALU.subtract)\
                   .then_inc(ad["lo"], 1)

            def gains(layer, which):
                r0 = ROWS_A["norm_g"][0] + (2 * layer + which) * KC
                for v in range(2):
                    dve.scalar_tensor_tensor(out=gain[layer][:, which, :, v],
                                             in0=mod[layer][:, 24 * which + 8:24 * which + 16, v], scalar=1.0,
                                             in1=cols_a[:, r0:r0 + KC], op0=ALU.add, op1=ALU.mult).then_inc(s_mod, 1)

            dve.memset(eps_col[:, :], EPS).then_inc(s_eps, 1)
            dve.wait_ge(s_silu, 3)
            dve.tensor_tensor(c4[:, :, 2:4], silu_c[:, :, :], c4[:, :, 0:2].bitcast(f32), ALU.subtract)\
               .then_inc(s_silu, 1)
            for n in range(2):
                lo_of(n, KC * ADA_W, n + 1)
            for kc in range(0, KC, 2):
                dve.wait_ge(s_xT, kc + 1)
                dve.tensor_copy(x_t[:, kc, :], B[2 + kc % 4][:, :]).then_inc(s_xc, 1)
            root("n01", T)
            for n in range(2, ADA_FIRST):
                lo_of(n % SLOTS, KC * ADA_W, n + 1)
            for k, cols in enumerate(PROJ0_COLS):
                lo_of((BASE_PROJ0 + k) % SLOTS, KC * cols, BASE_PROJ0 + k + 1)
            a0 = ROWS_A["ada_b0"][0]
            bias0 = cols_a[:, a0:a0 + NMOD]
            dve.wait_ge(ad["cols"], ADA_FIRST)
            dve.wait_ge(s_cols, 2)
            mod_cols(0, 0, 16, bias0, 0)
            gains(0, 0)
            dve.wait_ge(s_mod, 6)
            ga = [[gain[l][:, w] for w in range(2)] for l in range(2)]
            norm("n01", KC, T, lambda kc, cs: x_t[:, kc, cs], lambda kc, v: ga[0][0][:, kc, v:v + 1],
                 norms_of(0, 0)[1], h_hi, h_lo, 2, rooted=True)
            dve.wait_ge(s_cr, 3)
            dve.tensor_tensor(rw_lo[:, :, :], rw[:, :, :], rw_hi[:, :, :].bitcast(f32), ALU.subtract)\
               .then_inc(s_rwlo, 1)
            qg, kvg = ROWS_A["q_norm_g"][0], ROWS_A["kv_norm_g"][0]
            norm("nq", 3, T, lambda kc, cs: B[kc][:, cs], lambda kc, v: cols_a[:, qg + kc:qg + kc + 1],
                 None, qa_hi, qa_lo, 1)
            norm("nc", 2, T, lambda kc, cs: B[3 + kc][:, cs], lambda kc, v: cols_a[:, kvg + kc:kvg + kc + 1],
                 None, ca_hi, ca_lo, 1)
            rr = slice(NOPE, QKD)
            dve.wait_ge(s_krr, 1)
            dve.tensor_tensor(kr_rot[rr, :], B[5][rr, 0:TL], cs_mla[rr, 1, 0, :], ALU.mult).then_inc(s_kr, 1)
            dve.tensor_tensor(kr[rr, LAT], kr[rr, LAT], cs_mla[rr, 0, 0, :], ALU.mult).then_inc(s_kr, 1)
            dve.wait_ge(s_kr, 2)
            dve.tensor_tensor(kr[rr, LAT], kr[rr, LAT], kr_rot[rr, :], ALU.add).then_inc(s_kr, 1)
            dve.wait_ge(s_krhi, 2)
            for j in range(2):
                dve.tensor_tensor(mk_lo[rr, j, :], kr[rr, :], mk_hi[rr, j, :].bitcast(f32), ALU.subtract)\
                   .then_inc(s_krlo, 1)

            def mla_max(i, u):
                dve.wait_ge(m["scores"], i * 6 + (u + 1))
                if u % 3 < 2:
                    dve.tensor_reduce(nmax[:, u % 3, 0:1], B[u % 3][:, :], AX.X, ALU.max, negate=True)\
                       .then_inc(m["max"], 1)
                else:
                    dve.tensor_reduce(nmax[:, 2, :], B[2][:, :].rearrange("p (t k) -> p t k", t=2), AX.X, ALU.max,
                                      negate=True).then_inc(m["max"], 1)

            def mla_rsum(i, u):
                dve.wait_ge(m["exp"], ONE + i * 6 + (u + 1))
                w = 1 if u % 3 < 2 else 2
                dve.reciprocal(rsum[:, u % 3, 0:w], psum_e[:, u % 3, 0:w]).then_inc(m["rsum"], 1)

            def mla_p_lo(i, u):
                dve.wait_ge(m["p_hi"], i * 6 + (u + 1))
                turned = B[3 + u % 2]
                if u % 3 < 2:
                    cs = slice((u % 3) * P, (u % 3 + 1) * P)
                    dve.tensor_tensor(pl_lo[:, :, cs], turned[:, :].rearrange("p (c q) -> p c q", c=4),
                                      pl_hi[:, :, cs].bitcast(f32), ALU.subtract).then_inc(m["p_lo"], 1)
                else:
                    dve.tensor_tensor(pc_lo[:, :, :], turned[:, :].rearrange("p (c q) -> p c q", c=2),
                                      pc_hi[:, :, :].bitcast(f32), ALU.subtract).then_inc(m["p_lo"], 1)

            def mla_o_lo(i, j):
                dve.wait_ge(m["o_hi"], i * 2 + (j + 1))
                rows = slice(HD * j, HD * (j + 1))
                dve.tensor_tensor(h_lo[rows, i, :], B[5 + j][rows, :], h_hi[rows, i, :].bitcast(f32), ALU.subtract)\
                   .then_inc(m["o_lo"], 1)

            def mla_w_lo(n):
                dve.wait_ge(m["w_hi"], n * 2 + 1)
                dve.tensor_tensor(uq_lo[:, :, :], uq_raw[:, :, bass.ds(n * (2 * QKD), 2 * QKD)],
                                  uq_hi[:, :, :].bitcast(f32), ALU.subtract).then_inc(m["w_lo"], 1)
                dve.wait_ge(m["w_hi"], n * 2 + 2)
                dve.tensor_tensor(ukv_lo[:, :, :], ukv_raw[:, :, bass.ds(n * 256, 256)],
                                  ukv_hi[:, :, :].bitcast(f32), ALU.subtract).then_inc(m["w_lo"], 1)

            def mla_k_lo(n, j):
                dve.wait_ge(m["kv_hi"], n * 3 + (j + 1))
                dve.tensor_tensor(mk_lo[0:NOPE, j, :], B[K_BANKS[j]][0:NOPE, :], mk_hi[0:NOPE, j, :].bitcast(f32),
                                  ALU.subtract).then_inc(m["kv_lo"], 1)

            def mla_v_lo(n):
                dve.wait_ge(m["kv_hi"], n * 3 + 3)
                dve.tensor_tensor(mv_lo[:, :, :], B[3][:, :].rearrange("p (t n) -> p t n", t=4),
                                  mv_hi[:, :, :].bitcast(f32), ALU.subtract).then_inc(m["kv_lo"], 1)

            def mla_rope(n):
                dve.wait_ge(m["rot"], n + 1)
                dve.tensor_tensor(mq_rot[rr, :, :], B[0][rr, :].rearrange("p (j t) -> p j t", j=2),
                                  cs_mla[rr, 1, :, :], ALU.mult).then_inc(m["rope"], 1)
                dve.tensor_tensor(mq[rr, :, LAT], mq[rr, :, LAT], cs_mla[rr, 0, :, :], ALU.mult)\
                   .then_inc(m["rope"], 1)
                dve.wait_ge(m["rope"], n * 3 + 2)
                dve.tensor_tensor(mq[rr, :, LAT], mq[rr, :, LAT], mq_rot[rr, :, :], ALU.add).then_inc(m["rope"], 1)

            def mla_q_lo(n):
                dve.wait_ge(m["q_hi"], n + 1)
                dve.tensor_tensor(mq_lo[:, :, :], mq[:, :, :], mq_hi[:, :, :].bitcast(f32), ALU.subtract)\
                   .then_inc(m["q_lo"], 1)

            def mla_body(i, n):
                more = n is not None
                ada_half_lo(i * 2, 0)
                mla_max(i, 0)
                mla_max(i, 1)
                mla_rsum(i, 0)
                mla_max(i, 2)
                mla_rsum(i, 1)
                mla_p_lo(i, 0)
                mla_rsum(i, 2)
                ada_half_lo(i * 2, 1)
                mla_max(i, 3)
                mla_p_lo(i, 1)
                mla_rsum(i, 3)
                if more:
                    mla_w_lo(n)
                mla_p_lo(i, 2)
                mla_max(i, 4)
                mla_rsum(i, 4)
                ada_half_lo(i * 2 + 1, 0)
                mla_o_lo(i, 0)
                mla_p_lo(i, 3)
                mla_max(i, 5)
                mla_rsum(i, 5)
                ada_half_lo(i * 2 + 1, 1)
                mla_p_lo(i, 4)
                if more:
                    mla_k_lo(n, 0)
                mla_p_lo(i, 5)
                if more:
                    mla_k_lo(n, 1)
                    mla_rope(n)
                    mla_q_lo(n)
                mla_o_lo(i, 1)
                if more:
                    mla_v_lo(n)

            mla_w_lo(0)
            mla_k_lo(0, 0)
            mla_k_lo(0, 1)
            mla_rope(0)
            mla_q_lo(0)
            mla_v_lo(0)
            with dve.Fori(0, H // 2 - 1) as i:
                mla_body(i, i + 1)
            mla_body(H // 2 - 1, None)

            dve.wait_ge(ad["cols"], ADA_TILES)
            mod_cols(0, 16, NMOD, bias0, 6)
            gains(0, 1)
            dve.wait_ge(s_mod, 12)

            def add_out(layer, mc, bank, parts, which, done):
                for v in range(parts):
                    last = dve.scalar_tensor_tensor(out=x_t[:, mc, HALVES[v]], in0=bank[:, HALVES[v]],
                                                    scalar=mod[layer][:, 8 * which + mc, v:v + 1],
                                                    in1=x_t[:, mc, HALVES[v]], op0=ALU.mult, op1=ALU.add)
                last.then_inc(done, 1)

            def wo_phase(layer, base, cols, parts):
                mc = 0
                sizes = [KC * w for w in cols]
                for k in range(min(2, len(cols))):
                    lo_of((base + k) % SLOTS, sizes[k], base + k + 1)
                for k, w in enumerate(cols):
                    if k + 2 < len(cols):
                        lo_of((base + k + 2) % SLOTS, sizes[k + 2], base + k + 3)
                    for j in range(w // P):
                        dve.wait_ge(wo[layer]["done"], mc + 1)
                        add_out(layer, mc, B[mc % 2], parts, 2, wo[layer]["added"])
                        mc += 1

            def ffn_body(q, layer, e, base, nt, parts, last, tail):
                for s, item in enumerate(ITEMS):
                    if layer == 0 and s < ADA_TILES // 2:
                        ada_half_lo(e * (ADA_TILES // 2) + (ADA_MLA + s), 0)
                    if s + 2 < NITEMS or not last:
                        s2 = s + 2
                        lo_of(s2 % SLOTS, item_size(ITEMS[s2 % NITEMS]), e * NITEMS + (base + s2 + 1))
                    elif tail:
                        n, size = tail[s + 2 - NITEMS]
                        lo_of(n % SLOTS, size, n + 1)
                    if layer == 0 and s < ADA_TILES // 2:
                        ada_half_lo(e * (ADA_TILES // 2) + (ADA_MLA + s), 1)
                    if item[0] == "up":
                        k = item[3]
                        dve.wait_ge(q["silu"], e * 11 + (k + 1))
                        if k >= 2:
                            dve.wait_ge(q["hid_lo"], ONE + e * 11 + (k - 1))
                        else:
                            dve.wait_ge(q["hid_lo"], ONE + e * 11)
                        hb = hid[:, k % 2, 0:nt]
                        formed = dve.tensor_tensor(hb, B[2 * (k % 2) + 1][:, 0:nt], sil[:, k % 2, 0:nt], ALU.mult)
                        formed.then_inc(q["hid"], 1)
                    else:
                        _, gr, n_out, _, m0 = item
                        for j in range(n_out):
                            dve.wait_ge(q["pe"], ONE + e * PER_EXP + (DONE_BY_ITEM[s] + j + 1))
                            dve.wait_ge(q["added"], ONE + e * 16 + (m0 + j + 1 if gr else 0))
                            add_out(layer, m0 + j, B[4 + (m0 + j) % 3], parts, 5, q["added"])

            def ffn(q, layer, n_exp, base, nt, parts, tail):
                with dve.Fori(0, n_exp - 1) as e:
                    ffn_body(q, layer, e, base, nt, parts, False, None)
                ffn_body(q, layer, n_exp - 1, base, nt, parts, True, tail)

            wo_phase(0, BASE_WO0, WO_COLS_0, 2)
            for s in range(2):
                lo_of((BASE_FFN0 + s) % SLOTS, item_size(ITEMS[s]), BASE_FFN0 + s + 1)
            dve.wait_ge(wo[0]["added"], KC)
            norm("n02", KC, T, lambda kc, cs: x_t[:, kc, cs], lambda kc, v: ga[0][1][:, kc, v:v + 1],
                 norms_of(0, 1)[1], h_hi, h_lo, 2)
            ffn(ff, 0, 2, BASE_FFN0, T, 2, [(BASE_KV1, 2048), (BASE_KV1 + 1, 2048)])

            dve.wait_ge(ad["cols"], 2 * ADA_TILES)
            mod_cols(1, 0, NMOD, cols_b, 12)
            gains(1, 0)
            gains(1, 1)
            dve.wait_ge(s_mod, 20)
            dve.wait_ge(ff["added"], ONE + 32)
            norm("n11", KC, T, lambda kc, cs: x_t[:, kc, cs], lambda kc, v: ga[1][0][:, kc, v:v + 1],
                 norms_of(1, 0)[1], h_hi, h_lo, 2)
            dve.wait_ge(s_krot1, 1)
            dve.tensor_tensor(kf_rot[:, :, :], B[4][:, :].rearrange("p (c t) -> p c t", c=2), cs_gqa[:, 1],
                              ALU.mult).then_inc(s_krope1, 1)
            dve.tensor_tensor(kf[:, :, LAT], kf[:, :, LAT], cs_gqa[:, 0], ALU.mult).then_inc(s_krope1, 1)
            dve.wait_ge(s_krope1, 2)
            dve.tensor_tensor(kf[:, :, LAT], kf[:, :, LAT], kf_rot[:, :, :], ALU.add).then_inc(s_krope1, 1)
            for b in range(2):
                dve.wait_ge(s_v1hi, b + 1)
                dve.tensor_tensor(v_lo[:, 2 * b:2 * b + 2, :], B[2 + b][:, :].rearrange("p (t n) -> p t n", t=2),
                                  v_hi[:, 2 * b:2 * b + 2, :].bitcast(f32), ALU.subtract).then_inc(s_v1lo, 1)
            for gg in range(4):
                rows = slice(HD * (gg % 2), HD * (gg % 2 + 1))
                dve.wait_ge(s_kdup_hi, gg + 1)
                dve.tensor_tensor(k_lo[rows, gg, :], kf[rows, gg // 2, :], k_hi[rows, gg, :].bitcast(f32),
                                  ALU.subtract).then_inc(s_kdup_lo, 1)

            def g_max(gi, u):
                dve.wait_ge(g["scores"], gi * 8 + (u + 1))
                dve.tensor_reduce(mraw[:, u % 3, 0:1], B[u % 3][:, :], AX.X, ALU.max).then_inc(g["max"], 1)
                dve.wait_ge(g["max"], gi * 8 + (u + 1))
                dve.tensor_scalar(nmax[:, u % 3, 0:1], mraw[:, u % 3, 0:1], sink_g[:, u // 2:u // 2 + 1], -1.0,
                                  ALU.max, ALU.mult).then_inc(g["nmax"], 1)

            def g_rsum(gi, u):
                dve.wait_ge(g["esink"], gi * 8 + (u + 1))
                dve.tensor_tensor(mraw[:, u % 3, 1:2], psum_e[:, u % 3, 0:1], esink[:, u % 3, 0:1], ALU.add)\
                   .then_inc(g["sum"], 1)
                dve.wait_ge(g["sum"], gi * 8 + (u + 1))
                dve.reciprocal(rsum[:, u % 3, 0:1], mraw[:, u % 3, 1:2]).then_inc(g["rsum"], 1)

            def g_p_lo(gi, u):
                dve.wait_ge(g["p_hi"], gi * 8 + (u + 1))
                cs = slice((u % 2) * P, (u % 2 + 1) * P)
                dve.tensor_tensor(gt_lo[:, :, cs], B[3 + u % 2][:, :].rearrange("p (c q) -> p c q", c=4),
                                  gt_hi[:, :, cs].bitcast(f32), ALU.subtract).then_inc(g["p_lo"], 1)

            def g_o_lo(gi, j):
                dve.wait_ge(g["o_hi"], gi * 4 + (j + 1))
                rows = slice(HD * (j % 2), HD * (j % 2 + 1))
                dve.tensor_tensor(o_lo[rows, gi * 2 + j // 2, :], B[5 + j % 2][rows, 0:TL],
                                  o_hi[rows, gi * 2 + j // 2, :].bitcast(f32), ALU.subtract).then_inc(g["o_lo"], 1)

            def qw_low(n):
                dve.wait_ge(qw_hi, n + 1)
                dve.tensor_tensor(w_lo[:, Q_SLOT, 0:2048], raw[:, Q_SLOT, 0:2048],
                                  w_hi[:, Q_SLOT, 0:2048].bitcast(f32), ALU.subtract).then_inc(qw_lo, 1)

            def q_rope(n):
                dve.wait_ge(g["rot"], n + 1)
                dve.tensor_tensor(g_rot[:, :, :], B[7][:, :].rearrange("p (j t) -> p j t", j=2), cs_gqa[:, 1],
                                  ALU.mult).then_inc(g["rope"], 1)
                dve.tensor_tensor(gq[:, :, :], gq[:, :, :], cs_gqa[:, 0], ALU.mult).then_inc(g["rope"], 1)
                dve.wait_ge(g["rope"], n * 3 + 2)
                dve.tensor_tensor(gq[:, :, :], gq[:, :, :], g_rot[:, :, :], ALU.add).then_inc(g["rope"], 1)

            def q_low(n):
                dve.wait_ge(g["q_hi"], n + 1)
                dve.tensor_tensor(gq_lo[:, :, :], gq[:, :, :], gq_hi[:, :, :].bitcast(f32), ALU.subtract)\
                   .then_inc(g["q_lo"], 1)

            def g_body(gi, following):
                dve.wait_ge(g["sinks"], gi + 1)
                g_max(gi, 0)
                g_max(gi, 1)
                g_rsum(gi, 0)
                for u in range(8):
                    if u + 2 < 8:
                        g_max(gi, u + 2)
                    if u + 1 < 8:
                        g_rsum(gi, u + 1)
                    g_p_lo(gi, u)
                    if u % 2 == 0 and u >= 2:
                        g_o_lo(gi, u // 2 - 1)
                    if following:
                        if u == 0:
                            qw_low(gi + 1)
                        elif u == 5:
                            q_rope(gi + 1)
                        elif u == 7:
                            q_low(gi + 1)
                g_o_lo(gi, 3)

            qw_low(0)
            q_rope(0)
            q_low(0)
            with dve.Fori(0, 3) as gi:
                g_body(gi, True)
            g_body(3, False)

            wo_phase(1, BASE_WO1, WO_COLS_1, 1)
            for s in range(2):
                lo_of((BASE_FFN1 + s) % SLOTS, item_size(ITEMS[s]), BASE_FFN1 + s + 1)
            dve.wait_ge(wo[1]["added"], KC)
            norm("n12", KC, TL, lambda kc, cs: x_t[:, kc, cs], lambda kc, v: ga[1][1][:, kc, 0:1],
                 norms_of(1, 1)[1], h_hi, h_lo, 1)
            dve.wait_ge(s_lgp, 1)
            for t in range(2):
                dve.tensor_tensor(lg[:, t, :], B[0][:, t * NEXP:(t + 1) * NEXP], rb_b[:, :], ALU.add)\
                   .then_inc(s_rs, 1)
            dve.wait_ge(s_rs, 2)
            for t in range(2):
                dve.max(top[:, t, :], lg[:, t, :]).then_inc(s_rs, 1)
            dve.wait_ge(s_rs, 4)
            for t in range(2):
                dve.max_index(top_i[:, t, :], top[:, t, :], lg[:, t, :]).then_inc(s_rt, 1)
            dve.tensor_tensor(gate[:, :, 0:1], top[:, :, 1:2], top[:, :, 0:1], ALU.subtract).then_inc(s_rt, 1)
            dve.wait_ge(s_rt, 3)
            dve.tensor_copy(top_f[:, :, :], top_i[:, :, :]).then_inc(s_rs, 1)
            dve.wait_ge(s_rs, 5)
            for t in range(2):
                dve.tensor_scalar(sel[:, t, :], iota[:, 0:NEXP], top_f[:, t, 0:1], None, ALU.is_equal)\
                   .then_inc(s_sel, 1)
                dve.tensor_scalar(sel_b[:, t, :], iota[:, 0:NEXP], top_f[:, t, 1:2], None, ALU.is_equal)\
                   .then_inc(s_sel, 1)
            dve.wait_ge(s_sel, 4)
            dve.tensor_tensor(sel[:, :, :], sel[:, :, :], sel_b[:, :, :], ALU.add).then_inc(s_sel, 1)
            dve.wait_ge(mo["rank"], 1)
            dve.tensor_reduce(most[:, :], B[1][:, 2 * NEXP:3 * NEXP], AX.X, ALU.max).then_inc(s_sel, 1)
            dve.tensor_scalar(wide[:, :], B[1][:, 2 * NEXP:3 * NEXP], P + 0.5, None, ALU.is_gt).then_inc(mo["fits"], 1)
            dve.wait_ge(s_sel, 6)
            dve.tensor_scalar(any_wide[:, :], most[:, :], P + 0.5, None, ALU.is_gt).then_inc(mo["fits"], 1)
            dve.tensor_tensor(slot_no[:, :, :], B[1][:, 0:2 * NEXP].rearrange("p (t e) -> p t e", t=2),
                              sel[:, :, :], ALU.mult).then_inc(s_sel, 1)
            dve.wait_ge(s_sel, 7)
            dve.tensor_scalar(slot_no[:, :, :], slot_no[:, :, :], -1.0, None, ALU.add).then_inc(s_sel, 1)
            dve.wait_ge(s_sel, 8)
            dve.wait_ge(s_gx, 1)
            dve.tensor_scalar(gate[:, :, 2:3], gate[:, :, 1:2], 1.0, None, ALU.add).then_inc(s_rs, 1)
            dve.wait_ge(s_rs, 6)
            dve.reciprocal(gate[:, :, 3:4], gate[:, :, 2:3]).then_inc(s_rs, 1)
            dve.wait_ge(s_rs, 7)
            dve.tensor_tensor(gate[:, :, 2:3], gate[:, :, 1:2], gate[:, :, 3:4], ALU.mult).then_inc(s_rs, 1)
            dve.wait_ge(s_rs, 8)
            for t in range(2):
                dve.tensor_scalar(comb[:, t, :], iota[:, 0:NEXP], top_f[:, t, 0:1], gate[:, t, 3:4], ALU.is_equal,
                                  ALU.mult).then_inc(s_rs, 1)
                dve.tensor_scalar(hot[:, t, :], iota[:, 0:NEXP], top_f[:, t, 1:2], gate[:, t, 2:3], ALU.is_equal,
                                  ALU.mult).then_inc(s_rs, 1)
            dve.wait_ge(s_rs, 12)
            dve.tensor_tensor(comb[:, :, :], comb[:, :, :], hot[:, :, :], ALU.add).then_inc(s_rs, 1)
            dve.wait_ge(s_rs, 13)

            def turned_lo(e, k):
                dve.wait_ge(mo["hid_hi"], e * 11 + (k + 1))
                dve.tensor_tensor(sh_lo[:, k, 0:P], B[5][:, 0:P],
                                  sh_hi[:, k, 0:P].bitcast(f32), ALU.subtract).then_inc(mo["hid_lo"], 1)

            def moe_body(e, first, last, is_wide):
                n = TL if is_wide else P
                for s, item in enumerate(ITEMS):
                    if s in (6, 14) and not is_wide:
                        turned_lo(e, 5 if s == 6 else 10)
                    def low_ahead(s2):
                        lo_of(s2 % SLOTS, item_size(ITEMS[s2 % NITEMS]), e * NITEMS + (BASE_FFN1 + s2 + 1))

                    late = s in (5, 13)
                    if not late and (s + 2 < NITEMS or not last):
                        low_ahead(s + 2)
                    if item[0] == "up":
                        k = item[3]
                        dve.wait_ge(mo["silu"], e * 11 + (k + 1))
                        if is_wide:
                            dve.wait_ge(mo["hid_lo"], ONE + e * 11 + max(k - 1, 0))
                        elif k >= 2:
                            dve.wait_ge(mo["hid_turned"], e * 11 + (k - 1))
                        elif not first:
                            dve.wait_ge(mo["hid_lo"], ONE + e * 11)
                        dve.tensor_tensor(s_hid[:, k % 2, 0:n], B[6 + k % 2][:, n:2 * n], s_sil[:, k % 2, 0:n],
                                          ALU.mult).then_inc(mo["hid"], 1)
                    if s == 1 and not first:
                        put_back(e - 1)
                    if not is_wide:
                        if item[0] == "up" and item[2]:
                            turned_lo(e, item[3] - 1)
                    if late:
                        low_ahead(s + 2)
                for h in range(0 if is_wide else 2):
                    dve.wait_ge(mo["y_hi"], e * 2 + (h + 1))
                    dve.tensor_tensor(y_lo[:, h * 512:(h + 1) * 512], B[3 + h][:, :],
                                      y_hi[:, h * 512:(h + 1) * 512].bitcast(f32), ALU.subtract)\
                       .then_inc(mo["y_lo"], 1)
                if is_wide:
                    dve.sem_inc(mo["y_lo"], 2)

            def put_back(e):
                def gate5(mc):
                    return mod[1][:, 8 * 5 + mc, 0:1]

                with dve.If(dve.value_load(wide[0:1, bass.ds(e, 1)], min_val=0, max_val=1) > 0):
                    dve.wait_ge(mo["pe"], e * NITEMS + (ONE + NITEMS))
                    for j in range(4):
                        for i in range(2):
                            cs = slice(i * TL, (i + 1) * TL)
                            last = dve.scalar_tensor_tensor(out=y_tmp[:, j, cs], in0=B[OUT_WIDE[j]][:, cs],
                                                            scalar=gate5(2 * j + i), in1=cb[:, e, :],
                                                            op0=ALU.mult, op1=ALU.mult)
                        last.then_inc(mo["weighted"], 1)
                    for j in range(4):
                        dve.wait_ge(mo["weighted"], e * 4 + (j + 1))
                        dve.tensor_tensor(x_t[:, 2 * j:2 * j + 2, LAT], x_t[:, 2 * j:2 * j + 2, LAT],
                                          y_tmp[:, j, :].rearrange("p (i t) -> p i t", i=2), ALU.add)\
                           .then_inc(mo["added"], 1)
                with dve.Else():
                    for j in range(4):
                        dve.wait_ge(mo["scattered"], e * 4 + (j + 1))
                        for i in range(2):
                            mc = 2 * j + i
                            dve.scalar_tensor_tensor(out=x_t[:, mc, LAT], in0=B[OUT[j]][:, i * TL:(i + 1) * TL],
                                                     scalar=gate5(mc), in1=x_t[:, mc, LAT], op0=ALU.mult,
                                                     op1=ALU.add).then_inc(mo["added" if i else "weighted"], 1)

            def expert(e, first, last):
                with dve.If(dve.value_load(wide[0:1, bass.ds(e, 1)], min_val=0, max_val=1) > 0):
                    moe_body(e, first, last, True)
                with dve.Else():
                    moe_body(e, first, last, False)

            for e in range(NEXP):
                for t in range(2):
                    dve.tensor_scalar(pick[:, e, TL + t * P:TL + (t + 1) * P], iota[:, :],
                                      slot_no[:, t, e:e + 1], None, ALU.is_equal).then_inc(mo["pick"], 1)
            for e in range(NEXP):
                for t in range(2):
                    dve.tensor_scalar(put_tok[:, e, t * P:(t + 1) * P], iota[:, :], slot_no[:, t, e:e + 1],
                                      comb[:, t, e:e + 1], ALU.is_equal, ALU.mult).then_inc(mo["put_tok"], 1)
            for b in range(4):
                dve.wait_ge(mo["put_hi"], b + 1)
                dve.tensor_tensor(put_lo[:, 2 * b:2 * b + 2, CTX],
                                  B[(3, 4, 6, 7)[b]][:, :].rearrange("p (e t) -> p e t", e=2),
                                  put_hi[:, 2 * b:2 * b + 2, CTX].bitcast(f32), ALU.subtract)\
                   .then_inc(mo["put_lo"], 1)
            with dve.If(dve.value_load(any_wide[0:1, 0:1], min_val=0, max_val=1) > 0):
                for t in range(2):
                    for e in range(NEXP):
                        dve.tensor_scalar(comb_rep[:, t, e, :], ones[:, :], comb[:, t, e:e + 1], None, ALU.mult)\
                           .then_inc(s_rs, 1)
                dve.wait_ge(s_cb, 4)
            expert(0, True, False)
            with dve.Fori(1, NEXP - 1) as e:
                expert(e, False, False)
            expert(NEXP - 1, False, True)
            put_back(NEXP - 1)
            dve.wait_ge(mo["added"], 4 * NEXP)
            fg = ROWS_A["final_g"][0]
            norm("nf", KC, TL, lambda kc, cs: x_t[:, kc, cs], lambda kc, v: cols_a[:, fg + kc:fg + kc + 1],
                 None, None, None, 1)
            for t in range(2):
                for b in range(2):
                    dve.wait_ge(s_oT, 2 * t + b + 1)
                    dve.tensor_copy(out_rows[:, t, b * 512:(b + 1) * 512], B[2 * t + b][:, :]).then_inc(s_orow, 2)

        @block.tensor
        def _(pe):
            def mm(out_, lhs, rhs, start, stop):
                return pe.matmul(out_, lhs, rhs, start=start, stop=stop, skip_group_check=True)

            def three(out_, wh, wl, xh, xl, first, last):
                mm(out_, wh, xh, first, False)
                mm(out_, wh, xl, False, False)
                return mm(out_, wl, xh, False, last)

            def slot_view(t, slot, nk, cols):
                return t[:, slot, 0:nk * cols].rearrange("p (k n) -> p k n", k=nk)

            def ada_mms(wh, wl, k0, k1, bank=ADA_BANK):
                for kc in range(k0, k1):
                    mm(bank[0:4, 0:ADA_W], c4[:, kc, :], wh[:, kc - k0, :], kc == 0, False)
                    last = mm(bank[0:4, 0:ADA_W], c4[:, kc, :], wl[:, kc - k0, :], False, kc == KC - 1)
                return last

            def ada_half(n, h):
                pe.wait_ge(ad["lo"], n * 2 + (h + 2 + ONE))
                if h == 0:
                    pe.wait_ge(ad["cols"], n + ADA_FIRST)
                ada_mms(ada_hi, ada_lo, h * (KC // 2), (h + 1) * (KC // 2)).then_inc(ad["mm"], 1)

            def ada_turn(n, rows=ada_rows, bank=ADA_BANK):
                pe.wait_ge(ad["rows"], n + 1)
                for j in range(2):
                    last = mm(bank[:, 256 + 4 * j:260 + 4 * j], rows[:, j * P:(j + 1) * P],
                              ident[0:4, 0:4], True, True)
                last.then_inc(ad["turned"], 1)

            def norm_sum(key, chunks, nt, bank):
                for kc in range(chunks):
                    pe.wait_ge(*normed(key, "sq", kc + 1))
                    last = mm(bank[:, 0:nt], ones[:, :], sq[:, kc, 0:nt], kc == 0, kc == chunks - 1)
                last.then_inc(norm_sem["sum"], 1)

            def chunk_wait(key, kc, parts):
                pe.wait_ge(*normed(key, "hi", parts * (kc + 1)))
                pe.wait_ge(*normed(key, "lo", parts * (kc + 1)))

            pe.wait_ge(s_id, 16)
            pe.wait_ge(s_vec, 128)
            pe.transpose(B[0][:, 0:NROWS_A], rows_a[0:NROWS_A, :], ident[0:NROWS_A, 0:NROWS_A]).then_inc(s_vecT, 1)
            pe.transpose(B[1][:, 0:NMOD], rows_b[:, :], ident[0:NMOD, 0:NMOD]).then_inc(s_vecT, 1)
            pe.wait_ge(s_x, 32)
            for kc in range(KC):
                if kc >= 4:
                    pe.wait_ge(s_xc1 if kc % 2 else s_xc, kc // 2 - 1)
                for t in range(4):
                    last = pe.transpose(B[2 + kc % 4][:, t * P:(t + 1) * P], x_rows[:, t, kc * P:(kc + 1) * P],
                                        ident[:, :])
                last.then_inc(s_xT, 1)
            pe.wait_ge(s_ones, 1)
            norm_sum("n01", KC, T, B[6])
            pe.wait_ge(s_silu, 4)
            for a in range(ADA_FIRST):
                pe.wait_ge(split_hi, a + 1)
                pe.wait_ge(split_lo, a + 1)
                if a >= 2:
                    pe.wait_ge(ad["cols"], a - 1)
                elif a:
                    pe.wait_ge(s_cols, 1)
                ada_mms(slot_view(w_hi, a % SLOTS, KC, ADA_W), slot_view(w_lo, a % SLOTS, KC, ADA_W), 0, KC,
                        FIRST_BANKS[a % 2]).then_inc(ada_first_mm, 1)
                if a:
                    ada_turn(a - 1, first_rows[(a - 1) % 2], FIRST_BANKS[(a - 1) % 2])
            ada_turn(ADA_FIRST - 1, first_rows[(ADA_FIRST - 1) % 2], FIRST_BANKS[(ADA_FIRST - 1) % 2])

            pe.wait_ge(ad["cols"], ADA_FIRST)
            pe.wait_ge(s_xc, 4)
            pe.wait_ge(s_xc1, 4)
            bank = 0
            for k, cols in enumerate(PROJ0_COLS):
                n = BASE_PROJ0 + k
                pe.wait_ge(split_hi, n + 1)
                pe.wait_ge(split_lo, n + 1)
                wh, wl = slot_view(w_hi, n % SLOTS, KC, cols), slot_view(w_lo, n % SLOTS, KC, cols)
                for c0 in range(0, cols, P):
                    c1 = min(c0 + P, cols)
                    for kc in range(KC):
                        if bank == 0:
                            chunk_wait("n01", kc, 2)
                        last = three(B[bank][0:c1 - c0, :], wh[:, kc, c0:c1], wl[:, kc, c0:c1], h_hi[:, kc, :],
                                     h_lo[:, kc, :], kc == 0, kc == KC - 1)
                    last.then_inc(s_pj, 1)
                    if bank == 3:
                        norm_sum("nq", 3, T, B[6])
                    bank += 1
            rr = slice(NOPE, QKD)
            pe.wait_ge(s_pje, 1)
            pe.wait_ge(s_const, 16 * 10)
            mm(B[5][0:QKD, 0:TL], rot_mla[rr, :], kr[rr, LAT], True, True).then_inc(s_krr, 1)
            pe.wait_ge(*normed("nq", "rms", 1))
            norm_sum("nc", 2, T, B[6])

            chunk_wait("nq", 2, 1)
            chunk_wait("nc", 1, 1)
            pe.wait_ge(s_krhi, 2)
            pe.wait_ge(s_krlo, 2)

            def mla_scores(i, u):
                j, t = divmod(u, 3)
                if u >= 3:
                    pe.wait_ge(m["exp"], ONE + i * 6 + (u - 2))
                if t < 2:
                    qs = slice(t * P, (t + 1) * P)
                    last = three(B[t][:, :], mq_hi[:, j, qs], mq_lo[:, j, qs], mk_hi[:, j, :], mk_lo[:, j, :],
                                 True, True)
                else:
                    for t2 in range(2):
                        qs = slice(TL + t2 * P, TL + (t2 + 1) * P)
                        last = three(B[2][:, t2 * TL:(t2 + 1) * TL], mq_hi[:, j, qs], mq_lo[:, j, qs],
                                     mk_hi[:, j, CTX], mk_lo[:, j, CTX], True, True)
                last.then_inc(m["scores"], 1)

            def mla_turn(i, u):
                pe.wait_ge(m["normed"], i * 12 + (2 * u + 2))
                if u >= 2:
                    pe.wait_ge(m["p_lo"], ONE + i * 6 + (u - 1))
                for b in range(4):
                    src = b * P if u % 3 < 2 else (b % 2) * TL + (b // 2) * P
                    last = pe.transpose(B[3 + u % 2][:, b * P:(b + 1) * P], mp[:, u % 3, src:src + P], ident[:, :])
                last.then_inc(m["turned"], 1)

            def mla_pv(i, j):
                pe.wait_ge(m["p_hi"], i * 6 + (3 * j + 3))
                pe.wait_ge(m["p_lo"], ONE + i * 6 + (3 * j + 3))
                for b in range(4):
                    three(B[5 + j][:, LAT], mv_hi[:, b, :], mv_lo[:, b, :], pl_hi[:, b, :], pl_lo[:, b, :],
                          b == 0, b == 3)
                for b in range(2):
                    last = three(B[5 + j][:, CTX], mv_hi[:, 2 + b, :], mv_lo[:, 2 + b, :], pc_hi[:, b, :],
                                 pc_lo[:, b, :], b == 0, b == 1)
                last.then_inc(m["pv"], 1)

            def mla_q_proj(n, j, i):
                if i is not None:
                    pe.wait_ge(m["exp"], i * 6 + (4 + j + ONE))
                for kc in range(QL // P):
                    cs = slice(j * QKD, (j + 1) * QKD)
                    last = three(B[j][0:QKD, :], uq_hi[:, kc, cs], uq_lo[:, kc, cs], qa_hi[:, kc, :],
                                 qa_lo[:, kc, :], kc == 0, kc == QL // P - 1)
                last.then_inc(m["proj"], 1)

            def mla_k_proj(n, j, i):
                if i is not None and j == 0:
                    pe.wait_ge(m["o_lo"], i * 2 + (1 + ONE))
                if i is not None and j == 1:
                    pe.wait_ge(m["exp"], i * 6 + (6 + ONE))
                for kc in range(KVL // P):
                    cs = slice(j * 128, j * 128 + NOPE)
                    last = three(B[K_BANKS[j]][0:NOPE, :], ukv_hi[:, kc, cs], ukv_lo[:, kc, cs], ca_hi[:, kc, :],
                                 ca_lo[:, kc, :], kc == 0, kc == KVL // P - 1)
                last.then_inc(m["proj"], 1)

            def mla_v_proj(n, i):
                if i is not None:
                    pe.wait_ge(m["p_lo"], i * 6 + (5 + ONE))
                for t in range(4):
                    ts = slice(t * P, (t + 1) * P)
                    for kc in range(KVL // P):
                        vh = ukv_hi[:, kc, :].rearrange("p (j n) -> p j n", j=2)[:, :, NOPE:]
                        vl = ukv_lo[:, kc, :].rearrange("p (j n) -> p j n", j=2)[:, :, NOPE:]
                        last = three(B[3][:, ts].rearrange("p (j n) -> p j n", j=2), ca_hi[:, kc, ts],
                                     ca_lo[:, kc, ts], vh, vl, kc == 0, kc == KVL // P - 1)
                last.then_inc(m["proj"], 1)

            def mla_rot(n):
                pe.wait_ge(m["q_f32"], n * 2 + 2)
                mm(B[0][0:QKD, :].rearrange("p (j t) -> p j t", j=2), rot_mla[rr, :], mq[rr, :, LAT], True, True)\
                    .then_inc(m["rot"], 1)

            def mla_body(i, n):
                more = n is not None
                pe.wait_ge(m["q_hi"], i + 1)
                pe.wait_ge(m["q_lo"], i + 1)
                pe.wait_ge(m["kv_lo"], i * 3 + 2)
                mla_scores(i, 0)
                mla_scores(i, 1)
                mla_scores(i, 2)
                ada_half(i * 2, 0)
                pe.wait_ge(m["kv_lo"], i * 3 + 3)
                mla_turn(i, 0)
                mla_scores(i, 3)
                mla_turn(i, 1)
                mla_turn(i, 2)
                mla_scores(i, 4)
                ada_half(i * 2, 1)
                mla_pv(i, 0)
                ada_turn(i * 2 + ADA_FIRST)
                mla_turn(i, 3)
                mla_scores(i, 5)
                if more:
                    pe.wait_ge(m["w_hi"], n * 2 + 2)
                    pe.wait_ge(m["w_lo"], n * 2 + 2)
                    mla_q_proj(n, 0, i)
                    mla_q_proj(n, 1, i)
                ada_half(i * 2 + 1, 0)
                mla_turn(i, 4)
                if more:
                    mla_k_proj(n, 0, i)
                mla_turn(i, 5)
                if more:
                    mla_k_proj(n, 1, i)
                ada_half(i * 2 + 1, 1)
                if more:
                    mla_rot(n)
                mla_pv(i, 1)
                if more:
                    mla_v_proj(n, i)
                ada_turn(i * 2 + (ADA_FIRST + 1))

            pe.wait_ge(m["w_hi"], 2)
            pe.wait_ge(m["w_lo"], 2)
            for j in range(2):
                mla_q_proj(0, j, None)
            for j in range(2):
                mla_k_proj(0, j, None)
            mla_rot(0)
            mla_v_proj(0, None)
            with pe.Fori(0, H // 2 - 1) as i:
                mla_body(i, i + 1)
            mla_body(H // 2 - 1, None)

            def out_proj(layer, base, cols, yh, yl, nt):
                mc = 0
                for k, w in enumerate(cols):
                    n = base + k
                    pe.wait_ge(split_hi, n + 1)
                    pe.wait_ge(split_lo, n + 1)
                    wh, wl = slot_view(w_hi, n % SLOTS, KC, w), slot_view(w_lo, n % SLOTS, KC, w)
                    for j in range(w // P):
                        if mc >= 2:
                            pe.wait_ge(wo[layer]["added"], mc - 1)
                        for kc in range(KC):
                            last = three(B[mc % 2][:, 0:nt], wh[:, kc, j * P:(j + 1) * P],
                                         wl[:, kc, j * P:(j + 1) * P], yh[:, kc, 0:nt], yl[:, kc, 0:nt],
                                         kc == 0, kc == KC - 1)
                        last.then_inc(wo[layer]["done"], 1)
                        mc += 1

            def ffn(q, e, base, nt, with_ada):
                for s, (kind, gr, k, f0, m0) in enumerate(ITEMS):
                    slot = s % SLOTS
                    if with_ada and 1 <= s <= ADA_TILES // 2:
                        ada_turn(e * (ADA_TILES // 2) + (ADA_TILES + s - 1))
                    with_half = with_ada and s < ADA_TILES // 2
                    n_ada = e * (ADA_TILES // 2) + (ADA_MLA + s)
                    pe.wait_ge(split_hi, e * NITEMS + (base + s + 1))
                    pe.wait_ge(split_lo, e * NITEMS + (base + s + 1))
                    if kind == "up":
                        pe.wait_ge(q["hid"], ONE + e * 11 + max(f0 - 1, 0))
                        wh, wl = slot_view(w_hi, slot, KC, 256), slot_view(w_lo, slot, KC, 256)
                        for half in range(2):
                            cs = slice(half * P, (half + 1) * P)
                            if half and with_half:
                                ada_half(n_ada, 0)
                            for kc in range(KC):
                                if s == 0 and half == 0:
                                    chunk_wait("n02", kc, 2)
                                last = three(B[2 * (f0 % 2) + half][:, 0:nt], wh[:, kc, cs], wl[:, kc, cs],
                                             h_hi[:, kc, 0:nt], h_lo[:, kc, 0:nt], kc == 0, kc == KC - 1)
                        last.then_inc(q["pe"], 1)
                    else:
                        nf = GROUPS[gr][1]
                        wh, wl = slot_view(w_hi, slot, nf, k * P), slot_view(w_lo, slot, nf, k * P)
                        for j in range(k):
                            pe.wait_ge(q["added"], ONE + e * 16 + (8 * gr + max(m0 + j - 2, 0)))
                            if j == 0:
                                pe.wait_ge(q["hid_lo"], ONE + e * 11 + (f0 + nf - 1))
                            for kc in range(nf - 1):
                                three(B[4 + (m0 + j) % 3][:, 0:nt], wh[:, kc, j * P:(j + 1) * P],
                                      wl[:, kc, j * P:(j + 1) * P], hid_hi[:, kc, 0:nt], hid_lo[:, kc, 0:nt],
                                      kc == 0, False)
                        if with_half:
                            ada_half(n_ada, 0)
                        pe.wait_ge(q["hid_lo"], ONE + e * 11 + (f0 + nf))
                        for j in range(k):
                            three(B[4 + (m0 + j) % 3][:, 0:nt], wh[:, nf - 1, j * P:(j + 1) * P],
                                  wl[:, nf - 1, j * P:(j + 1) * P], hid_hi[:, nf - 1, 0:nt],
                                  hid_lo[:, nf - 1, 0:nt], False, True).then_inc(q["pe"], 1)
                    if with_half:
                        ada_half(n_ada, 1)

            pe.wait_ge(m["o_hi"], H)
            pe.wait_ge(m["o_lo"], ONE + H)
            out_proj(0, BASE_WO0, WO_COLS_0, h_hi, h_lo, T)
            norm_sum("n02", KC, T, B[6])
            with pe.Fori(0, 2) as e:
                ffn(ff, e, BASE_FFN0, T, True)

            norm_sum("n11", KC, T, B[6])
            pe.wait_ge(split_hi, BASE_KV1 + 1)
            pe.wait_ge(split_lo, BASE_KV1 + 1)
            kh, kl = slot_view(w_hi, 0, KC, 256), slot_view(w_lo, 0, KC, 256)
            for c2 in range(2):
                cs = slice(c2 * P, (c2 + 1) * P)
                for kc in range(KC):
                    if c2 == 0:
                        chunk_wait("n11", kc, 2)
                    last = three(B[c2][:, :], kh[:, kc, cs], kl[:, kc, cs], h_hi[:, kc, :], h_lo[:, kc, :],
                                 kc == 0, kc == KC - 1)
                last.then_inc(s_kv1, 1)
            pe.wait_ge(split_hi, BASE_KV1 + 2)
            pe.wait_ge(split_lo, BASE_KV1 + 2)
            vh, vl = slot_view(w_hi, 1, KC, 256), slot_view(w_lo, 1, KC, 256)
            for t in range(4):
                ts = slice(t * P, (t + 1) * P)
                for kc in range(KC):
                    last = three(B[2 + t // 2][:, (t % 2) * 256:(t % 2 + 1) * 256], h_hi[:, kc, ts],
                                 h_lo[:, kc, ts], vh[:, kc, :], vl[:, kc, :], kc == 0, kc == KC - 1)
                if t % 2:
                    last.then_inc(s_kv1, 1)
            pe.wait_ge(s_kf, 2)
            mm(B[4][:, :].rearrange("p (c t) -> p c t", c=2), rot_gqa[:, :], kf[:, :, LAT], True, True)\
                .then_inc(s_krot1, 1)
            pe.wait_ge(s_v1lo, 2)
            pe.wait_ge(s_krope1, 3)
            pe.wait_ge(s_cr, 3)

            def g_scores(gi, u):
                j, t = divmod(u, 2)
                if u >= 3:
                    pe.wait_ge(g["exp"], ONE + gi * 8 + (u - 2))
                rows, qs = slice(HD * (j % 2), HD * (j % 2 + 1)), slice(t * P, (t + 1) * P)
                three(B[u % 3][:, :], gq_hi[rows, j // 2, qs], gq_lo[rows, j // 2, qs], gk_hi[rows, :],
                      gk_lo[rows, :], True, False)
                mm(B[u % 3][:, (1 - t) * P:(2 - t) * P], ident_r[:, :], mask_r[:, t, :], False, True)\
                    .then_inc(g["scores"], 1)

            def g_turn(gi, u):
                pe.wait_ge(g["normed"], gi * 8 + (u + 1))
                pe.wait_ge(g["p_lo"], ONE + gi * 8 + max(u - 1, 0))
                for b in range(4):
                    last = pe.transpose(B[3 + u % 2][:, b * P:(b + 1) * P], gp[:, u % 3, b * P:(b + 1) * P],
                                        ident[:, :])
                last.then_inc(g["turned"], 1)

            def g_pv(gi, j):
                pe.wait_ge(g["p_hi"], gi * 8 + (2 * j + 2))
                pe.wait_ge(g["p_lo"], ONE + gi * 8 + (2 * j + 2))
                pe.wait_ge(g["o_lo"], ONE + gi * 4 + max(j - 1, 0))
                for b in range(4):
                    last = three(B[5 + j % 2][:, 0:TL], gv_hi[:, b, :], gv_lo[:, b, :], gt_hi[:, b, :],
                                 gt_lo[:, b, :], b == 0, b == 3)
                last.then_inc(g["pv"], 1)

            def q_project(n):
                pe.wait_ge(qw_hi, n + 1)
                pe.wait_ge(qw_lo, ONE + n + 1)
                for j in range(2):
                    qh, ql = slot_view(w_hi, Q_SLOT, KC, 256), slot_view(w_lo, Q_SLOT, KC, 256)
                    for kc in range(KC):
                        cs = slice(j * P, (j + 1) * P)
                        last = three(B[7][:, j * TL:(j + 1) * TL], qh[:, kc, cs], ql[:, kc, cs], h_hi[:, kc, LAT],
                                     h_lo[:, kc, LAT], kc == 0, kc == KC - 1)
                    last.then_inc(g["proj"], 1)

            def q_rotate(n):
                pe.wait_ge(g["q_f32"], n + 1)
                mm(B[7][:, :].rearrange("p (j t) -> p j t", j=2), rot_gqa[:, :], gq[:, :, :], True, True)\
                    .then_inc(g["rot"], 1)

            def g_body(gi, following):
                pe.wait_ge(g["q_hi"], gi + 1)
                pe.wait_ge(g["q_lo"], gi + 1)
                pe.wait_ge(g["k_copied"], gi * 2 + 2)
                pe.wait_ge(g["exp"], ONE + gi * 8)
                for u in range(3):
                    g_scores(gi, u)
                for u in range(8):
                    g_turn(gi, u)
                    if u + 3 < 8:
                        g_scores(gi, u + 3)
                    if u == 2:
                        pe.wait_ge(g["v_copied"], gi * 4 + 4)
                    if u % 2 == 0 and u >= 2:
                        g_pv(gi, u // 2 - 1)
                    if following:
                        if u == 2:
                            pe.wait_ge(g["rope"], gi * 3 + 3)
                            q_project(gi + 1)
                        elif u == 5:
                            q_rotate(gi + 1)
                g_pv(gi, 3)

            q_project(0)
            q_rotate(0)
            with pe.Fori(0, 3) as gi:
                g_body(gi, True)
            g_body(3, False)

            pe.wait_ge(g["o_hi"], H)
            pe.wait_ge(g["o_lo"], ONE + H)
            out_proj(1, BASE_WO1, WO_COLS_1, o_hi, o_lo, TL)
            norm_sum("n12", KC, TL, B[6])
            chunk_wait("n12", KC - 1, 1)
            pe.wait_ge(s_rwlo, 1)
            for t in range(2):
                ts = slice(t * P, (t + 1) * P)
                for kc in range(KC):
                    last = three(B[0][:, t * NEXP:(t + 1) * NEXP], h_hi[:, kc, ts], h_lo[:, kc, ts],
                                 rw_hi[:, kc, :], rw_lo[:, kc, :], kc == 0, kc == KC - 1)
            last.then_inc(s_lgp, 1)
            for k in range(8):
                if k >= 6:
                    pe.wait_ge(mo["tok"], k - 5)
                if k == 6:
                    pe.wait_ge(s_sel, 5)
                    pe.wait_ge(s_const, 16 * 10)
                    mm(B[1][:, 0:NEXP], tri[:, :], sel[:, 0, :], True, True)
                    mm(B[1][:, NEXP:2 * NEXP], tri[:, :], sel[:, 1, :], True, False)
                    mm(B[1][:, NEXP:2 * NEXP], ones[:, :], sel[:, 0, :], False, True)
                    mm(B[1][:, 2 * NEXP:3 * NEXP], ones[:, :], sel[:, 0, :], True, False)
                    mm(B[1][:, 2 * NEXP:3 * NEXP], ones[:, :], sel[:, 1, :], False, True).then_inc(mo["rank"], 1)
                src, t, c0 = (h_hi, h_lo)[k // 4], (k // 2) % 2, (k % 2) * 4
                for j in range(4):
                    last = pe.transpose(B[2 + k % 6][:, j * P:(j + 1) * P],
                                        src[:, c0 + j, t * P:(t + 1) * P].bitcast(f32), ident[:, :])
                last.then_inc(mo["tok_turned"], 1)

            def gather(e, banks):
                for j, (src, _, c0) in enumerate(GATHERS):
                    if banks[j] in banks[:j]:
                        pe.wait_ge(mo["xg"], e * 4 + (banks.index(banks[j]) + 1))
                    for kc in range(4):
                        for t in range(2):
                            last = mm(B[banks[j]][:, kc * P:(kc + 1) * P],
                                      src[:, t, (c0 + kc) * P:(c0 + kc + 1) * P],
                                      pick[:, e, TL + t * P:TL + (t + 1) * P] if isinstance(e, int) else
                                      pick[:, bass.ds(e, 1), TL + t * P:TL + (t + 1) * P], t == 0, t == 1)
                    last.then_inc(mo["gathered"], 1)

            def scatter(e):
                with pe.If(pe.value_load(wide[0:1, bass.ds(e, 1)], min_val=0, max_val=1) > 0):
                    pe.wait_ge(mo["added"], e * 4 + 4)
                    pe.sem_inc(mo["scattered"], 4)
                with pe.Else():
                    pe.wait_ge(mo["y_lo"], ONE + e * 2 + 2)
                    pe.wait_ge(mo["y_hi"], e * 2 + 2)
                    for j in range(4):
                        for i in range(2):
                            mc = 2 * j + i
                            cs = slice(mc * P, (mc + 1) * P)
                            out_ = B[OUT[j]][:, i * TL:(i + 1) * TL]
                            mm(out_, y_hi[:, cs], put_hi[:, e, CTX], True, False)
                            mm(out_, y_lo[:, cs], put_hi[:, e, CTX], False, False)
                            last = mm(out_, y_hi[:, cs], put_lo[:, e, CTX], False, True)
                        last.then_inc(mo["scattered"], 1)

            def turn_hidden(e, k):
                pe.wait_ge(mo["hid"], ONE + e * 11 + (k + 1))
                pe.wait_ge(mo["hid_lo"], ONE + e * 11 + k)
                pe.transpose(B[5][:, 0:P], s_hid[:, k % 2, 0:P], ident[:, :])\
                    .then_inc(mo["hid_turned"], 1)

            def narrow_down(e, gr, k, f0, m0, wh, wl):
                nf = GROUPS[gr][1]
                for kc in range(nf):
                    if m0 == 0 and kc == 2:
                        turn_hidden(e, f0 + nf - 1)
                    pe.wait_ge(mo["hid_lo"], ONE + e * 11 + (f0 + kc + 1))
                    for bank, c0, j, n in y_runs(m0, k):
                        out_, cs = B[bank][:, c0:c0 + n * P], slice(j * P, (j + n) * P)
                        mm(out_, sh_hi[:, f0 + kc, 0:P], wh[:, kc, cs], gr == 0 and kc == 0 and c0 == 0, False)
                        mm(out_, sh_hi[:, f0 + kc, 0:P], wl[:, kc, cs], False, False)
                        done = mm(out_, sh_lo[:, f0 + kc, 0:P], wh[:, kc, cs], False, gr == 1 and kc == nf - 1)
                return done

            def wide_down(e, gr, k, f0, m0, wh, wl):
                nf = GROUPS[gr][1]
                pe.wait_ge(mo["hid_lo"], ONE + e * 11 + (f0 + nf))
                for j in range(k):
                    mc = m0 + j
                    for kc in range(nf):
                        done = three(B[OUT_WIDE[mc // 2]][:, (mc % 2) * TL:(mc % 2 + 1) * TL],
                                     wh[:, kc, j * P:(j + 1) * P], wl[:, kc, j * P:(j + 1) * P],
                                     sh_hi[:, f0 + kc, :], sh_lo[:, f0 + kc, :], gr == 0 and kc == 0 and mc % 2 == 0,
                                     gr == 1 and kc == nf - 1)
                return done

            def moe_body(e, first, last, is_wide):
                pe.wait_ge(mo["xg"], e * 4 + 4)
                for s, (kind, gr, k, f0, m0) in enumerate(ITEMS):
                    slot = s % SLOTS
                    pe.wait_ge(split_hi, e * NITEMS + (BASE_FFN1 + s + 1))
                    pe.wait_ge(split_lo, e * NITEMS + (BASE_FFN1 + s + 1))
                    if kind == "up":
                        pe.wait_ge(mo["hid"], ONE + e * 11 + max(f0 - 1, 0))
                        wh, wl = slot_view(w_hi, slot, KC, 256), slot_view(w_lo, slot, KC, 256)
                        bank = B[6 + f0 % 2]
                        for half in range(2 if is_wide else 0):
                            cs = slice(half * P, (half + 1) * P)
                            for kc in range(KC):
                                done = three(bank[:, half * TL:(half + 1) * TL], wh[:, kc, cs], wl[:, kc, cs],
                                             h_hi[:, kc, LAT], h_lo[:, kc, LAT], kc == 0, kc == KC - 1)
                        for kc in range(0 if is_wide else KC):
                            mm(bank[:, 0:256], xg_hi[:, kc, :], wh[:, kc, :], kc == 0, False)
                            mm(bank[:, 0:256], xg_hi[:, kc, :], wl[:, kc, :], False, False)
                            done = mm(bank[:, 0:256], xg_lo[:, kc, :], wh[:, kc, :], False, kc == KC - 1)
                    else:
                        nf = GROUPS[gr][1]
                        wh, wl = slot_view(w_hi, slot, nf, k * P), slot_view(w_lo, slot, nf, k * P)
                        if gr == 0 and m0 == 0:
                            pe.wait_ge(mo["y_lo"], ONE + e * 2)
                            if not first:
                                pe.wait_ge(mo["added"], e * 4)
                        done = (wide_down if is_wide else narrow_down)(e, gr, k, f0, m0, wh, wl)
                    done.then_inc(mo["pe"], 1)
                    if s == 1 and not first:
                        scatter(e - 1)
                    if not is_wide and kind == "up" and k:
                        turn_hidden(e, f0 - 1)
                    if s == 13 and not last:
                        if is_wide:
                            pe.wait_ge(mo["y_lo"], ONE + e * 2)
                            gather(e + 1, AUX_WIDE)
                        else:
                            if not first:
                                pe.wait_ge(mo["added"], e * 4)
                            gather(e + 1, AUX)
                if is_wide:
                    pe.sem_inc(mo["hid_turned"], 11)

            def expert(e, first, last):
                with pe.If(pe.value_load(wide[0:1, bass.ds(e, 1)], min_val=0, max_val=1) > 0):
                    moe_body(e, first, last, True)
                with pe.Else():
                    moe_body(e, first, last, False)

            pe.wait_ge(mo["fits"], 2)
            pe.wait_ge(mo["tok"], 8)
            pe.wait_ge(mo["pick"], 2 * NEXP)
            gather(0, AUX)
            for b in range(4):
                pe.wait_ge(mo["put_tok"], 4 * (b + 1))
                for e in (2 * b, 2 * b + 1):
                    for t in range(2):
                        last = pe.transpose(B[(3, 4, 6, 7)[b]][:, (e % 2) * TL + t * P:(e % 2) * TL + (t + 1) * P],
                                            put_tok[:, e, t * P:(t + 1) * P], ident[:, :])
                last.then_inc(mo["put_turned"], 1)
            pe.wait_ge(mo["put_lo"], 4)
            with pe.If(pe.value_load(any_wide[0:1, 0:1], min_val=0, max_val=1) > 0):
                pe.wait_ge(s_rs, 13 + 2 * NEXP)
                for e in range(NEXP):
                    for t in range(2):
                        last = mm(B[(3, 4, 6, 7)[e // 2]][:, (e % 2) * TL + t * P:(e % 2) * TL + (t + 1) * P],
                                  comb_rep[:, t, e, :], ident[:, :], True, True)
                    if e % 2:
                        last.then_inc(s_cbp, 1)
                pe.wait_ge(s_cb, 4)
            expert(0, True, False)
            with pe.Fori(1, NEXP - 1) as e:
                expert(e, False, False)
            expert(NEXP - 1, False, True)
            scatter(NEXP - 1)

            norm_sum("nf", KC, TL, B[6])
            pe.wait_ge(*normed("nf", "tmp", KC))
            for t in range(2):
                for b in range(2):
                    for k in range(4):
                        last = pe.transpose(B[2 * t + b][:, k * P:(k + 1) * P],
                                            sq[:, 4 * b + k, t * P:(t + 1) * P], ident[:, :])
                    last.then_inc(s_oT, 1)


_NAMES = ("x", "c", "ctx", "c_ctx", "ada_w", "ada_b", "norm_g", "final_norm_g", "mla_w_dq", "mla_q_norm_g",
          "mla_w_uq", "mla_w_dkv", "mla_kv_norm_g", "mla_w_ukv", "mla_w_o", "swa_w_qkv", "swa_sinks", "swa_w_o",
          "ffn_w_gate_up", "ffn_w_down", "moe_router_w", "moe_router_b", "moe_w_gate_up", "moe_w_down")


def constants():
    def angles(rot_dim):
        n = rot_dim // 4
        inv = np.float32(10000.0) ** (-np.arange(n, dtype=np.float32) / np.float32(n))
        rows = np.repeat(np.arange(TL // GRID_W, dtype=np.float32), GRID_W)
        cols = np.tile(np.arange(GRID_W, dtype=np.float32), TL // GRID_W)
        return np.concatenate([rows[:, None] * inv, cols[:, None] * inv], axis=-1).astype(np.float32)

    def table(rot_dim, first, copies):
        a = angles(rot_dim).T
        out = np.zeros((P, 2, 2, TL), np.float32)
        for k in range(copies):
            for half in range(2):
                r = first + k * rot_dim + half * (rot_dim // 2)
                out[r:r + rot_dim // 2, 0] = np.cos(a)[:, None, :]
                out[r:r + rot_dim // 2, 1] = np.sin(a)[:, None, :]
        return out

    def rotation(width, rot_dim, first, copies):
        r = np.zeros((P, width), np.float32)
        half = rot_dim // 2
        for k in range(copies):
            for i in range(half):
                a = first + k * rot_dim + i
                r[a + half, a] = -1.0
                r[a, a + half] = 1.0
        return r

    q, k = np.arange(P)[:, None], np.arange(P)[None, :]
    mask = np.stack([np.where(k <= q, 0.0, NEG), np.where(k >= q, 0.0, NEG)], axis=1).astype(np.float32)
    return {
        "k_ident": np.eye(P, dtype=np.float32),
        "k_rot_mla": rotation(QKD, ROPE, NOPE, 1),
        "k_rot_gqa": rotation(P, HD, 0, 2),
        "k_cs_mla": table(ROPE, NOPE, 1),
        "k_cs_gqa": table(HD, 0, 2),
        "k_mask": mask,
        "k_iota": np.ascontiguousarray(np.broadcast_to(np.arange(P, dtype=np.float32), (P, P))),
        "k_tri": np.triu(np.ones((P, P), np.float32)),
    }


def kernel(**inputs):
    import concourse.bacc as bacc
    from concourse.bass_utils import run_bass_kernel_spmd

    nc = bacc.Bacc("TRN2", target_bir_lowering=False, num_devices=1)
    arrays = {f"in_{n}": np.ascontiguousarray(inputs[n]) for n in _NAMES}
    arrays.update(constants())
    args = [nc.dram_tensor(n, a.shape, mybir.dt.from_np(a.dtype), kind="ExternalInput").ap()
            for n, a in arrays.items()]
    args.append(nc.dram_tensor("out", (1, TL, D), mybir.dt.float32, kind="ExternalOutput").ap())
    build(nc, *args)
    r = run_bass_kernel_spmd(nc, [arrays], core_ids=[0])
    return r.results[0]["out"]
```
